# Optimizing a Trainium2 kernel written in Bass

```python
import math
import jax
import jax.numpy as jnp
from jax import lax
import numpy as np

D_MODEL = 1024
BATCH = 1
SEQ = 256
DEPTH = 2

HEAD_DIM = 64
RET_HEADS = 4
RET_DIM = RET_HEADS * HEAD_DIM
SSD_HEADS = 8
SSD_HEAD_DIM = 64
SSD_INNER = SSD_HEADS * SSD_HEAD_DIM
SSD_GROUPS = 2
SSD_STATE = 64
SSD_CONV = 4
SSD_CONV_DIM = SSD_INNER + 2 * SSD_GROUPS * SSD_STATE
SB_HEADS = 4
SB_DIM = SB_HEADS * HEAD_DIM
D_MIX = RET_DIM + SSD_INNER + SB_DIM
IN_SPLITS = (RET_DIM, RET_DIM, RET_DIM, RET_DIM, SSD_INNER, SSD_CONV_DIM, SSD_HEADS, SB_DIM, SB_DIM, SB_DIM)
D_IN = 4 * RET_DIM + SSD_INNER + SSD_CONV_DIM + SSD_HEADS + 3 * SB_DIM
CHUNK = 128
Q_BLOCK = 128
D_FF = 3584
N_EXPERTS = 8
TOP_K = 2
ROPE_BASE = 10000.0
EPS = 1e-6
N_DENSE = (DEPTH + 1) // 2
N_MOE = DEPTH // 2

kernel_name = 'hybrid_retention_ssd_stickbreaking_moe'

def rmsnorm(x, w):
    xf = x.astype(jnp.float32)
    y = xf * lax.rsqrt(jnp.mean(xf * xf, axis=-1, keepdims=True) + EPS)
    return (y * w.astype(jnp.float32)).astype(x.dtype)

def rotary(x, pos):
    half = x.shape[-1] // 2
    inv = 1.0 / (ROPE_BASE ** (jnp.arange(half, dtype=jnp.float32) / half))
    ang = pos.astype(jnp.float32)[:, None] * inv[None, :]
    cos = jnp.cos(ang)[None, :, None, :]
    sin = jnp.sin(ang)[None, :, None, :]
    x1, x2 = x[..., :half], x[..., half:]
    return jnp.concatenate([x1 * cos - x2 * sin, x1 * sin + x2 * cos], axis=-1).astype(x.dtype)

def retention_chunkwise(q, k, v):
    bsz, seq, nh, dh = q.shape
    nc = seq // CHUNK
    log_gamma = jnp.log(1.0 - 2.0 ** (-5.0 - jnp.arange(nh, dtype=jnp.float32)))
    idx = jnp.arange(CHUNK, dtype=jnp.float32)
    diff = idx[:, None] - idx[None, :]
    intra = jnp.where(diff >= 0, jnp.exp(log_gamma[:, None, None] * jnp.maximum(diff, 0.0)), 0.0)
    q_decay = jnp.exp(log_gamma[None, :] * (idx[:, None] + 1.0))
    k_decay = jnp.exp(log_gamma[None, :] * (CHUNK - 1.0 - idx[:, None]))
    chunk_decay = jnp.exp(log_gamma * CHUNK)
    qc = q.reshape(bsz, nc, CHUNK, nh, dh)
    kc = (k * dh ** -0.5).reshape(bsz, nc, CHUNK, nh, dh)
    vc = v.reshape(bsz, nc, CHUNK, nh, dh)
    scores = jnp.einsum('bnihd,bnjhd->bnhij', qc, kc) * intra
    y_intra = jnp.einsum('bnhij,bnjhe->bnihe', scores, vc)
    kv = jnp.einsum('bnjhd,bnjhe->bnhde', kc * k_decay[:, :, None], vc)

    def step(state, kv_n):
        return (state * chunk_decay[None, :, None, None] + kv_n).astype(kv.dtype), state

    init = jnp.zeros((bsz, nh, dh, dh), kv.dtype)
    _, prev = lax.scan(step, init, jnp.moveaxis(kv, 1, 0))
    prev = jnp.moveaxis(prev, 0, 1)
    y_inter = jnp.einsum('bnihd,bnhde->bnihe', qc * q_decay[:, :, None], prev)
    return (y_intra + y_inter).reshape(bsz, seq, nh, dh)

def head_groupnorm(y, w):
    yf = y.astype(jnp.float32)
    mu = jnp.mean(yf, axis=-1, keepdims=True)
    var = jnp.mean(jnp.square(yf - mu), axis=-1, keepdims=True)
    yn = (yf - mu) * lax.rsqrt(var + EPS)
    return yn.reshape(y.shape[0], y.shape[1], -1) * w.astype(jnp.float32)

def causal_dwconv(x, w, b):
    k = w.shape[0]
    out = lax.conv_general_dilated(x, w[:, None, :].astype(x.dtype), window_strides=(1,), padding=[(k - 1, 0)],
                                   dimension_numbers=('NWC', 'WIO', 'NWC'), feature_group_count=x.shape[-1])
    return out + b.astype(x.dtype)

def ssd_chunked(xh, dt, a_head, bm, cm):
    bsz, seq, nh, p = xh.shape
    g = bm.shape[2]
    hg = nh // g
    n = bm.shape[3]
    nc = seq // CHUNK
    x = (xh * dt[..., None]).reshape(bsz, nc, CHUNK, g, hg, p)
    a = (dt * a_head).reshape(bsz, nc, CHUNK, g, hg)
    a_cs = jnp.cumsum(a, axis=2)
    bc = bm.reshape(bsz, nc, CHUNK, g, n)
    cc = cm.reshape(bsz, nc, CHUNK, g, n)
    seg = a_cs[:, :, :, None] - a_cs[:, :, None, :]
    lower = (jnp.arange(CHUNK)[:, None] >= jnp.arange(CHUNK)[None, :])[None, None, :, :, None, None]
    l_mat = jnp.exp(jnp.where(lower, seg, -jnp.inf))
    cb = jnp.einsum('bclgn,bcsgn->bclsg', cc, bc)
    y_diag = jnp.einsum('bclsgh,bcsghp->bclghp', cb[..., None] * l_mat, x)
    decay_states = jnp.exp(a_cs[:, :, -1:] - a_cs)
    states = jnp.einsum('bclgn,bclghp->bcghpn', bc, x * decay_states[..., None])
    chunk_decay = jnp.exp(a_cs[:, :, -1])

    def step(state, inp):
        st, dec = inp
        return (state * dec[..., None, None] + st).astype(states.dtype), state

    init = jnp.zeros((bsz, g, hg, p, n), states.dtype)
    _, prev = lax.scan(step, init, (jnp.moveaxis(states, 1, 0), jnp.moveaxis(chunk_decay, 1, 0)))
    prev = jnp.moveaxis(prev, 0, 1)
    y_off = jnp.einsum('bclgn,bcghpn->bclghp', cc, prev) * jnp.exp(a_cs)[..., None]
    return (y_diag + y_off).reshape(bsz, seq, nh, p)

def gated_rmsnorm(y, z, w):
    gy = y.astype(jnp.float32) * jax.nn.silu(z.astype(jnp.float32))
    gg = gy.reshape(gy.shape[:-1] + (SSD_GROUPS, -1))
    gg = gg * lax.rsqrt(jnp.mean(gg * gg, axis=-1, keepdims=True) + EPS)
    return gg.reshape(gy.shape) * w.astype(jnp.float32)

def stick_breaking(q, k, v):
    seq = q.shape[1]
    scale = q.shape[-1] ** -0.5
    outs = []
    for blk in range(seq // Q_BLOCK):
        q0 = blk * Q_BLOCK
        end = q0 + Q_BLOCK
        z = jnp.einsum('bthd,bshd->bhts', q[:, q0:end], k[:, :end]).astype(jnp.float32) * scale
        t_idx = q0 + jnp.arange(Q_BLOCK)
        mask = jnp.arange(end)[None, :] < t_idx[:, None]
        sp = jnp.where(mask, jax.nn.softplus(z), 0.0)
        log_w = z - lax.cumsum(sp, axis=3, reverse=True)
        w = jnp.where(mask, jnp.exp(log_w), 0.0)
        outs.append(jnp.einsum('bhts,bshd->bthd', w.astype(v.dtype), v[:, :end]))
    return jnp.concatenate(outs, axis=1)

def hybrid_mixer(h, w_in, ret_norm_w, conv_w, conv_b, dt_bias, a_log, d_skip, ssd_norm_w, w_out):
    bsz, seq, _ = h.shape
    pos = jnp.arange(seq)
    proj = jnp.einsum('bsd,de->bse', h, w_in)
    offs = np.cumsum(IN_SPLITS)[:-1].tolist()
    rq, rk, rv, rg, sz, sxbc, sdt, bq, bk, bv = jnp.split(proj, offs, axis=-1)
    rq = rotary(rq.reshape(bsz, seq, RET_HEADS, HEAD_DIM), pos)
    rk = rotary(rk.reshape(bsz, seq, RET_HEADS, HEAD_DIM), pos)
    ro = retention_chunkwise(rq, rk, rv.reshape(bsz, seq, RET_HEADS, HEAD_DIM))
    ro = head_groupnorm(ro, ret_norm_w) * jax.nn.silu(rg.astype(jnp.float32))
    xbc = jax.nn.silu(causal_dwconv(sxbc, conv_w, conv_b))
    sx, sb, sc = jnp.split(xbc, [SSD_INNER, SSD_INNER + SSD_GROUPS * SSD_STATE], axis=-1)
    dt = jax.nn.softplus(sdt.astype(jnp.float32) + dt_bias.astype(jnp.float32))
    a_head = -jnp.exp(a_log.astype(jnp.float32))
    xh = sx.reshape(bsz, seq, SSD_HEADS, SSD_HEAD_DIM)
    y = ssd_chunked(xh, dt, a_head, sb.reshape(bsz, seq, SSD_GROUPS, SSD_STATE), sc.reshape(bsz, seq, SSD_GROUPS, SSD_STATE))
    y = y + d_skip[:, None] * xh
    so = gated_rmsnorm(y.reshape(bsz, seq, SSD_INNER), sz, ssd_norm_w)
    bo = stick_breaking(bq.reshape(bsz, seq, SB_HEADS, HEAD_DIM), bk.reshape(bsz, seq, SB_HEADS, HEAD_DIM),
                        bv.reshape(bsz, seq, SB_HEADS, HEAD_DIM)).reshape(bsz, seq, SB_DIM)
    mix = jnp.concatenate([ro.astype(h.dtype), so.astype(h.dtype), bo.astype(h.dtype)], axis=-1)
    return jnp.einsum('bse,ed->bsd', mix, w_out)

def swiglu(h, wg, wu, wd):
    a = jnp.einsum('bsd,df->bsf', h, wg)
    b = jnp.einsum('bsd,df->bsf', h, wu)
    return jnp.einsum('bsf,fd->bsd', jax.nn.silu(a) * b, wd)

def moe_swiglu(h, router_w, wg, wu, wd):
    logits = jnp.einsum('bsd,de->bse', h, router_w).astype(jnp.float32)
    top_val, top_idx = lax.top_k(logits, TOP_K)
    gates = jax.nn.softmax(top_val, axis=-1)
    combine = jnp.sum(jax.nn.one_hot(top_idx, N_EXPERTS, dtype=jnp.float32) * gates[..., None], axis=-2)
    out = jnp.zeros_like(h)
    for e in range(N_EXPERTS):
        out = out + combine[..., e:e + 1].astype(h.dtype) * swiglu(h, wg[e], wu[e], wd[e])
    return out

def setup_inputs(seed: int = 0) -> dict:
    key = jax.random.key(seed)
    ks = jax.random.split(key, 20)
    f32 = jnp.float32
    nrm = lambda k, shape, fan: jax.random.normal(k, shape, f32) * (fan ** -0.5)
    gain = lambda k, shape: 1.0 + 0.02 * jax.random.normal(k, shape, f32)
    dt = jnp.exp(jax.random.uniform(ks[6], (DEPTH, SSD_HEADS), f32) * (math.log(0.1) - math.log(0.001)) + math.log(0.001))
    return {
        'x': jax.random.normal(ks[0], (BATCH, SEQ, D_MODEL), f32),
        'norm1_w': gain(ks[1], (DEPTH, D_MODEL)),
        'w_in': nrm(ks[2], (DEPTH, D_MODEL, D_IN), D_MODEL),
        'ret_norm_w': gain(ks[3], (DEPTH, RET_DIM)),
        'ssd_conv_w': nrm(ks[4], (DEPTH, SSD_CONV, SSD_CONV_DIM), SSD_CONV),
        'ssd_conv_b': 0.01 * jax.random.normal(ks[5], (DEPTH, SSD_CONV_DIM), f32),
        'ssd_dt_bias': dt + jnp.log(-jnp.expm1(-dt)),
        'ssd_a_log': jnp.log(jax.random.uniform(ks[7], (DEPTH, SSD_HEADS), f32, 1.0, 16.0)),
        'ssd_d': gain(ks[8], (DEPTH, SSD_HEADS)),
        'ssd_norm_w': gain(ks[9], (DEPTH, SSD_INNER)),
        'w_out': nrm(ks[10], (DEPTH, D_MIX, D_MODEL), D_MIX),
        'norm2_w': gain(ks[11], (DEPTH, D_MODEL)),
        'ffn_w_gate': nrm(ks[12], (N_DENSE, D_MODEL, D_FF), D_MODEL),
        'ffn_w_up': nrm(ks[13], (N_DENSE, D_MODEL, D_FF), D_MODEL),
        'ffn_w_down': nrm(ks[14], (N_DENSE, D_FF, D_MODEL), D_FF),
        'moe_router': nrm(ks[15], (N_MOE, D_MODEL, N_EXPERTS), D_MODEL),
        'moe_w_gate': nrm(ks[16], (N_MOE, N_EXPERTS, D_MODEL, D_FF), D_MODEL),
        'moe_w_up': nrm(ks[17], (N_MOE, N_EXPERTS, D_MODEL, D_FF), D_MODEL),
        'moe_w_down': nrm(ks[18], (N_MOE, N_EXPERTS, D_FF, D_MODEL), D_FF),
        'final_norm_w': gain(ks[19], (D_MODEL,)),
    }

def reference(x, norm1_w, w_in, ret_norm_w, ssd_conv_w, ssd_conv_b, ssd_dt_bias, ssd_a_log, ssd_d, ssd_norm_w,
              w_out, norm2_w, ffn_w_gate, ffn_w_up, ffn_w_down, moe_router, moe_w_gate, moe_w_up, moe_w_down,
              final_norm_w):
    for layer in range(DEPTH):
        h = rmsnorm(x, norm1_w[layer])
        x = x + hybrid_mixer(h, w_in[layer], ret_norm_w[layer], ssd_conv_w[layer], ssd_conv_b[layer],
                             ssd_dt_bias[layer], ssd_a_log[layer], ssd_d[layer], ssd_norm_w[layer],
                             w_out[layer]).astype(x.dtype)
        h = rmsnorm(x, norm2_w[layer])
        j = layer // 2
        if layer % 2 == 0:
            f = swiglu(h, ffn_w_gate[j], ffn_w_up[j], ffn_w_down[j])
        else:
            f = moe_swiglu(h, moe_router[j], moe_w_gate[j], moe_w_up[j], moe_w_down[j])
        x = x + f.astype(x.dtype)
    return rmsnorm(x, final_norm_w)


_drawn_inputs = setup_inputs


def setup_inputs(seed=0):
    import zlib

    import numpy as np

    out = dict(_drawn_inputs(seed))
    spreads = {}
    factors = {'ret_norm_w': 3.046, 'ssd_conv_b': 3.13, 'ssd_d': 3.156, 'final_norm_w': 2.837}
    for name, (base, spread) in spreads.items():
        noise = np.random.default_rng([zlib.crc32(name.encode()), seed]).standard_normal(out[name].shape)
        drawn = base * np.exp(spread * noise) if base else spread * noise
        out[name] = jnp.asarray(drawn.astype(out[name].dtype))
    for name, factor in factors.items():
        out[name] = (out[name] * factor).astype(out[name].dtype)
    return out
```

```python
from contextlib import ExitStack

import concourse.bass as bass
import numpy as np
from concourse import mybir

F32 = mybir.dt.float32
F32R = mybir.dt.float32r
BF16 = mybir.dt.bfloat16
I32 = mybir.dt.int32
ALU = mybir.AluOpType
ACT = mybir.ActivationFunctionType
AX = mybir.AxisListType

P = 128
T = 256
NB = T // P
D = 1024
KD = D // P
LAYERS = 2
HD = 64
RH, SH, BH = 4, 8, 4
SG = 2
TAPS = 4
XT = 6
F = 3584
FC = F // 512
E = 8
EPS = 1e-6
SC = 384
RAW, SPL = 6, 3
SUB = 2048
MIX_SUBS, ITEM_SUBS = 18, 6 * FC
DENSE_ITEMS = NB
FFN_BASE = [MIX_SUBS, 2 * MIX_SUBS + DENSE_ITEMS * ITEM_SUBS]
MIX_BASE = [0, MIX_SUBS + DENSE_ITEMS * ITEM_SUBS]
ITEM_BASE = [0, DENSE_ITEMS]

WIN = [("xbc", 1536, 512), ("bc_dt", 2048, 264), ("rqk", 0, 512), ("bqk", 2312, 512),
       ("rvg", 512, 512), ("bv", 2824, 256), ("sz", 1024, 512)]
TILES_T = {"xbc": 4, "bc_dt": 2, "rqk": 4, "bqk": 4}
PRM = TAPS * XT + XT + 2 + 4
PRM_B, PRM_N = TAPS * XT, TAPS * XT + XT

C_ID, C_IOTA, C_LE, C_LT, C_GE, C_ONE, C_ROT = (P * i for i in range(7))
C_COS, C_SIN = 7 * P, 7 * P + T
C_CAUSAL = C_SIN + T
C_STRICT = C_CAUSAL + SC
C_RET = C_STRICT + SC
C_E8 = C_RET + RH * SC
C_RG = C_E8 + E
C_ALL = C_RG + 64


def tables():
    c = np.zeros((P, C_ALL), np.float64)
    a = np.arange(P)
    c[:, C_ID:C_ID + P] = np.eye(P)
    c[:, C_IOTA:C_IOTA + P] = a[None, :]
    c[:, C_LE:C_LE + P] = a[:, None] <= a[None, :]
    c[:, C_LT:C_LT + P] = a[:, None] < a[None, :]
    c[:, C_GE:C_GE + P] = a[:, None] >= a[None, :]
    c[:, C_ONE:C_ONE + P] = 1.0
    for m in range(P):
        if m % HD < HD // 2:
            c[m + HD // 2, C_ROT + m] = -1.0
        else:
            c[m - HD // 2, C_ROT + m] = 1.0
    half = HD // 2
    inv = (1.0 / (np.float32(10000.0) ** (np.arange(half, dtype=np.float32) / np.float32(half)))).astype(np.float32)
    ang = (np.arange(T, dtype=np.float32)[None, :] * inv[a % half][:, None]).astype(np.float32)
    c[:, C_COS:C_COS + T] = np.cos(ang.astype(np.float64))
    c[:, C_SIN:C_SIN + T] = np.sin(ang.astype(np.float64))
    j = np.concatenate([np.repeat(a[:, None], T, 1), np.repeat(a[:, None] + P, P, 1)], 1)
    i = np.concatenate([np.arange(T), np.arange(P, T)])[None, :]
    c[:, C_CAUSAL:C_CAUSAL + SC] = j <= i
    c[:, C_STRICT:C_STRICT + SC] = np.where(j < i, -1.0, 0.0)
    for h in range(RH):
        gamma = 1.0 - 2.0 ** (-5.0 - h)
        c[:, C_RET + h * SC:C_RET + (h + 1) * SC] = np.where(j <= i, gamma ** np.maximum(i - j, 0), 0.0) * HD ** -0.5
    c[:, C_E8:C_E8 + E] = np.arange(E) - 100.0
    rg = np.full((P, 2, NB, 16), -1.0)
    rg[:, 1] = 1.0
    for b in range(NB):
        rg[:, 0, b, b] = a
    c[:, C_RG:] = rg.reshape(P, 64)
    return c.astype(np.float32)


def hybrid_kernel(nc, x_d, norm1_d, w_in_d, ret_norm_d, conv_w_d, conv_b_d, dt_bias_d, a_log_d, d_skip_d,
                  ssd_norm_d, w_out_d, norm2_d, ffn_g_d, ffn_u_d, ffn_d_d, router_d, moe_g_d, moe_u_d, moe_d_d,
                  final_d, const_d, out_d):
    ctx = ExitStack()
    with ctx:
        def sb(name, shape, dt=F32):
            return ctx.enter_context(nc.sbuf_tensor(name, shape, dt))

        def sem(name):
            return ctx.enter_context(nc.semaphore(name))

        raw = sb("raw", [P, RAW, SUB])
        w_hi = sb("w_hi", [P, SPL, SUB], F32R)
        w_lo = sb("w_lo", [P, SPL, SUB], F32R)
        x = sb("x", [P, NB, D])
        hm = sb("hm", [P, NB, D])
        aT_hi = sb("aT_hi", [P, 2 * KD, P], F32R)
        aT_lo = sb("aT_lo", [P, 2 * KD, P], F32R)
        cst = sb("cst", [P, C_ALL])
        qkr = sb("qkr", [P, 4 * SC])
        xbc = sb("xbc", [P, XT, T + TAPS - 1])
        cv = sb("cv", [P, XT, T])
        bqk = sb("bqk", [P, 4, T])
        rv = sb("rv", [P, NB, RH * HD])
        rg = sb("rg", [P, NB, RH * HD])
        bv = sb("bv", [P, NB, BH * HD])
        sz = sb("sz", [P, NB, SH * HD])
        xtok = sb("xtok", [P, NB, SH * HD])
        xdt = sb("xdt", [P, NB, SH * HD])
        cb = sb("cb", [P, SG, SC])
        scr = sb("scr", [P, 3, 4 * SC])
        prm_rows = sb("prm_rows", [PRM, LAYERS, P])
        prm = sb("prm", [P, PRM])
        heads8 = sb("heads8", [P, LAYERS, 3, SH])
        small = sb("small", [P, 16, 16])
        rw = sb("rw", [P, KD, E])
        rank_gate = sb("rank_gate", [P, 2, NB, 16])
        cur = sb("cur", [P, 2, NB])
        n_items = sb("n_items", [P, 1], I32)
        zeros = sb("zeros", [1, P], BF16)

        ident = cst[:, C_ID:C_ID + P]
        iota = cst[:, C_IOTA:C_IOTA + P]
        m_le, m_lt, m_ge = (cst[:, c:c + P] for c in (C_LE, C_LT, C_GE))
        ones = cst[:, C_ONE:C_ONE + P]
        rot = cst[:, C_ROT:C_ROT + P]
        normw = bqk[:].rearrange("p a b -> p (a b)")
        csT = scr[0:SH, 1, 1024:1024 + T]
        flat = scr[:].rearrange("p a b -> p (a b)")
        cvf = cv[:].rearrange("p a b -> p (a b)")
        xbf = xbc[:].rearrange("p a b -> p (a b)")[:, 0:4 * SC]
        silu_g, s_act = flat[:, 0:512], flat[:, 512:1024]
        y_sb = flat[:, 1536:2560]
        sel = flat[:, 3072:3328].rearrange("p (b s) -> p b s", b=NB)
        selg = flat[:, 3328:3584].rearrange("p (b s) -> p b s", b=NB)
        selgT = flat[:, 3584:3840].rearrange("p (b s) -> p b s", b=NB)
        h2T = flat[:, 0:2048].rearrange("p (k t) -> p k t", k=2 * KD)

        def sm(i, n=16):
            return small[:, i, 0:n]

        def sm3(i):
            return small[:, i, :].rearrange("p (b e) -> p b e", b=NB)

        ps = ctx.enter_context(nc.psum_tensor("ps", [P, 8, 512], F32))

        def banks(a, b):
            return ps[:, a:b, :].rearrange("p a n -> p (a n)")

        landed = [sem(f"landed{i}") for i in range(RAW)]
        hi_ready = sem("hi_ready")
        lo_ready = [sem(f"lo_ready{i}") for i in range(RAW)]
        split_used = sem("split_used")
        (x_in, const_in, prm_in, normw_in, rw_in, zeros_set, pad_set) = map(
            sem, ("x_in", "const_in", "prm_in", "normw_in", "rw_in", "zeros_set", "pad_set"))
        (sumsq, rms_ready, rstd_ready, h_ready) = map(sem, ("sumsq", "rms_ready", "rstd_ready", "h_ready"))
        (hT_psum, hT_hi, hT_lo, prm_psum, prm_ready) = map(
            sem, ("hT_psum", "hT_hi", "hT_lo", "prm_psum", "prm_ready"))
        (win_psum, win_out, conv_tap, conv_silu) = map(sem, ("win_psum", "win_out", "conv_tap", "conv_silu"))
        (dt_biased, dt_ln, a_ready) = map(sem, ("dt_biased", "dt_ln", "a_ready"))
        (cs_psum, cs_ready, csT_ready, cb_psum, cb_ready) = map(
            sem, ("cs_psum", "cs_ready", "csT_ready", "cb_psum", "cb_ready"))
        (xT_psum, xtok_ready, xdt_ready, rot_psum, qk_ready) = map(
            sem, ("xT_psum", "xtok_ready", "xdt_ready", "rot_psum", "qk_ready"))
        (csb_psum, seg_ready, seg_exp, s_ssd) = map(sem, ("csb_psum", "seg_ready", "seg_exp", "s_ssd"))
        (ret_psum, s_ret, ssd_y, gated, gated_sq, ssd_rms) = map(
            sem, ("ret_psum", "s_ret", "ssd_y", "gated", "gated_sq", "ssd_rms"))
        (ret_y, ret_var, ret_std) = map(sem, ("ret_y", "ret_var", "ret_std"))
        (sb_z, sb_ln, sb_sp, sb_log, sb_min, sb_w, sb_wm, sb_y) = map(
            sem, ("sb_z", "sb_ln", "sb_sp", "sb_log", "sb_min", "sb_w", "sb_wm", "sb_y"))
        (mix_ret, mix_ssd, mix_sb, mixT_psum, mixT_hi, mixT_lo, wout_psum, x_mixed) = map(
            sem, ("mix_ret", "mix_ssd", "mix_sb", "mixT_psum", "mixT_hi", "mixT_lo", "wout_psum", "x_mixed"))
        (h2T_psum, h2T_ready, logits, gate_diff, gate_exp, sel_ready, ranks, routed) = map(
            sem, ("h2T_psum", "h2T_ready", "logits", "gate_diff", "gate_exp", "sel_ready", "ranks", "routed"))
        (cur_ready, sel_built, selgT_psum, selgT_ready, gath_psum, gath_hi, gath_lo) = map(
            sem, ("cur_ready", "sel_built", "selgT_psum", "selgT_ready", "gath_psum", "gath_hi", "gath_lo"))
        (gate_psum, up_psum, silu_done, s_ready, sT_psum, sT_hi, sT_lo) = map(
            sem, ("gate_psum", "up_psum", "silu_done", "s_ready", "sT_psum", "sT_hi", "sT_lo"))
        (y_psum, y_ready, comb_psum, x_added, stored, dve_step, act_step) = map(
            sem, ("y_psum", "y_ready", "comb_psum", "x_added", "stored", "dve_step", "act_step"))

        block = ctx.enter_context(nc.Block())

        def win_view(buf, slot, n):
            return buf[:, slot, 0:4 * n].rearrange("p (k n) -> p k n", k=4)

        def at(pos):
            return pos % 6, pos // 6

        @block.sync
        def _(sp):
            def load(slot, rnd, dst, src):
                if not isinstance(rnd, int) or rnd > 0:
                    sp.wait_ge(lo_ready[slot], rnd)
                sp.dma_start(dst, src).then_inc(landed[slot], 16)

            def mixer_weights(l):
                g = MIX_BASE[l]
                for name, c0, n in WIN:
                    src = w_in_d[l, :, c0:c0 + n].rearrange("(h k p) n -> h p k n", h=2, k=4)
                    for half in range(2):
                        load(g % 6, g // 6, win_view(raw, g % 6, n), src[half])
                        g += 1
                for n in range(2):
                    src = w_out_d[l, :, n * 512:(n + 1) * 512].rearrange("(h k p) n -> h p k n", h=2, k=4)
                    for half in range(2):
                        load(g % 6, g // 6, win_view(raw, g % 6, 512), src[half])
                        g += 1

            def item_weights(base_round, wg, wu, wd):
                gsrc = wg.rearrange("(h k p) (c n) -> c h p k n", h=2, k=4, n=512)
                usrc = wu.rearrange("(h k p) (c n) -> c h p k n", h=2, k=4, n=512)
                dsrc = wd.rearrange("(c h k p) n -> c h p k n", h=2, k=2, p=P)

                def gate_up(c, pos, rnd0):
                    for half in range(4):
                        slot, r = at(pos + half)
                        src = (gsrc if half < 2 else usrc)[c, half % 2]
                        load(slot, rnd0 + r, win_view(raw, slot, 512), src)

                def down(c, pos, rnd0):
                    for half in range(2):
                        slot, r = at(pos + half)
                        load(slot, rnd0 + r, raw[:, slot, :].rearrange("p (k n) -> p k n", k=2), dsrc[c, half])

                gate_up(0, 0, base_round)
                with sp.Fori(1, FC) as c:
                    gate_up(c, 4, base_round + (c - 1))
                    down(c - 1, 8, base_round + (c - 1))
                down(FC - 1, 6 * FC - 2, base_round)

            mixer_weights(0)
            with sp.Fori(0, DENSE_ITEMS) as i:
                item_weights(FFN_BASE[0] // 6 + i * FC, ffn_g_d[0], ffn_u_d[0], ffn_d_d[0])
            mixer_weights(1)
            with sp.Fori(0, E) as i:
                item_weights(FFN_BASE[1] // 6 + i * FC, moe_g_d[0][i], moe_u_d[0][i], moe_d_d[0][i])
            sp.wait_ge(routed, 1)
            n = sp.value_load(n_items[0:1, 0:1], min_val=E, max_val=2 * E)
            with sp.If(n > E):
                with sp.Fori(0, E) as i:
                    item_weights(FFN_BASE[1] // 6 + E * FC + i * FC, moe_g_d[0][i], moe_u_d[0][i], moe_d_d[0][i])
            sp.wait_ge(h_ready, 2 * 5)
            sp.dma_start(out_d[0].rearrange("(b p) d -> p b d", p=P), hm[:]).then_inc(stored, 16)
            sp.wait_ge(stored, 16)

        @block.gpsimd
        def _(pool):
            pool.memset(zeros[:], 0.0).then_inc(zeros_set, 1)
            pool.memset(xbc[:, :, 0:TAPS - 1], 0.0).then_inc(pad_set, 1)
            pool.dma_start(normw, norm1_d[0].partition_broadcast(P)).then_inc(normw_in, 16)
            for l in range(LAYERS):
                rows = prm_rows[:, l, :]
                pool.dma_start(rows[0:PRM_B], conv_w_d[l].rearrange("k (m c) -> (k m) c", c=P)).then_inc(prm_in, 16)
                pool.dma_start(rows[PRM_B:PRM_N], conv_b_d[l].rearrange("(m c) -> m c", c=P)).then_inc(prm_in, 16)
                pool.dma_start(rows[PRM_N:PRM_N + 2], ret_norm_d[l].rearrange("(m c) -> m c", c=P)).then_inc(prm_in, 16)
                pool.dma_start(rows[PRM_N + 2:PRM], ssd_norm_d[l].rearrange("(m c) -> m c", c=P)).then_inc(prm_in, 16)
                for i, src in enumerate((dt_bias_d, a_log_d, d_skip_d)):
                    pool.dma_start(heads8[:, l, i, :], src[l].partition_broadcast(P)).then_inc(prm_in, 16)
            pool.dma_start(rw[:], router_d[0].rearrange("(k p) e -> p k e", p=P)).then_inc(rw_in, 16)
            for l in range(LAYERS):
                pool.wait_ge(sb_z, l + 1)
                pool.wait_ge(normw_in, 16 * (2 * l + 1))
                pool.dma_start(normw, norm2_d[l].partition_broadcast(P)).then_inc(normw_in, 16)
                if l + 1 < LAYERS:
                    pool.wait_ge(mix_sb, l + 1)
                    pool.memset(xbc[:, :, 0:TAPS - 1], 0.0).then_inc(pad_set, 1)
                pool.wait_ge(h_ready, 2 * (2 * l + 2))
                pool.wait_ge(normw_in, 16 * (2 * l + 2))
                nxt = norm1_d[l + 1] if l + 1 < LAYERS else final_d
                pool.dma_start(normw, nxt.partition_broadcast(P)).then_inc(normw_in, 16)

        @block.scalar
        def _(act):
            steps = [0]

            def chain(ins):
                steps[0] += 1
                ins.then_inc(act_step, 1)
                act.wait_ge(act_step, steps[0])

            act.dma_start(x[:], x_d[0].rearrange("(b p) d -> p b d", p=P)).then_inc(x_in, 16)
            act.dma_start(cst[:], const_d[:, :]).then_inc(const_in, 16)

            def norm(u):
                for b in range(NB):
                    nc.scalar.activation(hm[:, b, :], x[:, b, :], ACT.Square, accum_out=sm(0)[:, b:b + 1])\
                        .then_inc(sumsq, 1)
                act.wait_ge(sumsq, 2 * (u + 1))
                nc.scalar.activation(sm(1)[:, 0:2], sm(0)[:, 0:2], ACT.Sqrt, bias=eps_ap, scale=1.0 / D)\
                    .then_inc(rms_ready, 1)

            def split(g, slot, rnd, n=SUB):
                act.wait_ge(landed[slot], (rnd + 1) * 16)
                if not isinstance(g, int) or g >= SPL:
                    act.wait_ge(split_used, g - (SPL - 1))
                nc.scalar.activation(w_hi[:, slot % SPL, 0:n], raw[:, slot, 0:n], ACT.Copy).then_inc(hi_ready, 1)

            def win_split(l, ci):
                for half in range(2):
                    g = MIX_BASE[l] + 2 * ci + half
                    split(g, g % 6, g // 6, 4 * WIN[ci][2])

            def mixer(l):
                act.wait_ge(prm_psum, l + 1)
                nc.scalar.activation(prm[:], ps[:, 0, 0:PRM], ACT.Copy).then_inc(prm_ready, 1)
                for q in range(4):
                    act.wait_ge(hT_psum, 4 * l + q + 1)
                    nc.scalar.activation(aT_hi[:, 4 * q:4 * q + 4, :].rearrange("p a b -> p (a b)"),
                                         ps[:, 4 + q, :], ACT.Copy).then_inc(hT_hi, 1)
                    if q < 2:
                        g = MIX_BASE[l] + q
                        split(g, g % 6, g // 6, 4 * WIN[0][2])
                win_split(l, 1)
                act.wait_ge(win_psum, 7 * l + 1)
                act.wait_ge(pad_set, l + 1)
                nc.scalar.activation(xbc[:, 0:4, TAPS - 1:], banks(0, 2).rearrange("p (m t) -> p m t", m=4),
                                     ACT.Copy).then_inc(win_out, 1)
                win_split(l, 2)
                act.wait_ge(win_psum, 7 * l + 2)
                nc.scalar.activation(xbc[:, 4:6, TAPS - 1:], ps[:, 2, :].rearrange("p (m t) -> p m t", m=2), ACT.Copy)
                nc.scalar.activation(sm(2), ps[:, 3, 0:16], ACT.Copy).then_inc(win_out, 1)
                act.wait_ge(prm_in, 16 * 7 * LAYERS)
                nc.scalar.activation(sm(3, 8), heads8[:, l, 1, :], ACT.Exp)
                act.wait_ge(dt_biased, l + 1)
                chain(nc.scalar.activation(sm(4), sm(2), ACT.Abs))
                chain(nc.scalar.activation(sm(4), sm(4), ACT.Exp, scale=-1.0))
                nc.scalar.activation(sm(5), sm(4), ACT.Ln, bias=1.0).then_inc(dt_ln, 1)
                win_split(l, 3)
                act.wait_ge(win_psum, 7 * l + 3)
                nc.scalar.activation(scr[:, 2, 0:1024], banks(0, 2), ACT.Copy).then_inc(win_out, 1)
                act.wait_ge(conv_tap, TAPS * (l + 1))
                nc.scalar.activation(cvf, cvf, ACT.Silu).then_inc(conv_silu, 1)
                act.wait_ge(cs_psum, l + 1)
                nc.scalar.activation(csT, ps[0:SH, 4, P:P + T], ACT.Copy).then_inc(csT_ready, 1)
                win_split(l, 4)
                act.wait_ge(win_psum, 7 * l + 4)
                if l > 0:
                    act.wait_ge(h_ready, 2 * (2 * l + 1))
                nc.scalar.activation(bqk[:, 0:2, :].rearrange("p a b -> p (a b)"), ps[:, 2, :], ACT.Copy,
                                     scale=HD ** -0.5)
                nc.scalar.activation(bqk[:, 2:4, :].rearrange("p a b -> p (a b)"), ps[:, 3, :], ACT.Copy)\
                    .then_inc(win_out, 1)
                win_split(l, 5)
                for b in range(NB):
                    act.wait_ge(xT_psum, 2 * l + b + 1)
                    nc.scalar.activation(xtok[:, b, :], ps[:, 7 if b == 0 else 4, :], ACT.Copy).then_inc(xtok_ready, 1)
                act.wait_ge(win_psum, 7 * l + 5)
                pv = ps[:, 0:2, :]
                nc.scalar.activation(rv[:], pv[:, :, 0:256], ACT.Copy)
                nc.scalar.activation(rg[:], pv[:, :, 256:512], ACT.Silu).then_inc(win_out, 1)
                win_split(l, 6)
                act.wait_ge(win_psum, 7 * l + 6)
                nc.scalar.activation(bv[:], ps[:, 2:4, 0:256], ACT.Copy).then_inc(win_out, 1)
                act.wait_ge(win_psum, 7 * l + 7)
                nc.scalar.activation(sz[:].rearrange("p a b -> p (a b)"), banks(0, 2), ACT.Silu).then_inc(win_out, 1)
                for g in range(2):
                    gg = MIX_BASE[l] + 14 + g
                    split(gg, gg % 6, gg // 6)
                for g in range(SG):
                    act.wait_ge(seg_ready, 2 * l + g + 1)
                    nc.scalar.activation(scr[:, g, :], scr[:, g, :], ACT.Exp).then_inc(seg_exp, 1)
                act.wait_ge(sb_z, l + 1)
                chain(nc.scalar.activation(xbf.rearrange("p (h n) -> p h n", h=BH), ps[:, 4:8, 0:SC], ACT.Abs))
                chain(nc.scalar.activation(xbf, xbf, ACT.Exp, scale=-1.0))
                nc.scalar.activation(xbf, xbf, ACT.Ln, bias=1.0).then_inc(sb_ln, 1)
                act.wait_ge(sb_min, l + 1)
                nc.scalar.activation(xbf, xbf, ACT.Exp).then_inc(sb_w, 1)
                act.wait_ge(ret_var, l + 1)
                nc.scalar.activation(sm(9, 8), sm(9, 8), ACT.Sqrt, bias=eps_ap, scale=1.0 / HD).then_inc(ret_std, 1)
                act.wait_ge(gated, l + 1)
                for b in range(NB):
                    for g in range(SG):
                        nc.scalar.activation(xdt[:, b, g * 256:(g + 1) * 256], sz[:, b, g * 256:(g + 1) * 256],
                                             ACT.Square, accum_out=sm(10)[:, 2 * b + g:2 * b + g + 1])\
                            .then_inc(gated_sq, 1)
                act.wait_ge(gated_sq, 4 * (l + 1))
                nc.scalar.activation(sm(10, 4), sm(10, 4), ACT.Sqrt, bias=eps_ap, scale=1.0 / 256).then_inc(ssd_rms, 1)
                act.wait_ge(sb_y, l + 1)
                nc.scalar.activation(hm[:, :, 768:1024], ps[:, 1, :].rearrange("p (b n) -> p b n", b=NB),
                                     ACT.Copy, scale=-1.0).then_inc(mix_sb, 1)
                for q in range(4):
                    act.wait_ge(mixT_psum, 4 * l + q + 1)
                    for k in (2 * q, 2 * q + 1):
                        dst = aT_hi[:, 2 * k:2 * k + 2, :].rearrange("p a b -> p (a b)")
                        src = ps[:, 4 + q, (k % 2) * 256:(k % 2) * 256 + 256]
                        if k < 6:
                            ins = nc.scalar.activation(dst, src, ACT.Copy, scale=prm[:, PRM_N + k:PRM_N + k + 1])
                        else:
                            ins = nc.scalar.activation(dst, src, ACT.Copy)
                    ins.then_inc(mixT_hi, 1)
                for g in range(2, 4):
                    gg = MIX_BASE[l] + 14 + g
                    split(gg, gg % 6, gg // 6)

            def item(i, ph):
                it = i + ITEM_BASE[ph]
                g0 = i * ITEM_SUBS + FFN_BASE[ph]
                r0 = i * FC + FFN_BASE[ph] // 6

                def sp_(pos, c=None):
                    slot, r = at(pos)
                    if c is None:
                        split(g0 + pos, slot, r0 + r)
                    else:
                        split(g0 + pos + (c - 1) * 6, slot, r0 + r + (c - 1))

                def silu(c):
                    act.wait_ge(gate_psum, it * FC + c + 1)
                    nc.scalar.activation(silu_g, ps[:, 0, :], ACT.Silu).then_inc(silu_done, 1)

                def evac_sT(c):
                    act.wait_ge(sT_psum, it * FC + c + 1)
                    nc.scalar.activation(aT_hi[:, 8:12, :].rearrange("p a b -> p (a b)"), ps[:, 2, :], ACT.Copy)\
                        .then_inc(sT_hi, 1)

                sp_(0)
                sp_(1)
                for q in range(2):
                    act.wait_ge(gath_psum, it * 2 + q + 1)
                    nc.scalar.activation(aT_hi[:, 4 * q:4 * q + 4, :].rearrange("p a b -> p (a b)"),
                                         ps[:, 5 + q, :], ACT.Copy).then_inc(gath_hi, 1)
                sp_(2)
                nc.scalar.activation(selgT, ps[:, 7, 0:256].rearrange("p (b s) -> p b s", b=NB), ACT.Copy)\
                    .then_inc(selgT_ready, 1)
                sp_(3)
                silu(0)
                with act.Fori(1, FC) as c:
                    sp_(4, c)
                    sp_(5, c)
                    sp_(6, c)
                    evac_sT(c - 1)
                    sp_(7, c)
                    act.wait_ge(s_ready, it * FC + c)
                    silu(c)
                    sp_(8, c)
                    sp_(9, c)
                sp_(6 * FC - 2)
                evac_sT(FC - 1)
                sp_(6 * FC - 1)
                act.wait_ge(y_psum, it + 1)
                nc.scalar.activation(y_sb, banks(3, 5), ACT.Copy).then_inc(y_ready, 1)

            eps_ap = EPS
            act.wait_ge(x_in, 16)
            norm(0)
            act.wait_ge(const_in, 16)
            mixer(0)
            act.wait_ge(x_mixed, 2)
            norm(1)
            with act.Fori(0, DENSE_ITEMS) as i:
                item(i, 0)
            act.wait_ge(x_added, 2 * DENSE_ITEMS)
            norm(2)
            mixer(1)
            act.wait_ge(x_mixed, 4)
            norm(3)
            for q in range(4):
                act.wait_ge(h2T_psum, q + 1)
                nc.scalar.activation(h2T[:, 4 * q:4 * q + 4, :].rearrange("p a b -> p (a b)"), ps[:, q, :], ACT.Copy)\
                    .then_inc(h2T_ready, 1)
            act.wait_ge(gate_diff, 1)
            nc.scalar.activation(sm(6, 2), sm(6, 2), ACT.Exp).then_inc(gate_exp, 1)
            act.wait_ge(routed, 1)
            n = act.value_load(n_items[0:1, 0:1], min_val=E, max_val=2 * E)
            with act.Fori(0, n) as i:
                item(i, 1)
            act.wait_ge(x_added, n * 2 + 2 * DENSE_ITEMS)
            norm(4)

        @block.vector
        def _(dve):
            steps = [0]
            V = nc.vector

            def chain(ins):
                steps[0] += 1
                ins.then_inc(dve_step, 1)
                dve.wait_ge(dve_step, steps[0])

            def norm(u):
                dve.wait_ge(rms_ready, u + 1)
                V.reciprocal(sm(1)[:, 2:4], sm(1)[:, 0:2]).then_inc(rstd_ready, 1)
                dve.wait_ge(rstd_ready, u + 1)
                dve.wait_ge(normw_in, 16 * (u + 1))
                for b in range(NB):
                    V.scalar_tensor_tensor(hm[:, b, :], x[:, b, :], sm(1)[:, 2 + b:3 + b], normw, ALU.mult, ALU.mult)\
                        .then_inc(h_ready, 1)

            def split(g, slot, n=SUB):
                dve.wait_ge(hi_ready, g + 1)
                V.tensor_tensor(w_lo[:, slot % SPL, 0:n], raw[:, slot, 0:n], w_hi[:, slot % SPL, 0:n].bitcast(F32),
                                ALU.subtract).then_inc(lo_ready[slot], 1)

            def win_split(l, ci):
                for half in range(2):
                    g = MIX_BASE[l] + 2 * ci + half
                    split(g, g % 6, 4 * WIN[ci][2])

            def lo_part(dst, src, hi):
                return V.tensor_tensor(dst.rearrange("p a b -> p (a b)"), src,
                                       hi.rearrange("p a b -> p (a b)").bitcast(F32), ALU.subtract)

            def bc(ap, shape):
                return ap.to_broadcast(shape)

            def mixer(l):
                for q in range(4):
                    dve.wait_ge(hT_hi, 4 * l + q + 1)
                    lo_part(aT_lo[:, 4 * q:4 * q + 4, :], ps[:, 4 + q, :], aT_hi[:, 4 * q:4 * q + 4, :])\
                        .then_inc(hT_lo, 1)
                    if q < 2:
                        g = MIX_BASE[l] + q
                        split(g, g % 6, 4 * WIN[0][2])
                win_split(l, 1)
                win_split(l, 2)
                dve.wait_ge(prm_in, 16 * 7 * LAYERS)
                dve.wait_ge(win_out, 7 * l + 2)
                V.tensor_tensor(sm3(2), sm3(2), bc(heads8[:, l, 0, :].unsqueeze(1), [P, NB, SH]), ALU.add)\
                    .then_inc(dt_biased, 1)
                dve.wait_ge(prm_ready, l + 1)
                for tap in range(TAPS - 1, -1, -1):
                    for m in range(XT):
                        w = prm[:, tap * XT + m:tap * XT + m + 1]
                        src = xbc[:, m, tap:tap + T]
                        if tap == TAPS - 1:
                            ins = V.tensor_scalar(cv[:, m, :], src, w, prm[:, PRM_B + m:PRM_B + m + 1],
                                                  ALU.mult, ALU.add)
                        else:
                            ins = V.scalar_tensor_tensor(cv[:, m, :], src, w, cv[:, m, :], ALU.mult, ALU.add)
                    ins.then_inc(conv_tap, 1)
                    dve.wait_ge(conv_tap, TAPS * l + TAPS - tap)
                    if tap == 2:
                        dve.wait_ge(dt_ln, l + 1)
                        chain(V.tensor_scalar(sm(6), sm(4), 1.0, None, ALU.add))
                        chain(V.scalar_tensor_tensor(sm(4), sm(6), -1.0, sm(4), ALU.add, ALU.subtract))
                        chain(V.reciprocal(sm(6), sm(6)))
                        chain(V.tensor_tensor(sm(4), sm(4), sm(6), ALU.mult))
                        chain(V.tensor_tensor(sm(5), sm(5), sm(4), ALU.subtract))
                        chain(V.scalar_tensor_tensor(sm(5), sm(2), 0.0, sm(5), ALU.max, ALU.add))
                        V.scalar_tensor_tensor(sm3(6), sm3(5), -1.0, bc(sm(3, 8).unsqueeze(1), [P, NB, SH]),
                                               ALU.mult, ALU.mult).then_inc(a_ready, 1)
                        win_split(l, 3)
                win_split(l, 4)
                dve.wait_ge(csT_ready, l + 1)
                V.tensor_copy(sm(7), ps[:, 4, 0:16]).then_inc(cs_ready, 1)
                for g in range(SG):
                    dve.wait_ge(cb_psum, 2 * l + g + 1)
                    V.tensor_tensor(cb[:, g, :], ps[:, 5 + g, 0:SC], cst[:, C_CAUSAL:C_CAUSAL + SC], ALU.mult)\
                        .then_inc(cb_ready, 1)
                dve.wait_ge(win_out, 7 * l + 3)
                v4 = lambda a: a.rearrange("p (m t) -> p m t", m=4)
                V.tensor_tensor(v4(scr[:, 0, 0:1024]), v4(scr[:, 2, 0:1024]),
                                bc(cst[:, C_COS:C_COS + T].unsqueeze(1), [P, 4, T]), ALU.mult)
                win_split(l, 5)
                for b in range(NB):
                    dve.wait_ge(xtok_ready, 2 * l + b + 1)
                    V.tensor_tensor(xdt[:, b, :].rearrange("p (h d) -> p h d", h=SH),
                                    ps[:, 7 if b == 0 else 4, :].rearrange("p (h d) -> p h d", h=SH),
                                    bc(sm(5)[:, 8 * b:8 * b + 8].unsqueeze(2), [P, SH, HD]), ALU.mult)\
                        .then_inc(xdt_ready, 1)
                dve.wait_ge(rot_psum, l + 1)
                chain(V.tensor_tensor(v4(scr[:, 1, 0:1024]), v4(banks(5, 7)),
                                      bc(cst[:, C_SIN:C_SIN + T].unsqueeze(1), [P, 4, T]), ALU.mult))
                V.tensor_tensor(qkr[:, 0:1024], scr[:, 0, 0:1024], scr[:, 1, 0:1024], ALU.add).then_inc(qk_ready, 1)
                dve.wait_ge(qk_ready, l + 1)
                win_split(l, 6)
                for g in range(2):
                    gg = MIX_BASE[l] + 14 + g
                    split(gg, gg % 6)
                dve.wait_ge(ret_psum, l + 1)
                V.tensor_tensor(scr[:, 2, :].rearrange("p (h n) -> p h n", h=RH), ps[:, 4:8, 0:SC],
                                cst[:, C_RET:C_RET + RH * SC].rearrange("p (h n) -> p h n", h=RH), ALU.mult)\
                    .then_inc(s_ret, 1)
                for g in range(SG):
                    dve.wait_ge(csb_psum, 2 * l + g + 1)
                    for hh in range(4):
                        h = 4 * g + hh
                        src = ps[:, (2 if g == 0 else 0) + hh // 2, (hh % 2) * T:(hh % 2) * T + T]
                        V.tensor_scalar(scr[:, g, hh * SC:hh * SC + T], src, sm(7)[:, h:h + 1], 0.0,
                                        ALU.subtract, ALU.min)
                        ins = V.tensor_scalar(scr[:, g, hh * SC + T:hh * SC + SC], src[:, P:T],
                                              sm(7)[:, 8 + h:9 + h], 0.0, ALU.subtract, ALU.min)
                    ins.then_inc(seg_ready, 1)
                z4 = ps[:, 4:8, 0:SC]
                xb4 = xbf.rearrange("p (h n) -> p h n", h=BH)
                sp4 = qkr[:].rearrange("p (h n) -> p h n", h=BH)
                strict = bc(cst[:, C_STRICT:C_STRICT + SC].unsqueeze(1), [P, BH, SC])
                for g in range(SG):
                    dve.wait_ge(seg_exp, 2 * l + g + 1)
                    s4 = scr[:, g, :].rearrange("p (h n) -> p h n", h=4)
                    V.tensor_tensor(s4, s4, bc(cb[:, g, :].unsqueeze(1), [P, 4, SC]), ALU.mult).then_inc(s_ssd, 1)
                dve.wait_ge(sb_ln, l + 1)
                chain(V.scalar_tensor_tensor(sp4, z4, 0.0, xb4, ALU.max, ALU.add))
                V.tensor_tensor(sp4, sp4, strict, ALU.mult).then_inc(sb_sp, 1)
                for b in range(NB):
                    dve.wait_ge(xtok_ready, 2 * l + b + 1)
                    xh = xtok[:, b, :].rearrange("p (h d) -> p h d", h=SH)
                    ins = V.tensor_tensor(xh, xh, bc(heads8[:, l, 2, :].unsqueeze(2), [P, SH, HD]), ALU.mult)
                chain(ins)
                r8 = lambda a: a.rearrange("p (h d) -> p h d", h=8)
                ry = ps[:, 0, :]
                dve.wait_ge(ret_y, l + 1)
                chain(V.tensor_reduce(sm(8, 8), r8(ry), AX.X, ALU.add))
                chain(V.tensor_scalar(sm(8, 8), sm(8, 8), 1.0 / HD, None, ALU.mult))
                chain(V.tensor_tensor(r8(cvf[:, 0:512]), r8(ry), bc(sm(8, 8).unsqueeze(2), [P, 8, HD]), ALU.subtract))
                chain(V.tensor_tensor(cvf[:, 512:1024], cvf[:, 0:512], cvf[:, 0:512], ALU.mult))
                V.tensor_reduce(sm(9, 8), r8(cvf[:, 512:1024]), AX.X, ALU.add).then_inc(ret_var, 1)
                dve.wait_ge(sb_log, l + 1)
                V.tensor_scalar(xb4, z4, 0.0, None, ALU.min).then_inc(sb_min, 1)
                dve.wait_ge(ssd_y, l + 1)
                xf = xtok[:].rearrange("p a b -> p (a b)")
                szf = sz[:].rearrange("p a b -> p (a b)")
                chain(V.tensor_tensor(xf, banks(2, 4), xf, ALU.add))
                dve.wait_ge(win_out, 7 * l + 7)
                V.tensor_tensor(szf, szf, xf, ALU.mult).then_inc(gated, 1)
                dve.wait_ge(sb_w, l + 1)
                V.tensor_tensor(xb4, xb4, strict, ALU.mult).then_inc(sb_wm, 1)
                dve.wait_ge(ret_std, l + 1)
                chain(V.reciprocal(sm(9, 8), sm(9, 8)))
                chain(V.tensor_tensor(r8(cvf[:, 0:512]), r8(cvf[:, 0:512]), bc(sm(9, 8).unsqueeze(2), [P, 8, HD]),
                                      ALU.mult))
                V.tensor_tensor(hm[:, :, 0:256], cvf[:, 0:512].rearrange("p (b n) -> p b n", b=NB), rg[:], ALU.mult)\
                    .then_inc(mix_ret, 1)
                dve.wait_ge(ssd_rms, l + 1)
                chain(V.reciprocal(sm(10, 4), sm(10, 4)))
                for b in range(NB):
                    ins = V.tensor_tensor(hm[:, b, 256:768].rearrange("p (g n) -> p g n", g=SG),
                                          sz[:, b, :].rearrange("p (g n) -> p g n", g=SG),
                                          bc(sm(10)[:, 2 * b:2 * b + 2].unsqueeze(2), [P, SG, 256]), ALU.mult)
                ins.then_inc(mix_ssd, 1)
                for q in range(4):
                    dve.wait_ge(mixT_hi, 4 * l + q + 1)
                    for k in (2 * q, 2 * q + 1):
                        dst = aT_lo[:, 2 * k:2 * k + 2, :].rearrange("p a b -> p (a b)")
                        hi = aT_hi[:, 2 * k:2 * k + 2, :].rearrange("p a b -> p (a b)").bitcast(F32)
                        src = ps[:, 4 + q, (k % 2) * 256:(k % 2) * 256 + 256]
                        if k < 6:
                            ins = V.scalar_tensor_tensor(dst, src, prm[:, PRM_N + k:PRM_N + k + 1], hi,
                                                         ALU.mult, ALU.subtract)
                        else:
                            ins = V.tensor_tensor(dst, src, hi, ALU.subtract)
                    ins.then_inc(mixT_lo, 1)
                for g in range(2, 4):
                    gg = MIX_BASE[l] + 14 + g
                    split(gg, gg % 6)
                for n in range(2):
                    dve.wait_ge(wout_psum, 2 * l + n + 1)
                    for b in range(NB):
                        xs = x[:, b, n * 512:(n + 1) * 512]
                        ins = V.tensor_tensor(xs, ps[:, 2 * b + n, :], xs, ALU.add)
                    ins.then_inc(x_mixed, 1)

            def route():
                lg, oh1, oh2, tmp, t2, gts = (sm3(i) for i in (11, 12, 13, 14, 15, 3))
                e8 = bc(cst[:, C_E8:C_E8 + E].unsqueeze(1), [P, NB, E])
                col = lambda i: bc(sm(i, 2).unsqueeze(2), [P, NB, E])
                dve.wait_ge(logits, 1)
                chain(V.tensor_copy(sm(11), ps[:, 4, 0:16]))
                chain(V.tensor_reduce(sm(8, 2), lg, AX.X, ALU.max))
                chain(V.tensor_tensor(tmp, lg, col(8), ALU.is_equal))
                chain(V.tensor_tensor(tmp, tmp, e8, ALU.mult))
                chain(V.tensor_reduce(sm(9, 2), tmp, AX.X, ALU.min))
                chain(V.tensor_tensor(oh1, e8, col(9), ALU.is_equal))
                chain(V.scalar_tensor_tensor(t2, oh1, -3e38, lg, ALU.mult, ALU.add))
                chain(V.tensor_reduce(sm(10, 2), t2, AX.X, ALU.max))
                V.tensor_tensor(sm(6, 2), sm(10, 2), sm(8, 2), ALU.subtract).then_inc(gate_diff, 1)
                chain(V.tensor_tensor(tmp, t2, col(10), ALU.is_equal))
                chain(V.tensor_tensor(tmp, tmp, e8, ALU.mult))
                chain(V.tensor_reduce(sm(9, 2), tmp, AX.X, ALU.min))
                chain(V.tensor_tensor(oh2, e8, col(9), ALU.is_equal))
                V.tensor_tensor(lg, oh1, oh2, ALU.add).then_inc(sel_ready, 1)
                dve.wait_ge(gate_exp, 1)
                chain(V.tensor_scalar(sm(7, 2), sm(6, 2), 1.0, None, ALU.add))
                chain(V.reciprocal(sm(7, 2), sm(7, 2)))
                chain(V.tensor_tensor(sm(6, 2), sm(6, 2), sm(7, 2), ALU.mult))
                chain(V.tensor_tensor(gts, oh1, col(7), ALU.mult))
                chain(V.tensor_tensor(tmp, oh2, col(6), ALU.mult))
                for half in range(2):
                    V.tensor_tensor(rank_gate[:, 1, :, E * half:E * half + E], gts, tmp, ALU.add)
                dve.wait_ge(sel_ready, 1)
                dve.wait_ge(ranks, 1)
                chain(V.scalar_tensor_tensor(t2, ps[:, 5, 0:16].rearrange("p (b e) -> p b e", b=NB), 1.0, lg,
                                             ALU.add, ALU.mult))
                for half in range(2):
                    V.tensor_scalar(rank_gate[:, 0, :, E * half:E * half + E], t2, -1.0 - P * half, None, ALU.add)
                chain(V.tensor_reduce(sm(8, 1), ps[:, 5, 16:16 + E], AX.X, ALU.max))
                chain(V.tensor_scalar(sm(8, 1), sm(8, 1), float(P), float(E), ALU.is_gt, ALU.mult))
                V.tensor_scalar(n_items[:], sm(8, 1), float(E), None, ALU.add).then_inc(routed, 1)
                dve.wait_ge(routed, 1)

            def item(i, ph):
                it = i + ITEM_BASE[ph]
                g0 = i * ITEM_SUBS + FFN_BASE[ph]

                def lo(pos, c=None):
                    split(g0 + pos if c is None else g0 + pos + (c - 1) * 6, pos % 6)

                def evac_sT(c):
                    dve.wait_ge(sT_hi, it * FC + c + 1)
                    lo_part(aT_lo[:, 8:12, :], ps[:, 2, :], aT_hi[:, 8:12, :]).then_inc(sT_lo, 1)

                def gate_times_up(c):
                    dve.wait_ge(silu_done, it * FC + c + 1)
                    dve.wait_ge(up_psum, it * FC + c + 1)
                    V.tensor_tensor(s_act, ps[:, 1, :], silu_g, ALU.mult).then_inc(s_ready, 1)

                V.tensor_copy(cur[:].rearrange("p a b -> p (a b)").unsqueeze(2),
                              rank_gate[:, :, :, bass.ds(i, 1)].rearrange("p a b i -> p (a b) i")).then_inc(cur_ready, 1)
                dve.wait_ge(cur_ready, it + 1)
                for b in range(NB):
                    V.tensor_scalar(sel[:, b, :], iota, cur[:, 0, b:b + 1], None, ALU.is_equal)
                    ins = V.tensor_scalar(selg[:, b, :], iota, cur[:, 0, b:b + 1], cur[:, 1, b:b + 1],
                                          ALU.is_equal, ALU.mult)
                ins.then_inc(sel_built, 1)
                lo(0)
                lo(1)
                for q in range(2):
                    dve.wait_ge(gath_hi, it * 2 + q + 1)
                    lo_part(aT_lo[:, 4 * q:4 * q + 4, :], ps[:, 5 + q, :], aT_hi[:, 4 * q:4 * q + 4, :])\
                        .then_inc(gath_lo, 1)
                lo(2)
                lo(3)
                gate_times_up(0)
                with dve.Fori(1, FC) as c:
                    lo(4, c)
                    lo(5, c)
                    lo(6, c)
                    evac_sT(c - 1)
                    lo(7, c)
                    lo(8, c)
                    lo(9, c)
                    gate_times_up(c)
                lo(6 * FC - 2)
                evac_sT(FC - 1)
                lo(6 * FC - 1)
                for b in range(NB):
                    dve.wait_ge(comb_psum, it * 2 + b + 1)
                    V.tensor_tensor(x[:, b, :], banks(5, 7) if b == 0 else banks(0, 2), x[:, b, :], ALU.add)\
                        .then_inc(x_added, 1)
                dve.wait_ge(x_added, it * 2 + 2)

            dve.wait_ge(x_in, 16)
            norm(0)
            dve.wait_ge(const_in, 16)
            V.tensor_copy(rank_gate[:].rearrange("p a b i -> p (a b i)"), cst[:, C_RG:C_RG + 64])
            mixer(0)
            norm(1)
            with dve.Fori(0, DENSE_ITEMS) as i:
                item(i, 0)
            norm(2)
            mixer(1)
            norm(3)
            route()
            n = dve.value_load(n_items[0:1, 0:1], min_val=E, max_val=2 * E)
            with dve.Fori(0, n) as i:
                item(i, 1)
            norm(4)

        @block.tensor
        def _(pe):
            mm = nc.tensor.matmul

            def passes(out, lhs_hi, lhs_lo, rhs_hi, rhs_lo, start, stop):
                mm(out, lhs_hi, rhs_hi, start=start, stop=False, skip_group_check=True)
                mm(out, lhs_hi, rhs_lo, start=False, stop=False, skip_group_check=True)
                return mm(out, lhs_lo, rhs_hi, start=False, stop=stop, skip_group_check=True)

            def win_chunk(l, ci):
                name, _, n = WIN[ci]
                par = 2 * (ci % 2)
                if ci >= 2:
                    pe.wait_ge(win_out, 7 * l + ci - 1)
                tiles = TILES_T.get(name, 0)
                for half in range(2):
                    g = MIX_BASE[l] + 2 * ci + half
                    pe.wait_ge(lo_ready[g % 6], g // 6 + 1)
                    hi, lo = win_view(w_hi, g % SPL, n), win_view(w_lo, g % SPL, n)
                    first = half == 0
                    for m in range(tiles):
                        out = banks(par, par + 2)[:, m * T:(m + 1) * T]
                        for kk in range(4):
                            k = 4 * half + kk
                            cols = slice(m * P, (m + 1) * P)
                            ins = passes(out, hi[:, kk, cols], lo[:, kk, cols],
                                         aT_hi[:, 2 * k:2 * k + 2, :].rearrange("p a b -> p (a b)"),
                                         aT_lo[:, 2 * k:2 * k + 2, :].rearrange("p a b -> p (a b)"),
                                         start=first and kk == 0 and m % 2 == 0, stop=k == KD - 1)
                    c0 = tiles * P
                    if c0 < n:
                        for b in range(NB):
                            if tiles:
                                out = ps[:, par + 1, 8 * b:8 * b + n - c0]
                            else:
                                out = ps[:, par + b, 0:n]
                            for kk in range(4):
                                k = 4 * half + kk
                                ins = passes(out, aT_hi[:, 2 * k + b, :], aT_lo[:, 2 * k + b, :],
                                             hi[:, kk, c0:n], lo[:, kk, c0:n],
                                             start=first and kk == 0 and not (tiles and b), stop=k == KD - 1)
                    ins.then_inc(split_used, 1)
                pe.wait_ge(split_used, MIX_BASE[l] + 2 * ci + 2)
                pe.sem_inc(win_psum, 1)

            def scores(dst, q, k):
                mm(dst[:, 0:T], k[:, 0:P], q, start=True, stop=True, skip_group_check=True)
                return mm(dst[:, T:SC], k[:, P:T], q[:, P:T], start=False, stop=True, skip_group_check=True)

            def weighted(dst, s, v, b):
                if b == 0:
                    return mm(dst, s[:, 0:P], v[:, 0], start=True, stop=True, skip_group_check=True)
                mm(dst, s[:, P:T], v[:, 0], start=True, stop=False, skip_group_check=True)
                return mm(dst, s[:, T:SC], v[:, 1], start=False, stop=True, skip_group_check=True)

            def mixer(l):
                pe.wait_ge(prm_in, 16 * 7 * LAYERS)
                pe.wait_ge(h_ready, 2 * (2 * l + 1))
                nc.tensor.transpose(ps[:, 0, 0:PRM], prm_rows[:, l, :], cst[0:PRM, C_ID:C_ID + PRM]).then_inc(prm_psum, 1)
                for q in range(4):
                    for j in range(4):
                        k, b = (4 * q + j) // 2, j % 2
                        ins = nc.tensor.transpose(ps[:, 4 + q, j * P:(j + 1) * P], hm[:, b, k * P:(k + 1) * P], ident)
                    ins.then_inc(hT_psum, 1)
                pe.wait_ge(hT_lo, 4 * (l + 1))
                pe.wait_ge(prm_ready, l + 1)
                win_chunk(l, 0)
                win_chunk(l, 1)
                win_chunk(l, 2)
                pe.wait_ge(a_ready, l + 1)
                a3 = sm3(6)
                c4 = ps[:, 4, :]
                opts = dict(skip_group_check=True)
                mm(c4[:, 0:8], m_le, a3[:, 0], start=True, stop=True, **opts)
                mm(c4[:, 8:16], ones, a3[:, 0], start=False, stop=False, **opts)
                mm(c4[:, 8:16], m_le, a3[:, 1], start=False, stop=True, **opts)
                cT = ps[0:SH, 4, P:P + T]
                mm(cT[:, 0:P], a3[:, 0], m_le, start=False, stop=True, **opts)
                mm(cT[:, P:T], a3[:, 0], ones, start=False, stop=False, **opts)
                mm(cT[:, P:T], a3[:, 1], m_le, start=False, stop=True, **opts).then_inc(cs_psum, 1)
                pe.wait_ge(conv_silu, l + 1)
                for g in range(SG):
                    s = slice(HD * g, HD * g + HD)
                    scores(ps[:, 5 + g, :], cv[s, 5, :], cv[s, 4, :]).then_inc(cb_psum, 1)
                win_chunk(l, 3)
                pe.wait_ge(cs_ready, l + 1)
                pe.wait_ge(csT_ready, l + 1)
                for b in range(NB):
                    for m in range(4):
                        ins = nc.tensor.transpose(ps[:, 7 if b == 0 else 4, m * P:(m + 1) * P],
                                                  cv[:, m, b * P:(b + 1) * P], ident)
                    ins.then_inc(xT_psum, 1)
                pe.wait_ge(cb_ready, 2 * (l + 1))
                for m in range(4):
                    ins = mm(banks(5, 7)[:, m * T:(m + 1) * T], rot, scr[:, 2, m * T:(m + 1) * T],
                             start=True, stop=True, **opts)
                ins.then_inc(rot_psum, 1)
                win_chunk(l, 4)
                win_chunk(l, 5)
                win_chunk(l, 6)
                pe.wait_ge(qk_ready, l + 1)
                pe.wait_ge(xdt_ready, 2 * (l + 1))
                pe.wait_ge(xtok_ready, 2 * (l + 1))
                for h in range(RH):
                    s = slice(HD * (h % 2), HD * (h % 2) + HD)
                    q, k = h // 2 * T, (2 + h // 2) * T
                    ins = scores(ps[:, 4 + h, :], qkr[s, q:q + T], qkr[s, k:k + T])
                ins.then_inc(ret_psum, 1)
                for g in range(SG):
                    pe.wait_ge(win_out, 7 * l + 6 + g)
                    for hh in range(4):
                        h = 4 * g + hh
                        ins = mm(ps[:, (2 if g == 0 else 0) + hh // 2, (hh % 2) * T:(hh % 2) * T + T],
                                 cst[0:SH, C_ID + h:C_ID + h + 1].to_broadcast([SH, P]), csT,
                                 start=True, stop=True, **opts)
                    ins.then_inc(csb_psum, 1)
                pe.wait_ge(s_ret, l + 1)
                for h in range(BH):
                    s = slice(HD * (h % 2), HD * (h % 2) + HD)
                    ins = scores(ps[:, 4 + h, :], bqk[s, h // 2, :], bqk[s, 2 + h // 2, :])
                ins.then_inc(sb_z, 1)
                pe.wait_ge(seg_ready, 2 * (l + 1))
                for h in range(RH):
                    for b in range(NB):
                        ins = weighted(ps[:, 0, b * 256 + h * HD:b * 256 + h * HD + HD],
                                       scr[:, 2, h * SC:(h + 1) * SC], rv[:, :, h * HD:(h + 1) * HD], b)
                ins.then_inc(ret_y, 1)
                for g in range(SG):
                    pe.wait_ge(s_ssd, 2 * l + g + 1)
                    for hh in range(4):
                        h = 4 * g + hh
                        for b in range(NB):
                            ins = weighted(ps[:, 2 + b, h * HD:(h + 1) * HD], scr[:, g, hh * SC:(hh + 1) * SC],
                                           xdt[:, :, h * HD:(h + 1) * HD], b)
                ins.then_inc(ssd_y, 1)
                pe.wait_ge(sb_sp, l + 1)
                for h in range(BH):
                    z = ps[:, 4 + h, :]
                    sp0 = qkr[:, h * SC:h * SC + T]
                    sp1 = qkr[:, h * SC + T:(h + 1) * SC]
                    mm(z[:, 0:T], m_ge, sp0, start=False, stop=True, **opts)
                    mm(z[:, P:T], ones, sp1, start=False, stop=True, **opts)
                    ins = mm(z[:, T:SC], m_ge, sp1, start=False, stop=True, **opts)
                ins.then_inc(sb_log, 1)
                pe.wait_ge(sb_wm, l + 1)
                for h in range(BH):
                    for b in range(NB):
                        ins = weighted(ps[:, 1, b * 256 + h * HD:b * 256 + h * HD + HD],
                                       xbf[:, h * SC:(h + 1) * SC], bv[:, :, h * HD:(h + 1) * HD], b)
                ins.then_inc(sb_y, 1)
                for q in range(4):
                    if q == 0:
                        pe.wait_ge(mix_ret, l + 1)
                    if q == 1:
                        pe.wait_ge(mix_ssd, l + 1)
                    if q == 3:
                        pe.wait_ge(mix_sb, l + 1)
                    for j in range(4):
                        k, b = (4 * q + j) // 2, j % 2
                        ins = nc.tensor.transpose(ps[:, 4 + q, j * P:(j + 1) * P], hm[:, b, k * P:(k + 1) * P], ident)
                    ins.then_inc(mixT_psum, 1)
                pe.wait_ge(mixT_lo, 4 * l + 4)
                for n in range(2):
                    for half in range(2):
                        g = MIX_BASE[l] + 14 + 2 * n + half
                        pe.wait_ge(lo_ready[g % 6], g // 6 + 1)
                        hi, lo = win_view(w_hi, g % SPL, 512), win_view(w_lo, g % SPL, 512)
                        for b in range(NB):
                            for kk in range(4):
                                k = 4 * half + kk
                                ins = passes(ps[:, 2 * b + n, :], aT_hi[:, 2 * k + b, :], aT_lo[:, 2 * k + b, :],
                                             hi[:, kk, :], lo[:, kk, :], start=k == 0, stop=k == KD - 1)
                        ins.then_inc(split_used, 1)
                    pe.wait_ge(split_used, MIX_BASE[l] + 14 + 2 * n + 2)
                    pe.sem_inc(wout_psum, 1)

            def item(i, ph):
                it = i + ITEM_BASE[ph]
                g0 = i * ITEM_SUBS + FFN_BASE[ph]
                r0 = i * FC + FFN_BASE[ph] // 6

                def wait_sub(pos, c):
                    slot, r = at(pos)
                    pe.wait_ge(lo_ready[slot], r0 + (r + 1) if c is None else r0 + (r + 1) + (c - 1))
                    return slot % SPL

                def proj(bank, pos, c, half, done):
                    q = wait_sub(pos, c)
                    hi, lo = win_view(w_hi, q, 512), win_view(w_lo, q, 512)
                    for kk in range(4):
                        k = 4 * half + kk
                        ins = passes(ps[:, bank, :], aT_hi[:, k, :], aT_lo[:, k, :], hi[:, kk, :], lo[:, kk, :],
                                     start=k == 0, stop=k == KD - 1)
                    ins.then_inc(split_used, 1)
                    if half == 1:
                        pe.wait_ge(split_used, g0 + (pos + 1) if c is None else g0 + (pos + 1) + (c - 1) * 6)
                        pe.sem_inc(done, 1)

                def transpose_s(c):
                    pe.wait_ge(s_ready, it * FC + c + 1)
                    for j in range(4):
                        ins = nc.tensor.transpose(ps[:, 2, j * P:(j + 1) * P], s_act[:, j * P:(j + 1) * P], ident)
                    ins.then_inc(sT_psum, 1)

                def down(pos, c, cc):
                    pe.wait_ge(sT_lo, it * FC + cc + 1)
                    for half in range(2):
                        q = wait_sub(pos + half, c)
                        hi = w_hi[:, q, :].rearrange("p (k n) -> p k n", k=2)
                        lo = w_lo[:, q, :].rearrange("p (k n) -> p k n", k=2)
                        for kk in range(2):
                            j = 8 + 2 * half + kk
                            for n in range(2):
                                cols = slice(n * 512, (n + 1) * 512)
                                ins = passes(ps[:, 3 + n, :], aT_hi[:, j, :], aT_lo[:, j, :], hi[:, kk, cols],
                                             lo[:, kk, cols], start=False, stop=False)
                        ins.then_inc(split_used, 1)

                pe.wait_ge(sel_built, it + 1)
                for b in range(NB):
                    ins = nc.tensor.transpose(ps[:, 7, b * P:(b + 1) * P], selg[:, b, :], ident)
                for k in range(KD):
                    for b in range(NB):
                        ins = mm(ps[:, 5 + k // 4, (k % 4) * P:(k % 4 + 1) * P], hm[:, b, k * P:(k + 1) * P],
                                 sel[:, b, :], start=b == 0, stop=b == NB - 1, skip_group_check=True)
                    if k % 4 == 3:
                        ins.then_inc(gath_psum, 1)
                for n in range(2):
                    mm(ps[:, 3 + n, :], zeros[0:1, 0:P], zeros[0:1, 0:1].to_broadcast([1, 512]), start=True, stop=False,
                       skip_group_check=True)
                pe.wait_ge(gath_lo, it * 2 + 2)
                proj(0, 0, None, 0, gate_psum)
                proj(0, 1, None, 1, gate_psum)
                proj(1, 2, None, 0, up_psum)
                proj(1, 3, None, 1, up_psum)
                with pe.Fori(1, FC) as c:
                    pe.wait_ge(silu_done, it * FC + c)
                    proj(0, 4, c, 0, gate_psum)
                    proj(0, 5, c, 1, gate_psum)
                    transpose_s(c - 1)
                    proj(1, 6, c, 0, up_psum)
                    proj(1, 7, c, 1, up_psum)
                    down(8, c, c - 1)
                transpose_s(FC - 1)
                down(6 * FC - 2, None, FC - 1)
                pe.wait_ge(split_used, g0 + ITEM_SUBS)
                pe.sem_inc(y_psum, 1)
                pe.wait_ge(selgT_ready, it + 1)
                pe.wait_ge(y_ready, it + 1)
                for b in range(NB):
                    for n in range(2):
                        ins = mm(ps[:, (5 if b == 0 else 0) + n, :], selgT[:, b, :], y_sb[:, n * 512:(n + 1) * 512],
                                 start=True, stop=True, skip_group_check=True)
                    ins.then_inc(comb_psum, 1)

            pe.wait_ge(const_in, 16)
            pe.wait_ge(zeros_set, 1)
            mixer(0)
            pe.wait_ge(h_ready, 4)
            with pe.Fori(0, DENSE_ITEMS) as i:
                item(i, 0)
            mixer(1)
            pe.wait_ge(h_ready, 8)
            for q in range(4):
                for j in range(4):
                    k, b = (4 * q + j) // 2, j % 2
                    ins = nc.tensor.transpose(ps[:, q, j * P:(j + 1) * P], hm[:, b, k * P:(k + 1) * P], ident)
                ins.then_inc(h2T_psum, 1)
            pe.wait_ge(h2T_ready, 4)
            pe.wait_ge(rw_in, 16)
            for b in range(NB):
                for k in range(KD):
                    ins = mm(ps[:, 4, b * E:(b + 1) * E], h2T[:, 2 * k + b, :], rw[:, k, :], start=k == 0,
                             stop=k == KD - 1, skip_group_check=True)
            ins.then_inc(logits, 1)
            pe.wait_ge(sel_ready, 1)
            s3 = sm3(11)
            opts = dict(skip_group_check=True)
            mm(ps[:, 5, 0:8], m_lt, s3[:, 0], start=True, stop=True, **opts)
            mm(ps[:, 5, 8:16], ones, s3[:, 0], start=False, stop=False, **opts)
            mm(ps[:, 5, 8:16], m_lt, s3[:, 1], start=False, stop=True, **opts)
            mm(ps[:, 5, 16:24], ones, s3[:, 0], start=False, stop=False, **opts)
            mm(ps[:, 5, 16:24], ones, s3[:, 1], start=False, stop=True, **opts).then_inc(ranks, 1)
            pe.wait_ge(routed, 1)
            n = pe.value_load(n_items[0:1, 0:1], min_val=E, max_val=2 * E)
            with pe.Fori(0, n) as i:
                item(i, 1)


_INS = ['x', 'norm1_w', 'w_in', 'ret_norm_w', 'ssd_conv_w', 'ssd_conv_b', 'ssd_dt_bias', 'ssd_a_log', 'ssd_d',
        'ssd_norm_w', 'w_out', 'norm2_w', 'ffn_w_gate', 'ffn_w_up', 'ffn_w_down', 'moe_router', 'moe_w_gate',
        'moe_w_up', 'moe_w_down', 'final_norm_w']
_OUTS = [((1, T, D), 'float32')]


def kernel(**inputs):
    import concourse.bacc as _bacc
    from concourse.bass_utils import run_bass_kernel_spmd as _run

    nc = _bacc.Bacc("TRN2", target_bir_lowering=False, num_devices=1)
    arrays, args = {}, []
    for name in _INS:
        a = np.ascontiguousarray(inputs[name])
        arrays[f"in_{name}_dram"] = a
        args.append(nc.dram_tensor(f"in_{name}_dram", a.shape, mybir.dt.from_np(a.dtype), kind="ExternalInput").ap())
    c = tables()
    arrays["tables_dram"] = c
    args.append(nc.dram_tensor("tables_dram", c.shape, mybir.dt.from_np(c.dtype), kind="ExternalInput").ap())
    for i, (shape, dtype) in enumerate(_OUTS):
        dt = mybir.dt.from_np(np.dtype(dtype))
        args.append(nc.dram_tensor(f"out_{i}_dram", shape, dt, kind="ExternalOutput").ap())
    hybrid_kernel(nc, *args)
    r = _run(nc, [arrays], core_ids=[0])
    return r.results[0]["out_0_dram"]
```

```python
from contextlib import ExitStack

import concourse.bass as bass
import numpy as np
from concourse import mybir

F32 = mybir.dt.float32
F32R = mybir.dt.float32r
BF16 = mybir.dt.bfloat16
COMB = [5, 6, 7, 2]
MIXT = [2, 0, 5, 4]
I32 = mybir.dt.int32
ALU = mybir.AluOpType
ACT = mybir.ActivationFunctionType
AX = mybir.AxisListType

P = 128
T = 256
NB = T // P
D = 1024
KD = D // P
LAYERS = 2
HD = 64
RH, SH, BH = 4, 8, 4
SG = 2
TAPS = 4
XT = 6
F = 3584
FC = F // 512
E = 8
EPS = 1e-6
SC = 384
RAW, SPL = 6, 3
SUB = 2048
MIX_SUBS, ITEM_SUBS = 18, 6 * FC
DENSE_ITEMS = NB
FFN_BASE = [MIX_SUBS, 2 * MIX_SUBS + DENSE_ITEMS * ITEM_SUBS]
MIX_BASE = [0, MIX_SUBS + DENSE_ITEMS * ITEM_SUBS]
ITEM_BASE = [0, DENSE_ITEMS]
SEL_BASE = [0, DENSE_ITEMS + 1]

WIN = [("xbc", 1536, 512), ("bc_dt", 2048, 264), ("rqk", 0, 512), ("bqk", 2312, 512),
       ("sz", 1024, 512), ("rvg", 512, 512), ("bv", 2824, 256)]
TILES_T = {"xbc": 4, "bc_dt": 2, "rqk": 4, "bqk": 4}
PRM = TAPS * XT + XT + 2 + 4
PRM_B, PRM_N = TAPS * XT, TAPS * XT + XT

C_ID, C_IOTA, C_LE, C_LT, C_GE, C_ONE, C_ROT = (P * i for i in range(7))
C_COS, C_SIN = 7 * P, 7 * P + T
C_CAUSAL = C_SIN + T
C_STRICT = C_CAUSAL + SC
C_RET = C_STRICT + SC
C_E8 = C_RET + RH * SC
C_RG = C_E8 + E
NI = 18
C_ALL = C_RG + 2 * NB * NI


def tables():
    c = np.zeros((P, C_ALL), np.float64)
    a = np.arange(P)
    c[:, C_ID:C_ID + P] = np.eye(P)
    c[:, C_IOTA:C_IOTA + P] = a[None, :]
    c[:, C_LE:C_LE + P] = a[:, None] <= a[None, :]
    c[:, C_LT:C_LT + P] = a[:, None] < a[None, :]
    c[:, C_GE:C_GE + P] = a[:, None] >= a[None, :]
    c[:, C_ONE:C_ONE + P] = 1.0
    for m in range(P):
        if m % HD < HD // 2:
            c[m + HD // 2, C_ROT + m] = -1.0
        else:
            c[m - HD // 2, C_ROT + m] = 1.0
    half = HD // 2
    inv = (1.0 / (np.float32(10000.0) ** (np.arange(half, dtype=np.float32) / np.float32(half)))).astype(np.float32)
    ang = (np.arange(T, dtype=np.float32)[None, :] * inv[a % half][:, None]).astype(np.float32)
    c[:, C_COS:C_COS + T] = np.cos(ang.astype(np.float64))
    c[:, C_SIN:C_SIN + T] = np.sin(ang.astype(np.float64))
    j = np.concatenate([np.repeat(a[:, None], T, 1), np.repeat(a[:, None] + P, P, 1)], 1)
    i = np.concatenate([np.arange(T), np.arange(P, T)])[None, :]
    c[:, C_CAUSAL:C_CAUSAL + SC] = j <= i
    c[:, C_STRICT:C_STRICT + SC] = np.where(j < i, -1.0, 0.0)
    for h in range(RH):
        gamma = 1.0 - 2.0 ** (-5.0 - h)
        c[:, C_RET + h * SC:C_RET + (h + 1) * SC] = np.where(j <= i, gamma ** np.maximum(i - j, 0), 0.0) * HD ** -0.5
    c[:, C_E8:C_E8 + E] = np.arange(E) - 100.0
    rg = np.full((P, 2, NB, NI), -1.0)
    rg[:, 1] = 1.0
    for b in range(NB):
        rg[:, 0, b, b + 1] = a
    c[:, C_RG:] = rg.reshape(P, 2 * NB * NI)
    return c.astype(np.float32)


def hybrid_kernel(nc, x_d, norm1_d, w_in_d, ret_norm_d, conv_w_d, conv_b_d, dt_bias_d, a_log_d, d_skip_d,
                  ssd_norm_d, w_out_d, norm2_d, ffn_g_d, ffn_u_d, ffn_d_d, router_d, moe_g_d, moe_u_d, moe_d_d,
                  final_d, const_d, out_d):
    ctx = ExitStack()
    with ctx:
        def sb(name, shape, dt=F32):
            return ctx.enter_context(nc.sbuf_tensor(name, shape, dt))

        def sem(name):
            return ctx.enter_context(nc.semaphore(name))

        raw = sb("raw", [P, RAW, SUB])
        w_hi = sb("w_hi", [P, SPL, SUB], F32R)
        w_lo = sb("w_lo", [P, SPL, SUB], F32R)
        x = sb("x", [P, NB, D])
        hm = sb("hm", [P, NB, D])
        aT_hi = sb("aT_hi", [P, 2 * KD, P], F32R)
        aT_lo = sb("aT_lo", [P, 2 * KD, P], F32R)
        cst = sb("cst", [P, C_ALL])
        qkr = sb("qkr", [P, 4 * SC])
        xbc = sb("xbc", [P, XT, T + TAPS - 1])
        cv = sb("cv", [P, XT, T])
        bqk = sb("bqk", [P, 4, T])
        rv = sb("rv", [P, NB, RH * HD])
        rg = sb("rg", [P, NB, RH * HD])
        bv = sb("bv", [P, NB, BH * HD])
        sz = sb("sz", [P, NB, SH * HD])
        xtok = sb("xtok", [P, NB, SH * HD])
        xdt = sb("xdt", [P, NB, SH * HD])
        cb = sb("cb", [P, SG, SC])
        scr = sb("scr", [P, 3, 4 * SC])
        prm_rows = sb("prm_rows", [PRM, LAYERS, P])
        prm = sb("prm", [P, PRM])
        heads8 = sb("heads8", [P, LAYERS, 3, SH])
        small = sb("small", [P, 16, 16])
        rw = sb("rw", [P, KD, E])
        rank_gate = sb("rank_gate", [P, 2, NB, NI])
        cur = sb("cur", [P, 2, NB, 2])
        n_items = sb("n_items", [P, 2], I32)
        zeros = sb("zeros", [1, P], BF16)

        ident = cst[:, C_ID:C_ID + P]
        iota = cst[:, C_IOTA:C_IOTA + P]
        m_le, m_lt, m_ge = (cst[:, c:c + P] for c in (C_LE, C_LT, C_GE))
        ones = cst[:, C_ONE:C_ONE + P]
        rot = cst[:, C_ROT:C_ROT + P]
        normw = bqk[:].rearrange("p a b -> p (a b)")
        csT = scr[0:SH, 1, 1024:1024 + T]
        flat = scr[:].rearrange("p a b -> p (a b)")
        cvf = cv[:].rearrange("p a b -> p (a b)")
        xbf = xbc[:].rearrange("p a b -> p (a b)")[:, 0:4 * SC]
        silu_g, s_act = flat[:, 0:512], flat[:, 512:1024]
        y_sb = flat[:, 1536:2560]
        sel = flat[:, 3072:3328].rearrange("p (b s) -> p b s", b=NB)
        selg = flat[:, 3328:3584].rearrange("p (b s) -> p b s", b=NB)
        selgT = flat[:, 3584:3840].rearrange("p (b s) -> p b s", b=NB)
        h2T = flat[:, 0:2048].rearrange("p (k t) -> p k t", k=2 * KD)

        def sm(i, n=16):
            return small[:, i, 0:n]

        def sm3(i):
            return small[:, i, :].rearrange("p (b e) -> p b e", b=NB)

        ps = ctx.enter_context(nc.psum_tensor("ps", [P, 8, 512], F32))

        def banks(a, b):
            return ps[:, a:b, :].rearrange("p a n -> p (a n)")

        landed = [sem(f"landed{i}") for i in range(RAW)]
        hi_ready = sem("hi_ready")
        lo_ready = [sem(f"lo_ready{i}") for i in range(RAW)]
        split_used = sem("split_used")
        (x_in, const_in, tables_in, normw0_in, prm_in, normw_in, rw_in, zeros_set, pad_set) = map(
            sem, ("x_in", "const_in", "tables_in", "normw0_in", "prm_in", "normw_in", "rw_in", "zeros_set", "pad_set"))
        (sumsq, rms_ready, rstd_ready, h_ready) = map(sem, ("sumsq", "rms_ready", "rstd_ready", "h_ready"))
        (hT_psum, hT_hi, hT_lo, prm_psum, prm_ready) = map(
            sem, ("hT_psum", "hT_hi", "hT_lo", "prm_psum", "prm_ready"))
        (win_out, conv_tap, conv_silu) = map(sem, ("win_out", "conv_tap", "conv_silu"))
        (dt_biased, dt_ln, a_ready) = map(sem, ("dt_biased", "dt_ln", "a_ready"))
        (cs_psum, cs_ready, csT_ready, cb_psum, cb_ready) = map(
            sem, ("cs_psum", "cs_ready", "csT_ready", "cb_psum", "cb_ready"))
        (xT_psum, xtok_ready, xdt_ready, rot_psum, qk_ready) = map(
            sem, ("xT_psum", "xtok_ready", "xdt_ready", "rot_psum", "qk_ready"))
        (csb_psum, seg_ready, seg_exp, s_ssd) = map(sem, ("csb_psum", "seg_ready", "seg_exp", "s_ssd"))
        (ret_psum, s_ret, ssd_y, gated, gated_sq, ssd_rms) = map(
            sem, ("ret_psum", "s_ret", "ssd_y", "gated", "gated_sq", "ssd_rms"))
        (ret_y, ret_var, ret_std) = map(sem, ("ret_y", "ret_var", "ret_std"))
        (sb_z, sb_ln, sb_sp, sb_log, sb_min, sb_w, sb_wm, sb_y) = map(
            sem, ("sb_z", "sb_ln", "sb_sp", "sb_log", "sb_min", "sb_w", "sb_wm", "sb_y"))
        (mix_ret, mix_ssd, mix_sb, mixT_psum, mixT_hi, mixT_lo, mix_block0, x_mixed) = map(
            sem, ("mix_ret", "mix_ssd", "mix_sb", "mixT_psum", "mixT_hi", "mixT_lo", "mix_block0", "x_mixed"))
        (h2T_psum, h2T_ready, logits, gate_diff, gate_exp, sel_ready, ranks, routed) = map(
            sem, ("h2T_psum", "h2T_ready", "logits", "gate_diff", "gate_exp", "sel_ready", "ranks", "routed"))
        (cur_ready, sel_built, selgT_psum, selgT_ready, gath_psum, gath_hi, gath_lo) = map(
            sem, ("cur_ready", "sel_built", "selgT_psum", "selgT_ready", "gath_psum", "gath_hi", "gath_lo"))
        (silu_done, s_ready, sT_psum, sT_hi, sT_lo) = map(
            sem, ("silu_done", "s_ready", "sT_psum", "sT_hi", "sT_lo"))
        (y_zero, y_ready, comb_psum, x_added, stored, dve_step, act_step) = map(
            sem, ("y_zero", "y_ready", "comb_psum", "x_added", "stored", "dve_step", "act_step"))

        block = ctx.enter_context(nc.Block())

        def win_view(buf, slot, n):
            return buf[:, slot, 0:4 * n].rearrange("p (k n) -> p k n", k=4)

        def at(pos):
            return pos % 6, pos // 6

        @block.sync
        def _(sp):
            def load(slot, rnd, dst, src):
                if not isinstance(rnd, int) or rnd > 0:
                    sp.wait_ge(lo_ready[slot], rnd)
                sp.dma_start(dst, src).then_inc(landed[slot], 16)

            def mixer_weights(l):
                g = MIX_BASE[l]
                for name, c0, n in WIN:
                    src = w_in_d[l, :, c0:c0 + n].rearrange("(h k p) n -> h p k n", h=2, k=4)
                    for half in range(2):
                        load(g % 6, g // 6, win_view(raw, g % 6, n), src[half])
                        g += 1
                        if g == 3:
                            sp.dma_start(cst[:, C_COS:], const_d[:, C_COS:]).then_inc(tables_in, 16)
                for half in range(2):
                    for n in range(2):
                        src = w_out_d[l, :, n * 512:(n + 1) * 512].rearrange("(h k p) n -> h p k n", h=2, k=4)
                        load(g % 6, g // 6, win_view(raw, g % 6, 512), src[half])
                        g += 1

            def item_weights(base_round, wg, wu, wd):
                gsrc = wg.rearrange("(h k p) (c n) -> c h p k n", h=2, k=4, n=512)
                usrc = wu.rearrange("(h k p) (c n) -> c h p k n", h=2, k=4, n=512)
                dsrc = wd.rearrange("(c h k p) n -> c h p k n", h=2, k=2, p=P)

                def gate_up(c, pos, rnd0):
                    for half in range(4):
                        slot, r = at(pos + half)
                        src = (gsrc if half < 2 else usrc)[c, half % 2]
                        load(slot, rnd0 + r, win_view(raw, slot, 512), src)

                def down(c, pos, rnd0):
                    for half in range(2):
                        slot, r = at(pos + half)
                        load(slot, rnd0 + r, raw[:, slot, :].rearrange("p (k n) -> p k n", k=2), dsrc[c, half])

                gate_up(0, 0, base_round)
                with sp.Fori(1, FC) as c:
                    gate_up(c, 4, base_round + (c - 1))
                    down(c - 1, 8, base_round + (c - 1))
                down(FC - 1, 6 * FC - 2, base_round)

            sp.wait_ge(x_in, 16)
            mixer_weights(0)
            with sp.Fori(0, DENSE_ITEMS) as i:
                item_weights(FFN_BASE[0] // 6 + i * FC, ffn_g_d[0], ffn_u_d[0], ffn_d_d[0])
            mixer_weights(1)
            with sp.Fori(0, E) as i:
                item_weights(FFN_BASE[1] // 6 + i * FC, moe_g_d[0][i], moe_u_d[0][i], moe_d_d[0][i])
            sp.wait_ge(routed, 1)
            n = sp.value_load(n_items[0:1, 0:1], min_val=E, max_val=2 * E)
            with sp.If(n > E):
                with sp.Fori(0, E) as i:
                    item_weights(FFN_BASE[1] // 6 + E * FC + i * FC, moe_g_d[0][i], moe_u_d[0][i], moe_d_d[0][i])
            sp.wait_ge(h_ready, 2 * 5)
            sp.dma_start(out_d[0].rearrange("(b p) d -> p b d", p=P), hm[:]).then_inc(stored, 16)
            sp.wait_ge(stored, 16)

        @block.gpsimd
        def _(pool):
            pool.memset(zeros[:], 0.0).then_inc(zeros_set, 1)
            pool.memset(xbc[:, :, 0:TAPS - 1], 0.0).then_inc(pad_set, 1)
            for l in range(LAYERS):
                rows = prm_rows[:, l, :]
                pool.dma_start(rows[0:PRM_B], conv_w_d[l].rearrange("k (m c) -> (k m) c", c=P)).then_inc(prm_in, 16)
                pool.dma_start(rows[PRM_B:PRM_N], conv_b_d[l].rearrange("(m c) -> m c", c=P)).then_inc(prm_in, 16)
                pool.dma_start(rows[PRM_N:PRM_N + 2], ret_norm_d[l].rearrange("(m c) -> m c", c=P)).then_inc(prm_in, 16)
                pool.dma_start(rows[PRM_N + 2:PRM], ssd_norm_d[l].rearrange("(m c) -> m c", c=P)).then_inc(prm_in, 16)
                for i, src in enumerate((dt_bias_d, a_log_d, d_skip_d)):
                    pool.dma_start(heads8[:, l, i, :], src[l].partition_broadcast(P)).then_inc(prm_in, 16)
            pool.dma_start(rw[:], router_d[0].rearrange("(k p) e -> p k e", p=P)).then_inc(rw_in, 16)
            for l in range(LAYERS):
                pool.wait_ge(sb_z, l + 1)
                if l > 0:
                    pool.wait_ge(normw_in, 16 * 2 * l)
                pool.dma_start(normw, norm2_d[l].partition_broadcast(P)).then_inc(normw_in, 16)
                if l + 1 < LAYERS:
                    pool.wait_ge(mix_sb, l + 1)
                    pool.memset(xbc[:, :, 0:TAPS - 1], 0.0).then_inc(pad_set, 1)
                pool.wait_ge(h_ready, 2 * (2 * l + 2))
                pool.wait_ge(normw_in, 16 * (2 * l + 1))
                nxt = norm1_d[l + 1] if l + 1 < LAYERS else final_d
                pool.dma_start(normw, nxt.partition_broadcast(P)).then_inc(normw_in, 16)

        @block.scalar
        def _(act):
            steps = [0]

            def chain(ins):
                steps[0] += 1
                ins.then_inc(act_step, 1)
                act.wait_ge(act_step, steps[0])

            act.dma_start(x[:], x_d[0].rearrange("(b p) d -> p b d", p=P)).then_inc(x_in, 16)
            act.dma_start(normw, norm1_d[0].partition_broadcast(P)).then_inc(normw0_in, 16)
            act.dma_start(cst[:, 0:C_COS], const_d[:, 0:C_COS]).then_inc(const_in, 16)

            def norm(u, ready, counts):
                nc.scalar.activation(sm(1)[0:1, 4:5], zeros[0:1, 0:1], ACT.Sqrt)
                for b in range(NB):
                    act.wait_ge(ready, counts[b])
                    nc.scalar.activation(hm[:, b, :], x[:, b, :], ACT.Square, accum_out=sm(0)[:, b:b + 1])\
                        .then_inc(sumsq, 1)
                    act.wait_ge(sumsq, 2 * u + b + 1)
                    nc.scalar.activation(sm(1)[:, b:b + 1], sm(0)[:, b:b + 1], ACT.Sqrt, bias=EPS, scale=1.0 / D)\
                        .then_inc(rms_ready, 1)

            def split(g, slot, rnd, n=SUB):
                act.wait_ge(landed[slot], (rnd + 1) * 16)
                if not isinstance(g, int) or g >= SPL:
                    act.wait_ge(split_used, g - (SPL - 1))
                nc.scalar.activation(w_hi[:, slot % SPL, 0:n], raw[:, slot, 0:n], ACT.Copy).then_inc(hi_ready, 1)

            def win_split(l, ci, halves=(0, 1)):
                for half in halves:
                    g = MIX_BASE[l] + 2 * ci + half
                    split(g, g % 6, g // 6, 4 * WIN[ci][2])

            def wout_split(l, i):
                g = MIX_BASE[l] + 14 + i
                split(g, g % 6, g // 6)

            def mixer(l):
                def chunk_done(ci):
                    act.wait_ge(split_used, MIX_BASE[l] + 2 * ci + 2)

                for q in range(4):
                    act.wait_ge(hT_psum, 4 * l + q + 1)
                    nc.scalar.activation(aT_hi[:, 4 * q:4 * q + 4, :].rearrange("p a b -> p (a b)"),
                                         ps[:, 4 + q, :], ACT.Copy).then_inc(hT_hi, 1)
                    if l == 0 and q % 2 == 1:
                        win_split(l, 0, (q // 2,))
                win_split(l, 1)
                chunk_done(0)
                act.wait_ge(pad_set, l + 1)
                nc.scalar.activation(xbc[:, 0:4, TAPS - 1:], banks(0, 2).rearrange("p (m t) -> p m t", m=4),
                                     ACT.Copy).then_inc(win_out, 1)
                act.wait_ge(prm_psum, l + 1)
                nc.scalar.activation(prm[:], ps[:, 4, 0:PRM], ACT.Copy).then_inc(prm_ready, 1)
                win_split(l, 2)
                chunk_done(1)
                nc.scalar.activation(xbc[:, 4:6, TAPS - 1:], ps[:, 2, :].rearrange("p (m t) -> p m t", m=2), ACT.Copy)
                nc.scalar.activation(sm(2), ps[:, 3, 0:16], ACT.Copy).then_inc(win_out, 1)
                nc.scalar.activation(sm(3, 8), heads8[:, l, 1, :], ACT.Exp)
                act.wait_ge(dt_biased, l + 1)
                chain(nc.scalar.activation(sm(4), sm(2), ACT.Abs))
                chain(nc.scalar.activation(sm(4), sm(4), ACT.Exp, scale=-1.0))
                nc.scalar.activation(sm(5), sm(4), ACT.Ln, bias=1.0).then_inc(dt_ln, 1)
                win_split(l, 3)
                chunk_done(2)
                nc.scalar.activation(scr[:, 2, 0:1024], banks(0, 2), ACT.Copy).then_inc(win_out, 1)
                act.wait_ge(conv_tap, TAPS * (l + 1))
                nc.scalar.activation(cvf, cvf, ACT.Silu).then_inc(conv_silu, 1)
                act.wait_ge(cs_psum, l + 1)
                nc.scalar.activation(csT, ps[0:SH, 4, P:P + T], ACT.Copy).then_inc(csT_ready, 1)
                win_split(l, 4)
                chunk_done(3)
                act.wait_ge(h_ready, 2 * (2 * l + 1))
                nc.scalar.activation(bqk[:, 0:2, :].rearrange("p a b -> p (a b)"), ps[:, 2, :], ACT.Copy,
                                     scale=HD ** -0.5)
                nc.scalar.activation(bqk[:, 2:4, :].rearrange("p a b -> p (a b)"), ps[:, 3, :], ACT.Copy)\
                    .then_inc(win_out, 1)
                for b in range(NB):
                    act.wait_ge(xT_psum, 2 * l + b + 1)
                    nc.scalar.activation(xtok[:, b, :], ps[:, 5 + b, :], ACT.Copy).then_inc(xtok_ready, 1)
                win_split(l, 5)
                for g in range(SG):
                    act.wait_ge(seg_ready, 2 * l + g + 1)
                    nc.scalar.activation(scr[:, g, :], scr[:, g, :], ACT.Exp).then_inc(seg_exp, 1)
                win_split(l, 6, (0,))
                chunk_done(4)
                nc.scalar.activation(sz[:].rearrange("p a b -> p (a b)"), banks(0, 2), ACT.Silu).then_inc(win_out, 1)
                win_split(l, 6, (1,))
                act.wait_ge(sb_z, l + 1)
                chain(nc.scalar.activation(xbf.rearrange("p (h n) -> p h n", h=BH), ps[:, 4:8, 0:SC], ACT.Abs))
                chain(nc.scalar.activation(xbf, xbf, ACT.Exp, scale=-1.0))
                nc.scalar.activation(xbf, xbf, ACT.Ln, bias=1.0).then_inc(sb_ln, 1)
                chunk_done(5)
                pv = ps[:, 2:4, :]
                nc.scalar.activation(rv[:], pv[:, :, 0:256], ACT.Copy)
                nc.scalar.activation(rg[:], pv[:, :, 256:512], ACT.Silu).then_inc(win_out, 1)
                wout_split(l, 0)
                wout_split(l, 1)
                act.wait_ge(ret_var, l + 1)
                nc.scalar.activation(sm(9, 8), sm(9, 8), ACT.Sqrt, bias=EPS, scale=1.0 / HD).then_inc(ret_std, 1)
                chunk_done(6)
                nc.scalar.activation(bv[:].rearrange("p a b -> p (a b)"), ps[:, 0, :], ACT.Copy).then_inc(win_out, 1)
                act.wait_ge(gated, l + 1)
                for b in range(NB):
                    for g in range(SG):
                        nc.scalar.activation(xdt[:, b, g * 256:(g + 1) * 256], sz[:, b, g * 256:(g + 1) * 256],
                                             ACT.Square, accum_out=sm(10)[:, 2 * b + g:2 * b + g + 1])\
                            .then_inc(gated_sq, 1)
                act.wait_ge(gated_sq, 4 * (l + 1))
                nc.scalar.activation(sm(10, 4), sm(10, 4), ACT.Sqrt, bias=EPS, scale=1.0 / 256).then_inc(ssd_rms, 1)
                wout_split(l, 2)

                def mixT(q):
                    act.wait_ge(mixT_psum, 4 * l + q + 1)
                    for k in (2 * q, 2 * q + 1):
                        dst = aT_hi[:, 2 * k:2 * k + 2, :].rearrange("p a b -> p (a b)")
                        src = ps[:, MIXT[q], (k % 2) * 256:(k % 2) * 256 + 256]
                        if k < 6:
                            ins = nc.scalar.activation(dst, src, ACT.Copy, scale=prm[:, PRM_N + k:PRM_N + k + 1])
                        else:
                            ins = nc.scalar.activation(dst, src, ACT.Copy)
                    ins.then_inc(mixT_hi, 1)

                mixT(0)
                mixT(1)
                act.wait_ge(sb_min, l + 1)
                nc.scalar.activation(xbf, xbf, ACT.Exp).then_inc(sb_w, 1)
                act.wait_ge(sb_y, l + 1)
                nc.scalar.activation(hm[:, :, 768:1024], ps[:, 7, :].rearrange("p (b n) -> p b n", b=NB),
                                     ACT.Copy, scale=-1.0).then_inc(mix_sb, 1)
                mixT(2)
                wout_split(l, 3)
                mixT(3)
                for half in range(2):
                    wout_split(l, 4 + half)

            def gathered(i, ph):
                n = i + SEL_BASE[ph]
                for q in range(2):
                    act.wait_ge(gath_psum, n * 2 + q + 1)
                    nc.scalar.activation(aT_hi[:, 4 * q:4 * q + 4, :].rearrange("p a b -> p (a b)"),
                                         ps[:, 5 + q, :], ACT.Copy).then_inc(gath_hi, 1)
                act.wait_ge(selgT_psum, n + 1)
                nc.scalar.activation(selgT, ps[:, 7, 0:256].rearrange("p (b s) -> p b s", b=NB), ACT.Copy)\
                    .then_inc(selgT_ready, 1)

            def take_y():
                nc.scalar.activation(y_sb, banks(3, 5), ACT.Copy).then_inc(y_ready, 1)

            def item(i, ph, more=True):
                it = i + ITEM_BASE[ph]
                g0 = i * ITEM_SUBS + FFN_BASE[ph]
                r0 = i * FC + FFN_BASE[ph] // 6

                def sp_(pos, c=None):
                    slot, r = at(pos)
                    if c is None:
                        split(g0 + pos, slot, r0 + r)
                    else:
                        split(g0 + pos + (c - 1) * 6, slot, r0 + r + (c - 1))

                def silu():
                    nc.scalar.activation(silu_g, ps[:, 0, :], ACT.Silu).then_inc(silu_done, 1)

                def evac_sT(c):
                    act.wait_ge(sT_psum, it * FC + c + 1)
                    nc.scalar.activation(aT_hi[:, 8:12, :].rearrange("p a b -> p (a b)"), ps[:, 2, :], ACT.Copy)\
                        .then_inc(sT_hi, 1)

                act.wait_ge(split_used, g0)
                act.wait_ge(y_zero, i + SEL_BASE[ph] + 1)
                take_y()
                sp_(2)
                sp_(3)
                act.wait_ge(split_used, g0 + 2)
                silu()
                sp_(4)
                with act.Fori(1, FC) as c:
                    sp_(5, c)
                    sp_(6, c)
                    sp_(7, c)
                    evac_sT(c - 1)
                    act.wait_ge(s_ready, it * FC + c)
                    act.wait_ge(split_used, g0 + c * 6)
                    silu()
                    sp_(8, c)
                    sp_(9, c)
                    sp_(10, c)
                evac_sT(FC - 1)
                sp_(6 * FC - 1)
                if more:
                    sp_(6 * FC)
                gathered(i + 1, ph)
                if more:
                    sp_(6 * FC + 1)

            def ffn(ph, last=None):
                gathered(0, ph)
                if last is None:
                    n = DENSE_ITEMS
                    with act.Fori(0, n) as i:
                        item(i, ph)
                else:
                    n = last + 1
                    with act.Fori(0, last) as i:
                        item(i, ph)
                    item(last, ph, more=False)
                act.wait_ge(split_used, n * ITEM_SUBS + FFN_BASE[ph])
                take_y()

            act.wait_ge(zeros_set, 1)
            norm(0, x_in, (16, 16))
            mixer(0)
            norm(1, x_mixed, (1, 2))
            ffn(0)
            norm(2, x_added, [DENSE_ITEMS + 1] * NB)
            mixer(1)
            norm(3, x_mixed, (3, 4))
            for q in range(4):
                act.wait_ge(h2T_psum, q + 1)
                nc.scalar.activation(h2T[:, 4 * q:4 * q + 4, :].rearrange("p a b -> p (a b)"), ps[:, q, :], ACT.Copy)\
                    .then_inc(h2T_ready, 1)
            act.wait_ge(gate_diff, 1)
            nc.scalar.activation(sm(6, 2), sm(6, 2), ACT.Exp).then_inc(gate_exp, 1)
            act.wait_ge(routed, 1)
            last = act.value_load(n_items[0:1, 1:2], min_val=E - 1, max_val=2 * E - 1)
            ffn(1, last)
            norm(4, x_added, [last + (SEL_BASE[1] + 2)] * NB)

        @block.vector
        def _(dve):
            steps = [0]
            V = nc.vector

            def chain(ins):
                steps[0] += 1
                ins.then_inc(dve_step, 1)
                dve.wait_ge(dve_step, steps[0])

            def norm(u):
                if u == 0:
                    dve.wait_ge(normw0_in, 16)
                else:
                    dve.wait_ge(normw_in, 16 * u)
                for b in range(NB):
                    dve.wait_ge(rms_ready, 2 * u + b + 1)
                    V.reciprocal(sm(1)[:, 2 + b:3 + b], sm(1)[:, b:b + 1]).then_inc(rstd_ready, 1)
                    dve.wait_ge(rstd_ready, 2 * u + b + 1)
                    V.scalar_tensor_tensor(hm[:, b, :], x[:, b, :], sm(1)[:, 2 + b:3 + b], normw, ALU.mult, ALU.mult)\
                        .then_inc(h_ready, 1)

            def split(g, slot, n=SUB):
                dve.wait_ge(hi_ready, g + 1)
                V.tensor_tensor(w_lo[:, slot % SPL, 0:n], raw[:, slot, 0:n], w_hi[:, slot % SPL, 0:n].bitcast(F32),
                                ALU.subtract).then_inc(lo_ready[slot], 1)

            def win_split(l, ci, halves=(0, 1)):
                for half in halves:
                    g = MIX_BASE[l] + 2 * ci + half
                    split(g, g % 6, 4 * WIN[ci][2])

            def wout_split(l, i):
                g = MIX_BASE[l] + 14 + i
                split(g, g % 6)

            def lo_part(dst, src, hi):
                return V.tensor_tensor(dst.rearrange("p a b -> p (a b)"), src,
                                       hi.rearrange("p a b -> p (a b)").bitcast(F32), ALU.subtract)

            def bc(ap, shape):
                return ap.to_broadcast(shape)

            def mixer(l):
                for q in range(4):
                    dve.wait_ge(hT_hi, 4 * l + q + 1)
                    lo_part(aT_lo[:, 4 * q:4 * q + 4, :], ps[:, 4 + q, :], aT_hi[:, 4 * q:4 * q + 4, :])\
                        .then_inc(hT_lo, 1)
                    if l == 0 and q % 2 == 1:
                        win_split(l, 0, (q // 2,))
                win_split(l, 1)
                win_split(l, 2)
                dve.wait_ge(prm_in, 16 * 7 * LAYERS)
                dve.wait_ge(win_out, 7 * l + 2)
                V.tensor_tensor(sm3(2), sm3(2), bc(heads8[:, l, 0, :].unsqueeze(1), [P, NB, SH]), ALU.add)\
                    .then_inc(dt_biased, 1)
                dve.wait_ge(prm_ready, l + 1)
                for tap in range(TAPS - 1, -1, -1):
                    for m in range(XT):
                        w = prm[:, tap * XT + m:tap * XT + m + 1]
                        src = xbc[:, m, tap:tap + T]
                        if tap == TAPS - 1:
                            ins = V.tensor_scalar(cv[:, m, :], src, w, prm[:, PRM_B + m:PRM_B + m + 1],
                                                  ALU.mult, ALU.add)
                        else:
                            ins = V.scalar_tensor_tensor(cv[:, m, :], src, w, cv[:, m, :], ALU.mult, ALU.add)
                    ins.then_inc(conv_tap, 1)
                    dve.wait_ge(conv_tap, TAPS * l + TAPS - tap)
                    if tap == 2:
                        dve.wait_ge(dt_ln, l + 1)
                        chain(V.tensor_scalar(sm(6), sm(4), 1.0, None, ALU.add))
                        chain(V.scalar_tensor_tensor(sm(4), sm(6), -1.0, sm(4), ALU.add, ALU.subtract))
                        chain(V.reciprocal(sm(6), sm(6)))
                        chain(V.tensor_tensor(sm(4), sm(4), sm(6), ALU.mult))
                        chain(V.tensor_tensor(sm(5), sm(5), sm(4), ALU.subtract))
                        chain(V.scalar_tensor_tensor(sm(5), sm(2), 0.0, sm(5), ALU.max, ALU.add))
                        V.scalar_tensor_tensor(sm3(6), sm3(5), -1.0, bc(sm(3, 8).unsqueeze(1), [P, NB, SH]),
                                               ALU.mult, ALU.mult).then_inc(a_ready, 1)
                        win_split(l, 3)
                dve.wait_ge(win_out, 7 * l + 3)
                dve.wait_ge(tables_in, 16)
                if l == 0:
                    V.tensor_copy(rank_gate[:].rearrange("p a b i -> p (a b i)"), cst[:, C_RG:C_ALL])
                v4 = lambda a: a.rearrange("p (m t) -> p m t", m=4)
                V.tensor_tensor(v4(scr[:, 0, 0:1024]), v4(scr[:, 2, 0:1024]),
                                bc(cst[:, C_COS:C_COS + T].unsqueeze(1), [P, 4, T]), ALU.mult)
                dve.wait_ge(rot_psum, l + 1)
                chain(V.tensor_tensor(v4(scr[:, 1, 0:1024]), v4(banks(5, 7)),
                                      bc(cst[:, C_SIN:C_SIN + T].unsqueeze(1), [P, 4, T]), ALU.mult))
                V.tensor_tensor(qkr[:, 0:1024], scr[:, 0, 0:1024], scr[:, 1, 0:1024], ALU.add).then_inc(qk_ready, 1)
                dve.wait_ge(csT_ready, l + 1)
                V.tensor_copy(sm(7), ps[:, 4, 0:16]).then_inc(cs_ready, 1)
                win_split(l, 4)
                for g in range(SG):
                    dve.wait_ge(cb_psum, 2 * l + g + 1)
                    V.tensor_tensor(cb[:, g, :], ps[:, 4 if g == 0 else 7, 0:SC], cst[:, C_CAUSAL:C_CAUSAL + SC],
                                    ALU.mult).then_inc(cb_ready, 1)
                for b in range(NB):
                    dve.wait_ge(xtok_ready, 2 * l + b + 1)
                    V.tensor_tensor(xdt[:, b, :].rearrange("p (h d) -> p h d", h=SH),
                                    ps[:, 5 + b, :].rearrange("p (h d) -> p h d", h=SH),
                                    bc(sm(5)[:, 8 * b:8 * b + 8].unsqueeze(2), [P, SH, HD]), ALU.mult)\
                        .then_inc(xdt_ready, 1)
                win_split(l, 5, (0,))
                dve.wait_ge(qk_ready, l + 1)
                for g in range(SG):
                    dve.wait_ge(csb_psum, 2 * l + g + 1)
                    for hh in range(4):
                        h = 4 * g + hh
                        src = ps[:, 4 + 2 * g + hh // 2, (hh % 2) * T:(hh % 2) * T + T]
                        V.tensor_scalar(scr[:, g, hh * SC:hh * SC + T], src, sm(7)[:, h:h + 1], 0.0,
                                        ALU.subtract, ALU.min)
                        ins = V.tensor_scalar(scr[:, g, hh * SC + T:hh * SC + SC], src[:, P:T],
                                              sm(7)[:, 8 + h:9 + h], 0.0, ALU.subtract, ALU.min)
                    ins.then_inc(seg_ready, 1)
                win_split(l, 5, (1,))
                for b in range(NB):
                    xh = xtok[:, b, :].rearrange("p (h d) -> p h d", h=SH)
                    ins = V.tensor_tensor(xh, xh, bc(heads8[:, l, 2, :].unsqueeze(2), [P, SH, HD]), ALU.mult)
                chain(ins)
                win_split(l, 6, (0,))
                dve.wait_ge(ret_psum, l + 1)
                V.tensor_tensor(scr[:, 2, :].rearrange("p (h n) -> p h n", h=RH), ps[:, 4:8, 0:SC],
                                cst[:, C_RET:C_RET + RH * SC].rearrange("p (h n) -> p h n", h=RH), ALU.mult)\
                    .then_inc(s_ret, 1)
                for g in range(SG):
                    dve.wait_ge(seg_exp, 2 * l + g + 1)
                    s4 = scr[:, g, :].rearrange("p (h n) -> p h n", h=4)
                    V.tensor_tensor(s4, s4, bc(cb[:, g, :].unsqueeze(1), [P, 4, SC]), ALU.mult).then_inc(s_ssd, 1)
                win_split(l, 6, (1,))
                z4 = ps[:, 4:8, 0:SC]
                xb4 = xbf.rearrange("p (h n) -> p h n", h=BH)
                sp4 = qkr[:].rearrange("p (h n) -> p h n", h=BH)
                strict = bc(cst[:, C_STRICT:C_STRICT + SC].unsqueeze(1), [P, BH, SC])
                dve.wait_ge(sb_ln, l + 1)
                chain(V.scalar_tensor_tensor(sp4, z4, 0.0, xb4, ALU.max, ALU.add))
                V.tensor_tensor(sp4, sp4, strict, ALU.mult).then_inc(sb_sp, 1)
                wout_split(l, 0)
                r8 = lambda a: a.rearrange("p (h d) -> p h d", h=8)
                ry = ps[:, 2, :]
                dve.wait_ge(ret_y, l + 1)
                chain(V.tensor_reduce(sm(8, 8), r8(ry), AX.X, ALU.add))
                chain(V.tensor_scalar(sm(8, 8), sm(8, 8), 1.0 / HD, None, ALU.mult))
                chain(V.tensor_tensor(r8(cvf[:, 0:512]), r8(ry), bc(sm(8, 8).unsqueeze(2), [P, 8, HD]), ALU.subtract))
                chain(V.tensor_tensor(cvf[:, 512:1024], cvf[:, 0:512], cvf[:, 0:512], ALU.mult))
                V.tensor_reduce(sm(9, 8), r8(cvf[:, 512:1024]), AX.X, ALU.add).then_inc(ret_var, 1)
                wout_split(l, 1)
                dve.wait_ge(ssd_y, l + 1)
                szf = sz[:].rearrange("p a b -> p (a b)")
                for b in range(NB):
                    ins = V.tensor_tensor(xtok[:, b, :], ps[:, 1 + 2 * b, :], xtok[:, b, :], ALU.add)
                chain(ins)
                V.tensor_tensor(szf, szf, xtok[:].rearrange("p a b -> p (a b)"), ALU.mult).then_inc(gated, 1)
                dve.wait_ge(ret_std, l + 1)
                chain(V.reciprocal(sm(9, 8), sm(9, 8)))
                chain(V.tensor_tensor(r8(cvf[:, 0:512]), r8(cvf[:, 0:512]), bc(sm(9, 8).unsqueeze(2), [P, 8, HD]),
                                      ALU.mult))
                V.tensor_tensor(hm[:, :, 0:256], cvf[:, 0:512].rearrange("p (b n) -> p b n", b=NB), rg[:], ALU.mult)\
                    .then_inc(mix_ret, 1)
                dve.wait_ge(ssd_rms, l + 1)
                chain(V.reciprocal(sm(10, 4), sm(10, 4)))
                for b in range(NB):
                    ins = V.tensor_tensor(hm[:, b, 256:768].rearrange("p (g n) -> p g n", g=SG),
                                          sz[:, b, :].rearrange("p (g n) -> p g n", g=SG),
                                          bc(sm(10)[:, 2 * b:2 * b + 2].unsqueeze(2), [P, SG, 256]), ALU.mult)
                ins.then_inc(mix_ssd, 1)

                def mixT(q):
                    dve.wait_ge(mixT_hi, 4 * l + q + 1)
                    for k in (2 * q, 2 * q + 1):
                        dst = aT_lo[:, 2 * k:2 * k + 2, :].rearrange("p a b -> p (a b)")
                        hi = aT_hi[:, 2 * k:2 * k + 2, :].rearrange("p a b -> p (a b)").bitcast(F32)
                        src = ps[:, MIXT[q], (k % 2) * 256:(k % 2) * 256 + 256]
                        if k < 6:
                            ins = V.scalar_tensor_tensor(dst, src, prm[:, PRM_N + k:PRM_N + k + 1], hi,
                                                         ALU.mult, ALU.subtract)
                        else:
                            ins = V.tensor_tensor(dst, src, hi, ALU.subtract)
                    ins.then_inc(mixT_lo, 1)

                mixT(0)
                dve.wait_ge(sb_log, l + 1)
                V.tensor_scalar(xb4, z4, 0.0, None, ALU.min).then_inc(sb_min, 1)
                mixT(1)
                dve.wait_ge(sb_w, l + 1)
                V.tensor_tensor(xb4, xb4, strict, ALU.mult).then_inc(sb_wm, 1)
                wout_split(l, 2)
                mixT(2)
                wout_split(l, 3)
                mixT(3)
                wout_split(l, 4)

                def add_mixed(b, n):
                    xs = x[:, b, n * 512:(n + 1) * 512]
                    return V.tensor_tensor(xs, ps[:, 2 * b + n, :], xs, ALU.add)

                dve.wait_ge(split_used, MIX_BASE[l] + 17)
                add_mixed(0, 0)
                add_mixed(1, 0)
                wout_split(l, 5)
                dve.wait_ge(mix_block0, l + 1)
                add_mixed(0, 1).then_inc(x_mixed, 1)
                dve.wait_ge(split_used, MIX_BASE[l] + 18)
                add_mixed(1, 1).then_inc(x_mixed, 1)

            def route():
                lg, oh1, oh2, tmp, t2, gts = (sm3(i) for i in (11, 12, 13, 14, 15, 3))
                e8 = bc(cst[:, C_E8:C_E8 + E].unsqueeze(1), [P, NB, E])
                col = lambda i: bc(sm(i, 2).unsqueeze(2), [P, NB, E])
                dve.wait_ge(logits, 1)
                chain(V.tensor_copy(sm(11), ps[:, 4, 0:16]))
                chain(V.tensor_reduce(sm(8, 2), lg, AX.X, ALU.max))
                chain(V.tensor_tensor(tmp, lg, col(8), ALU.is_equal))
                chain(V.tensor_tensor(tmp, tmp, e8, ALU.mult))
                chain(V.tensor_reduce(sm(9, 2), tmp, AX.X, ALU.min))
                chain(V.tensor_tensor(oh1, e8, col(9), ALU.is_equal))
                chain(V.scalar_tensor_tensor(t2, oh1, -3e38, lg, ALU.mult, ALU.add))
                chain(V.tensor_reduce(sm(10, 2), t2, AX.X, ALU.max))
                V.tensor_tensor(sm(6, 2), sm(10, 2), sm(8, 2), ALU.subtract).then_inc(gate_diff, 1)
                chain(V.tensor_tensor(tmp, t2, col(10), ALU.is_equal))
                chain(V.tensor_tensor(tmp, tmp, e8, ALU.mult))
                chain(V.tensor_reduce(sm(9, 2), tmp, AX.X, ALU.min))
                chain(V.tensor_tensor(oh2, e8, col(9), ALU.is_equal))
                V.tensor_tensor(lg, oh1, oh2, ALU.add).then_inc(sel_ready, 1)
                dve.wait_ge(gate_exp, 1)
                chain(V.tensor_scalar(sm(7, 2), sm(6, 2), 1.0, None, ALU.add))
                chain(V.reciprocal(sm(7, 2), sm(7, 2)))
                chain(V.tensor_tensor(sm(6, 2), sm(6, 2), sm(7, 2), ALU.mult))
                chain(V.tensor_tensor(gts, oh1, col(7), ALU.mult))
                chain(V.tensor_tensor(tmp, oh2, col(6), ALU.mult))
                for half in range(2):
                    V.tensor_tensor(rank_gate[:, 1, :, 1 + E * half:1 + E * half + E], gts, tmp, ALU.add)
                dve.wait_ge(sel_ready, 1)
                dve.wait_ge(ranks, 1)
                chain(V.scalar_tensor_tensor(t2, ps[:, 5, 0:16].rearrange("p (b e) -> p b e", b=NB), 1.0, lg,
                                             ALU.add, ALU.mult))
                for half in range(2):
                    V.tensor_scalar(rank_gate[:, 0, :, 1 + E * half:1 + E * half + E], t2, -1.0 - P * half, None, ALU.add)
                chain(V.tensor_reduce(sm(8, 1), ps[:, 5, 16:16 + E], AX.X, ALU.max))
                chain(V.tensor_scalar(sm(8, 1), sm(8, 1), float(P), float(E), ALU.is_gt, ALU.mult))
                V.tensor_scalar(n_items[:, 0:1], sm(8, 1), float(E), None, ALU.add)
                V.tensor_scalar(n_items[:, 1:2], sm(8, 1), float(E - 1), None, ALU.add).then_inc(routed, 1)
                dve.wait_ge(routed, 1)

            def select(i, ph, dyn):
                n = i + SEL_BASE[ph]
                cols = rank_gate[:, :, :, bass.ds(i, 2)] if dyn else rank_gate[:, :, :, i:i + 2]
                V.tensor_copy(cur[:].rearrange("p a b i -> p (a b) i"), cols.rearrange("p a b i -> p (a b) i"))\
                    .then_inc(cur_ready, 1)
                dve.wait_ge(cur_ready, n + 1)
                for b in range(NB):
                    V.tensor_scalar(sel[:, b, :], iota, cur[:, 0, b, 1:2], None, ALU.is_equal)
                    ins = V.tensor_scalar(selg[:, b, :], iota, cur[:, 0, b, 0:1], cur[:, 1, b, 0:1],
                                          ALU.is_equal, ALU.mult)
                ins.then_inc(sel_built, 1)

            def gathered(i, ph):
                n = i + SEL_BASE[ph]
                for q in range(2):
                    dve.wait_ge(gath_hi, n * 2 + q + 1)
                    lo_part(aT_lo[:, 4 * q:4 * q + 4, :], ps[:, 5 + q, :], aT_hi[:, 4 * q:4 * q + 4, :])\
                        .then_inc(gath_lo, 1)

            def add_y(i, ph):
                n = i + SEL_BASE[ph]
                dve.wait_ge(comb_psum, n + 1)
                for b in range(NB):
                    for h in range(2):
                        xs = x[:, b, h * 512:(h + 1) * 512]
                        ins = V.tensor_tensor(xs, ps[:, COMB[2 * b + h], :], xs, ALU.add)
                ins.then_inc(x_added, 1)

            def item(i, ph, more=True):
                it = i + ITEM_BASE[ph]
                g0 = i * ITEM_SUBS + FFN_BASE[ph]

                def lo(pos, c=None):
                    split(g0 + pos if c is None else g0 + pos + (c - 1) * 6, pos % 6)

                def evac_sT(c):
                    dve.wait_ge(sT_hi, it * FC + c + 1)
                    lo_part(aT_lo[:, 8:12, :], ps[:, 2, :], aT_hi[:, 8:12, :]).then_inc(sT_lo, 1)

                def gate_times_up(c, done):
                    dve.wait_ge(silu_done, it * FC + c + 1)
                    dve.wait_ge(split_used, done)
                    V.tensor_tensor(s_act, ps[:, 1, :], silu_g, ALU.mult).then_inc(s_ready, 1)

                lo(2)
                lo(3)
                lo(4)
                add_y(i, ph)
                gate_times_up(0, g0 + 4)
                with dve.Fori(1, FC) as c:
                    lo(5, c)
                    lo(6, c)
                    lo(7, c)
                    evac_sT(c - 1)
                    lo(8, c)
                    lo(9, c)
                    lo(10, c)
                    gate_times_up(c, g0 + 2 + c * 6)
                dve.wait_ge(x_added, i + (SEL_BASE[ph] + 1))
                select(i + 1, ph, True)
                evac_sT(FC - 1)
                lo(6 * FC - 1)
                if more:
                    lo(6 * FC)
                gathered(i + 1, ph)
                if more:
                    lo(6 * FC + 1)

            def ffn(ph, last=None):
                select(0, ph, False)
                gathered(0, ph)
                if last is None:
                    n = DENSE_ITEMS
                    with dve.Fori(0, n) as i:
                        item(i, ph)
                else:
                    n = last + 1
                    with dve.Fori(0, last) as i:
                        item(i, ph)
                    item(last, ph, more=False)
                add_y(n, ph)
                dve.wait_ge(x_added, n + (SEL_BASE[ph] + 1))

            dve.wait_ge(x_in, 16)
            norm(0)
            mixer(0)
            norm(1)
            ffn(0)
            norm(2)
            mixer(1)
            norm(3)
            route()
            last = dve.value_load(n_items[0:1, 1:2], min_val=E - 1, max_val=2 * E - 1)
            ffn(1, last)
            norm(4)

        @block.tensor
        def _(pe):
            mm = nc.tensor.matmul

            def passes(out, lhs_hi, lhs_lo, rhs_hi, rhs_lo, start, stop):
                mm(out, lhs_hi, rhs_hi, start=start, stop=False, skip_group_check=True)
                mm(out, lhs_hi, rhs_lo, start=False, stop=False, skip_group_check=True)
                return mm(out, lhs_lo, rhs_hi, start=False, stop=stop, skip_group_check=True)

            def win_chunk(l, ci, halves=(0, 1)):
                name, _, n = WIN[ci]
                par = 2 * (ci % 2)
                if ci >= 2:
                    pe.wait_ge(win_out, 7 * l + ci - 1)
                tiles = TILES_T.get(name, 0)
                for half in halves:
                    g = MIX_BASE[l] + 2 * ci + half
                    pe.wait_ge(lo_ready[g % 6], g // 6 + 1)
                    hi, lo = win_view(w_hi, g % SPL, n), win_view(w_lo, g % SPL, n)
                    first = half == 0
                    for m in range(tiles):
                        out = banks(par, par + 2)[:, m * T:(m + 1) * T]
                        for kk in range(4):
                            k = 4 * half + kk
                            cols = slice(m * P, (m + 1) * P)
                            ins = passes(out, hi[:, kk, cols], lo[:, kk, cols],
                                         aT_hi[:, 2 * k:2 * k + 2, :].rearrange("p a b -> p (a b)"),
                                         aT_lo[:, 2 * k:2 * k + 2, :].rearrange("p a b -> p (a b)"),
                                         start=first and kk == 0 and m % 2 == 0, stop=k == KD - 1)
                    c0 = tiles * P
                    if c0 < n:
                        for b in range(NB):
                            if tiles:
                                out = ps[:, par + 1, 8 * b:8 * b + n - c0]
                            elif n <= 256:
                                out = ps[:, par, b * n:(b + 1) * n]
                            else:
                                out = ps[:, par + b, 0:n]
                            for kk in range(4):
                                k = 4 * half + kk
                                ins = passes(out, aT_hi[:, 2 * k + b, :], aT_lo[:, 2 * k + b, :],
                                             hi[:, kk, c0:n], lo[:, kk, c0:n],
                                             start=first and kk == 0 and not ((tiles or n <= 256) and b), stop=k == KD - 1)
                    ins.then_inc(split_used, 1)

            def scores(dst, q, k):
                mm(dst[:, 0:T], k[:, 0:P], q, start=True, stop=True, skip_group_check=True)
                return mm(dst[:, T:SC], k[:, P:T], q[:, P:T], start=False, stop=True, skip_group_check=True)

            def weighted(dst, s, v, b):
                if b == 0:
                    return mm(dst, s[:, 0:P], v[:, 0], start=True, stop=True, skip_group_check=True)
                mm(dst, s[:, P:T], v[:, 0], start=True, stop=False, skip_group_check=True)
                return mm(dst, s[:, T:SC], v[:, 1], start=False, stop=True, skip_group_check=True)

            def mixer(l):
                opts = dict(skip_group_check=True)
                pe.wait_ge(h_ready, 2 * (2 * l + 1))
                for q in range(4):
                    for j in range(4):
                        k, b = (4 * q + j) // 2, j % 2
                        ins = nc.tensor.transpose(ps[:, 4 + q, j * P:(j + 1) * P], hm[:, b, k * P:(k + 1) * P], ident)
                    ins.then_inc(hT_psum, 1)
                pe.wait_ge(hT_lo, 4 * l + 2)
                win_chunk(l, 0, (0,))
                pe.wait_ge(hT_lo, 4 * l + 4)
                win_chunk(l, 0, (1,))
                pe.wait_ge(prm_in, 16 * 7 * LAYERS)
                nc.tensor.transpose(ps[:, 4, 0:PRM], prm_rows[:, l, :], cst[0:PRM, C_ID:C_ID + PRM]).then_inc(prm_psum, 1)
                win_chunk(l, 1)
                win_chunk(l, 2)
                pe.wait_ge(prm_ready, l + 1)
                pe.wait_ge(a_ready, l + 1)
                a3 = sm3(6)
                c4 = ps[:, 4, :]
                mm(c4[:, 0:8], m_le, a3[:, 0], start=True, stop=True, **opts)
                mm(c4[:, 8:16], ones, a3[:, 0], start=False, stop=False, **opts)
                mm(c4[:, 8:16], m_le, a3[:, 1], start=False, stop=True, **opts)
                cT = ps[0:SH, 4, P:P + T]
                mm(cT[:, 0:P], a3[:, 0], m_le, start=False, stop=True, **opts)
                mm(cT[:, P:T], a3[:, 0], ones, start=False, stop=False, **opts)
                mm(cT[:, P:T], a3[:, 1], m_le, start=False, stop=True, **opts).then_inc(cs_psum, 1)
                pe.wait_ge(win_out, 7 * l + 3)
                for m in range(4):
                    ins = mm(banks(5, 7)[:, m * T:(m + 1) * T], rot, scr[:, 2, m * T:(m + 1) * T],
                             start=True, stop=True, **opts)
                ins.then_inc(rot_psum, 1)
                win_chunk(l, 3)
                pe.wait_ge(conv_silu, l + 1)
                pe.wait_ge(cs_ready, l + 1)
                for g in range(SG):
                    s = slice(HD * g, HD * g + HD)
                    scores(ps[:, 4 if g == 0 else 7, :], cv[s, 5, :], cv[s, 4, :]).then_inc(cb_psum, 1)
                pe.wait_ge(qk_ready, l + 1)
                for b in range(NB):
                    for m in range(4):
                        ins = nc.tensor.transpose(ps[:, 5 + b, m * P:(m + 1) * P],
                                                  cv[:, m, b * P:(b + 1) * P], ident)
                    ins.then_inc(xT_psum, 1)
                win_chunk(l, 4, (0,))
                pe.wait_ge(cb_ready, 2 * (l + 1))
                pe.wait_ge(xdt_ready, 2 * (l + 1))
                for g in range(SG):
                    for hh in range(4):
                        h = 4 * g + hh
                        ins = mm(ps[:, 4 + 2 * g + hh // 2, (hh % 2) * T:(hh % 2) * T + T],
                                 cst[0:SH, C_ID + h:C_ID + h + 1].to_broadcast([SH, P]), csT,
                                 start=True, stop=True, **opts)
                    ins.then_inc(csb_psum, 1)
                win_chunk(l, 4, (1,))
                pe.wait_ge(seg_ready, 2 * (l + 1))
                for h in range(RH):
                    s = slice(HD * (h % 2), HD * (h % 2) + HD)
                    q, k = h // 2 * T, (2 + h // 2) * T
                    ins = scores(ps[:, 4 + h, :], qkr[s, q:q + T], qkr[s, k:k + T])
                ins.then_inc(ret_psum, 1)
                win_chunk(l, 5, (0,))
                pe.wait_ge(s_ret, l + 1)
                for h in range(BH):
                    s = slice(HD * (h % 2), HD * (h % 2) + HD)
                    ins = scores(ps[:, 4 + h, :], bqk[s, h // 2, :], bqk[s, 2 + h // 2, :])
                ins.then_inc(sb_z, 1)
                win_chunk(l, 5, (1,))
                win_chunk(l, 6, (0,))
                pe.wait_ge(win_out, 7 * l + 6)
                for h in range(RH):
                    for b in range(NB):
                        ins = weighted(ps[:, 2, b * 256 + h * HD:b * 256 + h * HD + HD],
                                       scr[:, 2, h * SC:(h + 1) * SC], rv[:, :, h * HD:(h + 1) * HD], b)
                ins.then_inc(ret_y, 1)
                for g in range(SG):
                    pe.wait_ge(s_ssd, 2 * l + g + 1)
                    for hh in range(4):
                        h = 4 * g + hh
                        for b in range(NB):
                            ins = weighted(ps[:, 1 + 2 * b, h * HD:(h + 1) * HD], scr[:, g, hh * SC:(hh + 1) * SC],
                                           xdt[:, :, h * HD:(h + 1) * HD], b)
                ins.then_inc(ssd_y, 1)
                win_chunk(l, 6, (1,))

                def log_weights(h):
                    z = ps[:, 4 + h, :]
                    sp0 = qkr[:, h * SC:h * SC + T]
                    sp1 = qkr[:, h * SC + T:(h + 1) * SC]
                    mm(z[:, 0:T], m_ge, sp0, start=False, stop=True, **opts)
                    mm(z[:, P:T], ones, sp1, start=False, stop=True, **opts)
                    return mm(z[:, T:SC], m_ge, sp1, start=False, stop=True, **opts)

                def mixT(q):
                    for j in range(4):
                        k, b = (4 * q + j) // 2, j % 2
                        ins = nc.tensor.transpose(ps[:, MIXT[q], j * P:(j + 1) * P], hm[:, b, k * P:(k + 1) * P], ident)
                    ins.then_inc(mixT_psum, 1)

                def w_out(half, n):
                    g = MIX_BASE[l] + 14 + 2 * half + n
                    pe.wait_ge(lo_ready[g % 6], g // 6 + 1)
                    hi, lo = win_view(w_hi, g % SPL, 512), win_view(w_lo, g % SPL, 512)
                    for b in range(NB):
                        for kk in range(4):
                            k = 4 * half + kk
                            ins = passes(ps[:, 2 * b + n, :], aT_hi[:, 2 * k + b, :], aT_lo[:, 2 * k + b, :],
                                         hi[:, kk, :], lo[:, kk, :], start=k == 0, stop=k == KD - 1)
                        if (half, n, b) == (1, 1, 0):
                            ins.then_inc(mix_block0, 1)
                    ins.then_inc(split_used, 1)

                pe.wait_ge(sb_sp, l + 1)
                log_weights(0)
                log_weights(1)
                pe.wait_ge(mix_ret, l + 1)
                mixT(0)
                log_weights(2)
                log_weights(3).then_inc(sb_log, 1)
                pe.wait_ge(win_out, 7 * l + 7)
                pe.wait_ge(mix_ssd, l + 1)
                mixT(1)
                pe.wait_ge(mixT_lo, 4 * l + 2)
                w_out(0, 0)
                pe.wait_ge(sb_wm, l + 1)
                for h in range(BH):
                    for b in range(NB):
                        ins = weighted(ps[:, 7, b * 256 + h * HD:b * 256 + h * HD + HD],
                                       xbf[:, h * SC:(h + 1) * SC], bv[:, :, h * HD:(h + 1) * HD], b)
                ins.then_inc(sb_y, 1)
                mixT(2)
                w_out(0, 1)
                pe.wait_ge(mix_sb, l + 1)
                mixT(3)
                pe.wait_ge(mixT_lo, 4 * l + 4)
                w_out(1, 0)
                w_out(1, 1)

            def item(i, ph):
                it = i + ITEM_BASE[ph]
                g0 = i * ITEM_SUBS + FFN_BASE[ph]
                r0 = i * FC + FFN_BASE[ph] // 6

                def wait_sub(pos, c):
                    slot, r = at(pos)
                    pe.wait_ge(lo_ready[slot], r0 + (r + 1) if c is None else r0 + (r + 1) + (c - 1))
                    return slot % SPL

                def proj(bank, pos, c, half):
                    q = wait_sub(pos, c)
                    hi, lo = win_view(w_hi, q, 512), win_view(w_lo, q, 512)
                    for kk in range(4):
                        k = 4 * half + kk
                        ins = passes(ps[:, bank, :], aT_hi[:, k, :], aT_lo[:, k, :], hi[:, kk, :], lo[:, kk, :],
                                     start=k == 0, stop=k == KD - 1)
                    ins.then_inc(split_used, 1)

                def transpose_s(c):
                    pe.wait_ge(s_ready, it * FC + c + 1)
                    for j in range(4):
                        ins = nc.tensor.transpose(ps[:, 2, j * P:(j + 1) * P], s_act[:, j * P:(j + 1) * P], ident)
                    ins.then_inc(sT_psum, 1)

                def down(pos, c, cc):
                    pe.wait_ge(sT_lo, it * FC + cc + 1)
                    for half in range(2):
                        q = wait_sub(pos + half, c)
                        hi = w_hi[:, q, :].rearrange("p (k n) -> p k n", k=2)
                        lo = w_lo[:, q, :].rearrange("p (k n) -> p k n", k=2)
                        for kk in range(2):
                            j = 8 + 2 * half + kk
                            for n in range(2):
                                cols = slice(n * 512, (n + 1) * 512)
                                ins = passes(ps[:, 3 + n, :], aT_hi[:, j, :], aT_lo[:, j, :], hi[:, kk, cols],
                                             lo[:, kk, cols], start=False, stop=False)
                        ins.then_inc(split_used, 1)

                proj(0, 0, None, 0)
                proj(0, 1, None, 1)
                scatter(i, ph)
                zero_y()
                proj(1, 2, None, 0)
                proj(1, 3, None, 1)
                with pe.Fori(1, FC) as c:
                    pe.wait_ge(silu_done, it * FC + c)
                    proj(0, 4, c, 0)
                    proj(0, 5, c, 1)
                    transpose_s(c - 1)
                    proj(1, 6, c, 0)
                    proj(1, 7, c, 1)
                    down(8, c, c - 1)
                transpose_s(FC - 1)
                gather(i + 1, ph)
                down(6 * FC - 2, None, FC - 1)
                pe.wait_ge(gath_lo, (i + (SEL_BASE[ph] + 1)) * 2 + 2)

            def gather(i, ph):
                pe.wait_ge(sel_built, i + (SEL_BASE[ph] + 1))
                for k in range(KD):
                    for b in range(NB):
                        ins = mm(ps[:, 5 + k // 4, (k % 4) * P:(k % 4 + 1) * P], hm[:, b, k * P:(k + 1) * P],
                                 sel[:, b, :], start=b == 0, stop=b == NB - 1, skip_group_check=True)
                    if k % 4 == 3:
                        ins.then_inc(gath_psum, 1)
                for b in range(NB):
                    ins = nc.tensor.transpose(ps[:, 7, b * P:(b + 1) * P], selg[:, b, :], ident)
                ins.then_inc(selgT_psum, 1)

            def scatter(i, ph):
                n = i + (SEL_BASE[ph] + 1)
                pe.wait_ge(selgT_ready, n)
                pe.wait_ge(y_ready, n)
                for b in range(NB):
                    for h in range(2):
                        ins = mm(ps[:, COMB[2 * b + h], :], selgT[:, b, :], y_sb[:, h * 512:(h + 1) * 512],
                                 start=True, stop=True, skip_group_check=True)
                ins.then_inc(comb_psum, 1)

            def zero_y():
                for n in range(2):
                    ins = mm(ps[:, 3 + n, :], zeros[0:1, 0:P], zeros[0:1, 0:1].to_broadcast([1, 512]), start=True,
                             stop=False, skip_group_check=True)
                ins.then_inc(y_zero, 1)

            def ffn(n, ph):
                gather(0, ph)
                zero_y()
                pe.wait_ge(gath_lo, 2 * SEL_BASE[ph] + 2)
                with pe.Fori(0, n) as i:
                    item(i, ph)
                scatter(n, ph)

            pe.wait_ge(const_in, 16)
            pe.wait_ge(zeros_set, 1)
            mixer(0)
            pe.wait_ge(h_ready, 4)
            ffn(DENSE_ITEMS, 0)
            mixer(1)
            pe.wait_ge(h_ready, 8)
            for q in range(4):
                for j in range(4):
                    k, b = (4 * q + j) // 2, j % 2
                    ins = nc.tensor.transpose(ps[:, q, j * P:(j + 1) * P], hm[:, b, k * P:(k + 1) * P], ident)
                ins.then_inc(h2T_psum, 1)
            pe.wait_ge(h2T_ready, 4)
            pe.wait_ge(rw_in, 16)
            for b in range(NB):
                for k in range(KD):
                    ins = mm(ps[:, 4, b * E:(b + 1) * E], h2T[:, 2 * k + b, :], rw[:, k, :], start=k == 0,
                             stop=k == KD - 1, skip_group_check=True)
            ins.then_inc(logits, 1)
            pe.wait_ge(sel_ready, 1)
            s3 = sm3(11)
            opts = dict(skip_group_check=True)
            mm(ps[:, 5, 0:8], m_lt, s3[:, 0], start=True, stop=True, **opts)
            mm(ps[:, 5, 8:16], ones, s3[:, 0], start=False, stop=False, **opts)
            mm(ps[:, 5, 8:16], m_lt, s3[:, 1], start=False, stop=True, **opts)
            mm(ps[:, 5, 16:24], ones, s3[:, 0], start=False, stop=False, **opts)
            mm(ps[:, 5, 16:24], ones, s3[:, 1], start=False, stop=True, **opts).then_inc(ranks, 1)
            pe.wait_ge(routed, 1)
            n = pe.value_load(n_items[0:1, 0:1], min_val=E, max_val=2 * E)
            ffn(n, 1)


_INS = ['x', 'norm1_w', 'w_in', 'ret_norm_w', 'ssd_conv_w', 'ssd_conv_b', 'ssd_dt_bias', 'ssd_a_log', 'ssd_d',
        'ssd_norm_w', 'w_out', 'norm2_w', 'ffn_w_gate', 'ffn_w_up', 'ffn_w_down', 'moe_router', 'moe_w_gate',
        'moe_w_up', 'moe_w_down', 'final_norm_w']
_OUTS = [((1, T, D), 'float32')]


def kernel(**inputs):
    import concourse.bacc as _bacc
    from concourse.bass_utils import run_bass_kernel_spmd as _run

    nc = _bacc.Bacc("TRN2", target_bir_lowering=False, num_devices=1)
    arrays, args = {}, []
    for name in _INS:
        a = np.ascontiguousarray(inputs[name])
        arrays[f"in_{name}_dram"] = a
        args.append(nc.dram_tensor(f"in_{name}_dram", a.shape, mybir.dt.from_np(a.dtype), kind="ExternalInput").ap())
    c = tables()
    arrays["tables_dram"] = c
    args.append(nc.dram_tensor("tables_dram", c.shape, mybir.dt.from_np(c.dtype), kind="ExternalInput").ap())
    for i, (shape, dtype) in enumerate(_OUTS):
        dt = mybir.dt.from_np(np.dtype(dtype))
        args.append(nc.dram_tensor(f"out_{i}_dram", shape, dt, kind="ExternalOutput").ap())
    hybrid_kernel(nc, *args)
    r = _run(nc, [arrays], core_ids=[0])
    return r.results[0]["out_0_dram"]
```

```python
from contextlib import ExitStack

import concourse.bass as bass
import numpy as np
from concourse import mybir

F32 = mybir.dt.float32
F32R = mybir.dt.float32r
BF16 = mybir.dt.bfloat16
COMB = [5, 6, 7, 2]
MIXT = [1, 0, 5, 4]
I32 = mybir.dt.int32
ALU = mybir.AluOpType
ACT = mybir.ActivationFunctionType
AX = mybir.AxisListType

P = 128
T = 256
NB = T // P
D = 1024
KD = D // P
LAYERS = 2
HD = 64
RH, SH, BH = 4, 8, 4
SG = 2
TAPS = 4
XT = 6
F = 3584
FC = F // 512
E = 8
EPS = 1e-6
SC = 384
RAW, SPL = 6, 3
SUB = 2048
MIX_SUBS, ITEM_SUBS = 18, 6 * FC
MIX_BASE = [0, MIX_SUBS + ITEM_SUBS]
DENSE_BASE, MOE_BASE = MIX_SUBS, 2 * MIX_SUBS + ITEM_SUBS

WIN = [("xbc", 1536, 512), ("bc_dt", 2048, 264), ("rqk", 0, 512), ("bqk", 2312, 512),
       ("sz", 1024, 512), ("rvg", 512, 512), ("bv", 2824, 256)]
TILES_T = {"xbc": 4, "bc_dt": 2, "rqk": 4, "bqk": 4}
PRM = TAPS * XT + XT + 2 + 4
PRM_B, PRM_N = TAPS * XT, TAPS * XT + XT

C_ID, C_IOTA, C_LE, C_GE, C_ONE, C_ROT = (P * i for i in range(6))
C_COS, C_SIN = 6 * P, 6 * P + T
C_CAUSAL = C_SIN + T
C_STRICT = C_CAUSAL + SC
C_RET = C_STRICT + SC
C_E8 = C_RET + RH * SC
C_ALL = C_E8 + E
NI = 18


def tables():
    c = np.zeros((P, C_ALL), np.float64)
    a = np.arange(P)
    c[:, C_ID:C_ID + P] = np.eye(P)
    c[:, C_IOTA:C_IOTA + P] = a[None, :]
    c[:, C_LE:C_LE + P] = a[:, None] <= a[None, :]
    c[:, C_GE:C_GE + P] = a[:, None] >= a[None, :]
    c[:, C_ONE:C_ONE + P] = 1.0
    for m in range(P):
        if m % HD < HD // 2:
            c[m + HD // 2, C_ROT + m] = -1.0
        else:
            c[m - HD // 2, C_ROT + m] = 1.0
    half = HD // 2
    inv = (1.0 / (np.float32(10000.0) ** (np.arange(half, dtype=np.float32) / np.float32(half)))).astype(np.float32)
    ang = (np.arange(T, dtype=np.float32)[None, :] * inv[a % half][:, None]).astype(np.float32)
    c[:, C_COS:C_COS + T] = np.cos(ang.astype(np.float64))
    c[:, C_SIN:C_SIN + T] = np.sin(ang.astype(np.float64))
    j = np.concatenate([np.repeat(a[:, None], T, 1), np.repeat(a[:, None] + P, P, 1)], 1)
    i = np.concatenate([np.arange(T), np.arange(P, T)])[None, :]
    c[:, C_CAUSAL:C_CAUSAL + SC] = j <= i
    c[:, C_STRICT:C_STRICT + SC] = np.where(j < i, -1.0, 0.0)
    for h in range(RH):
        gamma = 1.0 - 2.0 ** (-5.0 - h)
        c[:, C_RET + h * SC:C_RET + (h + 1) * SC] = np.where(j <= i, gamma ** np.maximum(i - j, 0), 0.0) * HD ** -0.5
    c[:, C_E8:C_E8 + E] = np.arange(E) - 100.0
    return c.astype(np.float32)


def hybrid_kernel(nc, x_d, norm1_d, w_in_d, ret_norm_d, conv_w_d, conv_b_d, dt_bias_d, a_log_d, d_skip_d,
                  ssd_norm_d, w_out_d, norm2_d, ffn_g_d, ffn_u_d, ffn_d_d, router_d, moe_g_d, moe_u_d, moe_d_d,
                  final_d, const_d, out_d):
    ctx = ExitStack()
    with ctx:
        def sb(name, shape, dt=F32):
            return ctx.enter_context(nc.sbuf_tensor(name, shape, dt))

        def sem(name):
            return ctx.enter_context(nc.semaphore(name))

        raw = sb("raw", [P, RAW, SUB])
        w_hi = sb("w_hi", [P, SPL, SUB], F32R)
        w_lo = sb("w_lo", [P, SPL, SUB], F32R)
        x = sb("x", [P, NB, D])
        hm = sb("hm", [P, NB, D])
        aT_hi = sb("aT_hi", [P, 2 * KD, P], F32R)
        aT_lo = sb("aT_lo", [P, 2 * KD, P], F32R)
        s2T_hi = sb("s2T_hi", [P, NB * 4, P], F32R)
        s2T_lo = sb("s2T_lo", [P, NB * 4, P], F32R)
        cst = sb("cst", [P, C_ALL])
        qkr = sb("qkr", [P, 4 * SC])
        xbc = sb("xbc", [P, XT, T + TAPS - 1])
        cv = sb("cv", [P, XT, T])
        bqk = sb("bqk", [P, 4, T])
        rv = sb("rv", [P, NB, RH * HD])
        rg = sb("rg", [P, NB, RH * HD])
        bv = sb("bv", [P, NB, BH * HD])
        sz = sb("sz", [P, NB, SH * HD])
        xtok = sb("xtok", [P, NB, SH * HD])
        scr = sb("scr", [P, 3, 4 * SC])
        prm_rows = sb("prm_rows", [PRM, LAYERS, P])
        prm = sb("prm", [P, PRM])
        heads8 = sb("heads8", [P, LAYERS, 3, SH])
        small = sb("small", [P, 16, 16])
        rw = sb("rw", [P, KD, E])
        rank_gate = sb("rank_gate", [P, 2, NB, NI])
        cur = sb("cur", [P, 2, NB, 2])
        n_items = sb("n_items", [P, 2], I32)
        zeros = sb("zeros", [P, P], BF16)

        ident = cst[:, C_ID:C_ID + P]
        iota = cst[:, C_IOTA:C_IOTA + P]
        m_le, m_ge = (cst[:, c:c + P] for c in (C_LE, C_GE))
        ones = cst[:, C_ONE:C_ONE + P]
        rot = cst[:, C_ROT:C_ROT + P]
        xdt = hm[:, 1, :].rearrange("p (b n) -> p b n", b=NB)
        cb = hm[:, 0, 0:SG * SC].rearrange("p (g n) -> p g n", g=SG)
        normw = bqk[:].rearrange("p a b -> p (a b)")
        csT = scr[0:SH, 1, 1024:1024 + T]
        flat = scr[:].rearrange("p a b -> p (a b)")
        cvf = cv[:].rearrange("p a b -> p (a b)")
        xbf = xbc[:].rearrange("p a b -> p (a b)")[:, 0:4 * SC]
        silu_g, s_act = flat[:, 0:512], flat[:, 512:1024]
        y_sb = flat[:, 1536:2560]
        silu_g2, s_act2 = flat[:, 0:1024], flat[:, 1024:2048]
        sel = flat[:, 3072:3328].rearrange("p (b s) -> p b s", b=NB)
        selg = flat[:, 3328:3584].rearrange("p (b s) -> p b s", b=NB)
        selgT = flat[:, 3584:3840].rearrange("p (b s) -> p b s", b=NB)
        h2T = flat[:, 0:2048].rearrange("p (k t) -> p k t", k=2 * KD)

        def sm(i, n=16):
            return small[:, i, 0:n]

        def sm3(i):
            return small[:, i, :].rearrange("p (b e) -> p b e", b=NB)

        ps = ctx.enter_context(nc.psum_tensor("ps", [P, 8, 512], F32))

        def banks(a, b):
            return ps[:, a:b, :].rearrange("p a n -> p (a n)")

        landed = [sem(f"landed{i}") for i in range(RAW)]
        hi_ready = sem("hi_ready")
        lo_ready = [sem(f"lo_ready{i}") for i in range(RAW)]
        split_used = sem("split_used")
        x_in = [sem(f"x_in{b}") for b in range(NB)]
        (const_in, tables_in, normw0_in, prm_in, normw_in, rw_in, zeros_set, pad_set) = map(
            sem, ("const_in", "tables_in", "normw0_in", "prm_in", "normw_in", "rw_in", "zeros_set", "pad_set"))
        (sumsq, rms_ready, rstd_ready, h_ready) = map(sem, ("sumsq", "rms_ready", "rstd_ready", "h_ready"))
        (hT_psum, hT_hi, hT_lo, prm_psum, prm_ready) = map(
            sem, ("hT_psum", "hT_hi", "hT_lo", "prm_psum", "prm_ready"))
        (win_out, conv_tap, conv_silu) = map(sem, ("win_out", "conv_tap", "conv_silu"))
        (dt_biased, dt_ln, a_ready) = map(sem, ("dt_biased", "dt_ln", "a_ready"))
        (cs_psum, cs_ready, csT_ready, cb_psum, cb_ready) = map(
            sem, ("cs_psum", "cs_ready", "csT_ready", "cb_psum", "cb_ready"))
        (xT_psum, xtok_ready, xdt_ready, rot_psum, qk_ready) = map(
            sem, ("xT_psum", "xtok_ready", "xdt_ready", "rot_psum", "qk_ready"))
        (csb_psum, seg_ready, seg_exp, s_ssd) = map(sem, ("csb_psum", "seg_ready", "seg_exp", "s_ssd"))
        (rv_ready, ret_psum, s_ret, ssd_y, gated, gated_sq, ssd_rms) = map(
            sem, ("rv_ready", "ret_psum", "s_ret", "ssd_y", "gated", "gated_sq", "ssd_rms"))
        (ret_y, ret_var, ret_std) = map(sem, ("ret_y", "ret_var", "ret_std"))
        (sb_z, sb_ln, sb_sp, sb_log, sb_min, sb_w, sb_wm, sb_y) = map(
            sem, ("sb_z", "sb_ln", "sb_sp", "sb_log", "sb_min", "sb_w", "sb_wm", "sb_y"))
        (mix_ret, mix_ssd, mix_sb, mixT_psum, mixT_hi, mixT_lo, mix_block0, x_mixed) = map(
            sem, ("mix_ret", "mix_ssd", "mix_sb", "mixT_psum", "mixT_hi", "mixT_lo", "mix_block0", "x_mixed"))
        (h2T_psum, h2T_ready, logits, gate_diff, gate_exp, sel_ready, ranks, routed) = map(
            sem, ("h2T_psum", "h2T_ready", "logits", "gate_diff", "gate_exp", "sel_ready", "ranks", "routed"))
        (cur_ready, sel_built, selgT_psum, selgT_ready, gath_psum, gath_hi, gath_lo) = map(
            sem, ("cur_ready", "sel_built", "selgT_psum", "selgT_ready", "gath_psum", "gath_hi", "gath_lo"))
        (silu_done, s_ready, sT_psum, sT_hi, sT_lo) = map(
            sem, ("silu_done", "s_ready", "sT_psum", "sT_hi", "sT_lo"))
        (y_zero, y_ready, comb_psum, x_added, dense_block0, x_dense, stored, dve_step, act_step) = map(
            sem, ("y_zero", "y_ready", "comb_psum", "x_added", "dense_block0", "x_dense", "stored", "dve_step", "act_step"))

        block = ctx.enter_context(nc.Block())

        def win_view(buf, slot, n):
            return buf[:, slot, 0:4 * n].rearrange("p (k n) -> p k n", k=4)

        def at(pos):
            return pos % 6, pos // 6

        @block.sync
        def _(sp):
            def load(slot, rnd, dst, src):
                if not isinstance(rnd, int) or rnd > 0:
                    sp.wait_ge(lo_ready[slot], rnd)
                sp.dma_start(dst, src).then_inc(landed[slot], 16)

            def mixer_weights(l):
                g = MIX_BASE[l]
                for name, c0, n in WIN:
                    src = w_in_d[l, :, c0:c0 + n].rearrange("(h k p) n -> h p k n", h=2, k=4)
                    for half in range(2):
                        load(g % 6, g // 6, win_view(raw, g % 6, n), src[half])
                        g += 1
                        if g == 3:
                            sp.dma_start(cst[:, C_COS:], const_d[:, C_COS:]).then_inc(tables_in, 16)
                for half in range(2):
                    for n in range(2):
                        src = w_out_d[l, :, n * 512:(n + 1) * 512].rearrange("(h k p) n -> h p k n", h=2, k=4)
                        load(g % 6, g // 6, win_view(raw, g % 6, 512), src[half])
                        g += 1

            def item_weights(base_round, wg, wu, wd):
                gsrc = wg.rearrange("(h k p) (c n) -> c h p k n", h=2, k=4, n=512)
                usrc = wu.rearrange("(h k p) (c n) -> c h p k n", h=2, k=4, n=512)
                dsrc = wd.rearrange("(c h k p) n -> c h p k n", h=2, k=2, p=P)

                def gate_up(c, pos, rnd0):
                    for half in range(4):
                        slot, r = at(pos + half)
                        src = (gsrc if half < 2 else usrc)[c, half % 2]
                        load(slot, rnd0 + r, win_view(raw, slot, 512), src)

                def down(c, pos, rnd0):
                    for half in range(2):
                        slot, r = at(pos + half)
                        load(slot, rnd0 + r, raw[:, slot, :].rearrange("p (k n) -> p k n", k=2), dsrc[c, half])

                gate_up(0, 0, base_round)
                with sp.Fori(1, FC) as c:
                    gate_up(c, 4, base_round + (c - 1))
                    down(c - 1, 8, base_round + (c - 1))
                down(FC - 1, 6 * FC - 2, base_round)

            sp.wait_ge(x_in[NB - 1], 16)
            mixer_weights(0)
            item_weights(DENSE_BASE // 6, ffn_g_d[0], ffn_u_d[0], ffn_d_d[0])
            mixer_weights(1)
            with sp.Fori(0, E) as i:
                item_weights(MOE_BASE // 6 + i * FC, moe_g_d[0][i], moe_u_d[0][i], moe_d_d[0][i])
            sp.wait_ge(routed, 1)
            n = sp.value_load(n_items[0:1, 0:1], min_val=E, max_val=2 * E)
            with sp.If(n > E):
                with sp.Fori(0, E) as i:
                    item_weights(MOE_BASE // 6 + E * FC + i * FC, moe_g_d[0][i], moe_u_d[0][i], moe_d_d[0][i])
            for b in range(NB):
                sp.wait_ge(h_ready, 2 * 4 + b + 1)
                sp.dma_start(out_d[0, b * P:(b + 1) * P, :], hm[:, b, :]).then_inc(stored, 16)
            sp.wait_ge(stored, 16 * NB)

        @block.gpsimd
        def _(pool):
            pool.memset(zeros[:], 0.0).then_inc(zeros_set, 1)
            pool.memset(xbc[:, :, 0:TAPS - 1], 0.0).then_inc(pad_set, 1)
            for l in range(LAYERS):
                rows = prm_rows[:, l, :]
                pool.dma_start(rows[0:PRM_B], conv_w_d[l].rearrange("k (m c) -> (k m) c", c=P)).then_inc(prm_in, 16)
                pool.dma_start(rows[PRM_B:PRM_N], conv_b_d[l].rearrange("(m c) -> m c", c=P)).then_inc(prm_in, 16)
                pool.dma_start(rows[PRM_N:PRM_N + 2], ret_norm_d[l].rearrange("(m c) -> m c", c=P)).then_inc(prm_in, 16)
                pool.dma_start(rows[PRM_N + 2:PRM], ssd_norm_d[l].rearrange("(m c) -> m c", c=P)).then_inc(prm_in, 16)
                for i, src in enumerate((dt_bias_d, a_log_d, d_skip_d)):
                    pool.dma_start(heads8[:, l, i, :], src[l].partition_broadcast(P)).then_inc(prm_in, 16)
            pool.dma_start(rw[:], router_d[0].rearrange("(k p) e -> p k e", p=P)).then_inc(rw_in, 16)
            for l in range(LAYERS):
                pool.wait_ge(sb_z, l + 1)
                if l > 0:
                    pool.wait_ge(normw_in, 16 * 2 * l)
                pool.dma_start(normw, norm2_d[l].partition_broadcast(P)).then_inc(normw_in, 16)
                if l + 1 < LAYERS:
                    pool.wait_ge(mix_sb, l + 1)
                    pool.memset(xbc[:, :, 0:TAPS - 1], 0.0).then_inc(pad_set, 1)
                pool.wait_ge(h_ready, 2 * (2 * l + 2))
                pool.wait_ge(normw_in, 16 * (2 * l + 1))
                nxt = norm1_d[l + 1] if l + 1 < LAYERS else final_d
                pool.dma_start(normw, nxt.partition_broadcast(P)).then_inc(normw_in, 16)

        @block.scalar
        def _(act):
            steps = [0]

            def chain(ins):
                steps[0] += 1
                ins.then_inc(act_step, 1)
                act.wait_ge(act_step, steps[0])

            for b in range(NB):
                act.dma_start(x[:, b, :], x_d[0, b * P:(b + 1) * P, :]).then_inc(x_in[b], 16)
            act.dma_start(normw, norm1_d[0].partition_broadcast(P)).then_inc(normw0_in, 16)
            act.dma_start(cst[:, 0:C_COS], const_d[:, 0:C_COS]).then_inc(const_in, 16)

            def norm(u, ready, counts):
                nc.scalar.activation(sm(1)[0:1, 4:5], zeros[0:1, 0:1], ACT.Sqrt)
                for b in range(NB):
                    act.wait_ge(ready[b], counts[b])
                    nc.scalar.activation(hm[:, b, :], x[:, b, :], ACT.Square, accum_out=sm(0)[:, b:b + 1])\
                        .then_inc(sumsq, 1)
                    act.wait_ge(sumsq, 2 * u + b + 1)
                    nc.scalar.activation(sm(1)[:, b:b + 1], sm(0)[:, b:b + 1], ACT.Sqrt, bias=EPS, scale=1.0 / D)\
                        .then_inc(rms_ready, 1)

            def split(g, slot, rnd, n=SUB):
                act.wait_ge(landed[slot], (rnd + 1) * 16)
                if not isinstance(g, int) or g >= SPL:
                    act.wait_ge(split_used, g - (SPL - 1))
                nc.scalar.activation(w_hi[:, slot % SPL, 0:n], raw[:, slot, 0:n], ACT.Copy).then_inc(hi_ready, 1)

            def win_split(l, ci, halves=(0, 1)):
                for half in halves:
                    g = MIX_BASE[l] + 2 * ci + half
                    split(g, g % 6, g // 6, 4 * WIN[ci][2])

            def wout_split(l, i):
                g = MIX_BASE[l] + 14 + i
                split(g, g % 6, g // 6)

            def hT(u, bank, q):
                act.wait_ge(hT_psum, 4 * u + q + 1)
                nc.scalar.activation(aT_hi[:, 4 * q:4 * q + 4, :].rearrange("p a b -> p (a b)"),
                                     ps[:, bank + q, :], ACT.Copy).then_inc(hT_hi, 1)

            def mixer(l):
                def chunk_done(ci):
                    act.wait_ge(split_used, MIX_BASE[l] + 2 * ci + 2)

                for q in range(4):
                    hT(2 * l, 4, q)
                    if l == 0 and q % 2 == 1:
                        win_split(l, 0, (q // 2,))
                win_split(l, 1)
                chunk_done(0)
                act.wait_ge(pad_set, l + 1)
                nc.scalar.activation(xbc[:, 0:4, TAPS - 1:], banks(0, 2).rearrange("p (m t) -> p m t", m=4),
                                     ACT.Copy).then_inc(win_out, 1)
                act.wait_ge(prm_psum, l + 1)
                nc.scalar.activation(prm[:], ps[:, 4, 0:PRM], ACT.Copy).then_inc(prm_ready, 1)
                win_split(l, 2)
                chunk_done(1)
                nc.scalar.activation(xbc[:, 4:6, TAPS - 1:], ps[:, 2, :].rearrange("p (m t) -> p m t", m=2), ACT.Copy)
                nc.scalar.activation(sm(2), ps[:, 3, 0:16], ACT.Copy).then_inc(win_out, 1)
                nc.scalar.activation(sm(3, 8), heads8[:, l, 1, :], ACT.Exp)
                act.wait_ge(dt_biased, l + 1)
                chain(nc.scalar.activation(sm(4), sm(2), ACT.Abs))
                chain(nc.scalar.activation(sm(4), sm(4), ACT.Exp, scale=-1.0))
                nc.scalar.activation(sm(5), sm(4), ACT.Ln, bias=1.0).then_inc(dt_ln, 1)
                win_split(l, 3)
                chunk_done(2)
                nc.scalar.activation(scr[:, 2, 0:1024], banks(0, 2), ACT.Copy).then_inc(win_out, 1)
                act.wait_ge(conv_tap, TAPS * (l + 1))
                nc.scalar.activation(cvf, cvf, ACT.Silu).then_inc(conv_silu, 1)
                act.wait_ge(cs_psum, l + 1)
                nc.scalar.activation(csT, ps[0:SH, 4, P:P + T], ACT.Copy).then_inc(csT_ready, 1)
                win_split(l, 4)
                chunk_done(3)
                act.wait_ge(h_ready, 2 * (2 * l + 1))
                nc.scalar.activation(bqk[:, 0:2, :].rearrange("p a b -> p (a b)"), ps[:, 2, :], ACT.Copy,
                                     scale=HD ** -0.5)
                nc.scalar.activation(bqk[:, 2:4, :].rearrange("p a b -> p (a b)"), ps[:, 3, :], ACT.Copy)\
                    .then_inc(win_out, 1)
                for b in range(NB):
                    act.wait_ge(xT_psum, 2 * l + b + 1)
                    nc.scalar.activation(xtok[:, b, :], ps[:, 5 + b, :], ACT.Copy).then_inc(xtok_ready, 1)
                win_split(l, 5)
                for g in range(SG):
                    act.wait_ge(seg_ready, 2 * l + g + 1)
                    nc.scalar.activation(scr[:, g, :], scr[:, g, :], ACT.Exp).then_inc(seg_exp, 1)
                win_split(l, 6, (0,))
                chunk_done(4)
                nc.scalar.activation(sz[:].rearrange("p a b -> p (a b)"), banks(0, 2), ACT.Silu).then_inc(win_out, 1)
                win_split(l, 6, (1,))
                act.wait_ge(sb_z, l + 1)
                chain(nc.scalar.activation(xbf.rearrange("p (h n) -> p h n", h=BH), ps[:, 4:8, 0:SC], ACT.Abs))
                chain(nc.scalar.activation(xbf, xbf, ACT.Exp, scale=-1.0))
                nc.scalar.activation(xbf, xbf, ACT.Ln, bias=1.0).then_inc(sb_ln, 1)
                chunk_done(5)
                pv = ps[:, 2:4, :]
                nc.scalar.activation(rv[:], pv[:, :, 0:256], ACT.Copy).then_inc(rv_ready, 1)
                nc.scalar.activation(rg[:], pv[:, :, 256:512], ACT.Silu).then_inc(win_out, 1)
                wout_split(l, 0)
                wout_split(l, 1)
                act.wait_ge(ret_var, l + 1)
                nc.scalar.activation(sm(9, 8), sm(9, 8), ACT.Sqrt, bias=EPS, scale=1.0 / HD).then_inc(ret_std, 1)
                act.wait_ge(gated, l + 1)
                for b in range(NB):
                    for g in range(SG):
                        nc.scalar.activation(xtok[:, b, g * 256:(g + 1) * 256], sz[:, b, g * 256:(g + 1) * 256],
                                             ACT.Square, accum_out=sm(10)[:, 2 * b + g:2 * b + g + 1])\
                            .then_inc(gated_sq, 1)
                act.wait_ge(gated_sq, 4 * (l + 1))
                nc.scalar.activation(sm(10, 4), sm(10, 4), ACT.Sqrt, bias=EPS, scale=1.0 / 256).then_inc(ssd_rms, 1)
                chunk_done(6)
                nc.scalar.activation(bv[:].rearrange("p a b -> p (a b)"), ps[:, 0, :], ACT.Copy).then_inc(win_out, 1)

                def mixT(q):
                    act.wait_ge(mixT_psum, 4 * l + q + 1)
                    for k in (2 * q, 2 * q + 1):
                        dst = aT_hi[:, 2 * k:2 * k + 2, :].rearrange("p a b -> p (a b)")
                        src = ps[:, MIXT[q], (k % 2) * 256:(k % 2) * 256 + 256]
                        if k < 6:
                            ins = nc.scalar.activation(dst, src, ACT.Copy, scale=prm[:, PRM_N + k:PRM_N + k + 1])
                        else:
                            ins = nc.scalar.activation(dst, src, ACT.Copy)
                    ins.then_inc(mixT_hi, 1)

                mixT(0)
                mixT(1)
                wout_split(l, 2)
                act.wait_ge(sb_min, l + 1)
                nc.scalar.activation(xbf, xbf, ACT.Exp).then_inc(sb_w, 1)
                act.wait_ge(sb_y, l + 1)
                nc.scalar.activation(hm[:, :, 768:1024], ps[:, 7, :].rearrange("p (b n) -> p b n", b=NB),
                                     ACT.Copy, scale=-1.0).then_inc(mix_sb, 1)
                mixT(2)
                wout_split(l, 3)
                mixT(3)
                for half in range(2):
                    wout_split(l, 4 + half)

            def gathered(i):
                n = i
                for q in range(2):
                    act.wait_ge(gath_psum, n * 2 + q + 1)
                    nc.scalar.activation(aT_hi[:, 4 * q:4 * q + 4, :].rearrange("p a b -> p (a b)"),
                                         ps[:, 5 + q, :], ACT.Copy).then_inc(gath_hi, 1)
                act.wait_ge(selgT_psum, n + 1)
                nc.scalar.activation(selgT, ps[:, 7, 0:256].rearrange("p (b s) -> p b s", b=NB), ACT.Copy)\
                    .then_inc(selgT_ready, 1)

            def take_y():
                nc.scalar.activation(y_sb, banks(3, 5), ACT.Copy).then_inc(y_ready, 1)

            def item(i, more=True):
                it = i + 1
                g0 = i * ITEM_SUBS + MOE_BASE
                r0 = i * FC + MOE_BASE // 6

                def sp_(pos, c=None):
                    slot, r = at(pos)
                    if c is None:
                        split(g0 + pos, slot, r0 + r)
                    else:
                        split(g0 + pos + (c - 1) * 6, slot, r0 + r + (c - 1))

                def silu():
                    nc.scalar.activation(silu_g, ps[:, 0, :], ACT.Silu).then_inc(silu_done, 1)

                def evac_sT(c):
                    act.wait_ge(sT_psum, it * FC + c + 1)
                    nc.scalar.activation(aT_hi[:, 8:12, :].rearrange("p a b -> p (a b)"), ps[:, 2, :], ACT.Copy)\
                        .then_inc(sT_hi, 1)

                act.wait_ge(split_used, g0)
                act.wait_ge(y_zero, i + 1)
                take_y()
                sp_(2)
                sp_(3)
                act.wait_ge(split_used, g0 + 2)
                silu()
                sp_(4)
                with act.Fori(1, FC) as c:
                    sp_(5, c)
                    sp_(6, c)
                    sp_(7, c)
                    evac_sT(c - 1)
                    act.wait_ge(s_ready, it * FC + c)
                    act.wait_ge(split_used, g0 + c * 6)
                    silu()
                    sp_(8, c)
                    sp_(9, c)
                    sp_(10, c)
                evac_sT(FC - 1)
                sp_(6 * FC - 1)
                if more:
                    sp_(6 * FC)
                gathered(i + 1)
                if more:
                    sp_(6 * FC + 1)

            def moe(last):
                gathered(0)
                with act.Fori(0, last) as i:
                    item(i)
                item(last, more=False)
                act.wait_ge(split_used, (last + 1) * ITEM_SUBS + MOE_BASE)
                take_y()

            def dense():
                def sp_(pos, c=None):
                    slot, r = at(pos)
                    step = 0 if c is None else c - 1
                    split(DENSE_BASE + pos + step * 6, slot, DENSE_BASE // 6 + r + step)

                def silu():
                    nc.scalar.activation(silu_g2, banks(0, 2), ACT.Silu).then_inc(silu_done, 1)

                def evac_sT(c):
                    act.wait_ge(sT_psum, c + 1)
                    act.wait_ge(split_used, DENSE_BASE + 4 + c * 6)
                    nc.scalar.activation(s2T_hi[:].rearrange("p a b -> p (a b)"), banks(2, 4), ACT.Copy)\
                        .then_inc(sT_hi, 1)

                for q in range(4):
                    hT(1, 0, q)
                sp_(2)
                sp_(3)
                act.wait_ge(split_used, DENSE_BASE + 2)
                silu()
                sp_(4)
                with act.Fori(1, FC) as c:
                    sp_(5, c)
                    evac_sT(c - 1)
                    sp_(6, c)
                    sp_(7, c)
                    act.wait_ge(s_ready, c)
                    act.wait_ge(split_used, c * 6 + DENSE_BASE)
                    silu()
                    sp_(8, c)
                    sp_(9, c)
                    sp_(10, c)
                evac_sT(FC - 1)
                for pos in range(3):
                    sp_(6 * FC - 1 + pos)

            act.wait_ge(zeros_set, 1)
            norm(0, x_in, (16, 16))
            mixer(0)
            norm(1, [x_mixed] * NB, (1, 2))
            dense()
            norm(2, [x_dense] * NB, (1, 2))
            mixer(1)
            norm(3, [x_mixed] * NB, (3, 4))
            for q in range(4):
                act.wait_ge(h2T_psum, q + 1)
                nc.scalar.activation(h2T[:, 4 * q:4 * q + 4, :].rearrange("p a b -> p (a b)"), ps[:, q, :], ACT.Copy)\
                    .then_inc(h2T_ready, 1)
            act.wait_ge(gate_diff, 1)
            nc.scalar.activation(sm(6, 2), sm(6, 2), ACT.Exp).then_inc(gate_exp, 1)
            act.wait_ge(routed, 1)
            last = act.value_load(n_items[0:1, 1:2], min_val=E - 1, max_val=2 * E - 1)
            moe(last)
            norm(4, [x_added] * NB, (last * 2 + 3, last * 2 + 4))

        @block.vector
        def _(dve):
            steps = [0]
            V = nc.vector

            def chain(ins):
                steps[0] += 1
                ins.then_inc(dve_step, 1)
                dve.wait_ge(dve_step, steps[0])

            def norm(u):
                if u == 0:
                    dve.wait_ge(normw0_in, 16)
                else:
                    dve.wait_ge(normw_in, 16 * u)
                for b in range(NB):
                    dve.wait_ge(rms_ready, 2 * u + b + 1)
                    V.reciprocal(sm(1)[:, 2 + b:3 + b], sm(1)[:, b:b + 1]).then_inc(rstd_ready, 1)
                    dve.wait_ge(rstd_ready, 2 * u + b + 1)
                    V.scalar_tensor_tensor(hm[:, b, :], x[:, b, :], sm(1)[:, 2 + b:3 + b], normw, ALU.mult, ALU.mult)\
                        .then_inc(h_ready, 1)

            def split(g, slot, n=SUB):
                dve.wait_ge(hi_ready, g + 1)
                V.tensor_tensor(w_lo[:, slot % SPL, 0:n], raw[:, slot, 0:n], w_hi[:, slot % SPL, 0:n].bitcast(F32),
                                ALU.subtract).then_inc(lo_ready[slot], 1)

            def win_split(l, ci, halves=(0, 1)):
                for half in halves:
                    g = MIX_BASE[l] + 2 * ci + half
                    split(g, g % 6, 4 * WIN[ci][2])

            def wout_split(l, i):
                g = MIX_BASE[l] + 14 + i
                split(g, g % 6)

            def lo_part(dst, src, hi):
                return V.tensor_tensor(dst.rearrange("p a b -> p (a b)"), src,
                                       hi.rearrange("p a b -> p (a b)").bitcast(F32), ALU.subtract)

            def hT(u, bank, q):
                dve.wait_ge(hT_hi, 4 * u + q + 1)
                lo_part(aT_lo[:, 4 * q:4 * q + 4, :], ps[:, bank + q, :], aT_hi[:, 4 * q:4 * q + 4, :])\
                    .then_inc(hT_lo, 1)

            def bc(ap, shape):
                return ap.to_broadcast(shape)

            def mixer(l):
                for q in range(4):
                    hT(2 * l, 4, q)
                    if l == 0 and q % 2 == 1:
                        win_split(l, 0, (q // 2,))
                win_split(l, 1)
                win_split(l, 2)
                dve.wait_ge(prm_in, 16 * 7 * LAYERS)
                dve.wait_ge(win_out, 7 * l + 2)
                V.tensor_tensor(sm3(2), sm3(2), bc(heads8[:, l, 0, :].unsqueeze(1), [P, NB, SH]), ALU.add)\
                    .then_inc(dt_biased, 1)
                dve.wait_ge(prm_ready, l + 1)
                for tap in range(TAPS - 1, -1, -1):
                    for m in range(XT):
                        w = prm[:, tap * XT + m:tap * XT + m + 1]
                        src = xbc[:, m, tap:tap + T]
                        if tap == TAPS - 1:
                            ins = V.tensor_scalar(cv[:, m, :], src, w, prm[:, PRM_B + m:PRM_B + m + 1],
                                                  ALU.mult, ALU.add)
                        else:
                            ins = V.scalar_tensor_tensor(cv[:, m, :], src, w, cv[:, m, :], ALU.mult, ALU.add)
                    ins.then_inc(conv_tap, 1)
                    dve.wait_ge(conv_tap, TAPS * l + TAPS - tap)
                    if tap == 2:
                        dve.wait_ge(dt_ln, l + 1)
                        chain(V.tensor_scalar(sm(6), sm(4), 1.0, None, ALU.add))
                        chain(V.scalar_tensor_tensor(sm(4), sm(6), -1.0, sm(4), ALU.add, ALU.subtract))
                        chain(V.reciprocal(sm(6), sm(6)))
                        chain(V.tensor_tensor(sm(4), sm(4), sm(6), ALU.mult))
                        chain(V.tensor_tensor(sm(5), sm(5), sm(4), ALU.subtract))
                        chain(V.scalar_tensor_tensor(sm(5), sm(2), 0.0, sm(5), ALU.max, ALU.add))
                        V.scalar_tensor_tensor(sm3(6), sm3(5), -1.0, bc(sm(3, 8).unsqueeze(1), [P, NB, SH]),
                                               ALU.mult, ALU.mult).then_inc(a_ready, 1)
                        win_split(l, 3)
                dve.wait_ge(win_out, 7 * l + 3)
                dve.wait_ge(tables_in, 16)
                v4 = lambda a: a.rearrange("p (m t) -> p m t", m=4)
                V.tensor_tensor(v4(scr[:, 0, 0:1024]), v4(scr[:, 2, 0:1024]),
                                bc(cst[:, C_COS:C_COS + T].unsqueeze(1), [P, 4, T]), ALU.mult)
                dve.wait_ge(rot_psum, l + 1)
                chain(V.tensor_tensor(v4(scr[:, 1, 0:1024]), v4(banks(5, 7)),
                                      bc(cst[:, C_SIN:C_SIN + T].unsqueeze(1), [P, 4, T]), ALU.mult))
                V.tensor_tensor(qkr[:, 0:1024], scr[:, 0, 0:1024], scr[:, 1, 0:1024], ALU.add).then_inc(qk_ready, 1)
                dve.wait_ge(csT_ready, l + 1)
                V.tensor_copy(sm(7), ps[:, 4, 0:16]).then_inc(cs_ready, 1)
                win_split(l, 4)
                for g in range(SG):
                    dve.wait_ge(cb_psum, 2 * l + g + 1)
                    V.tensor_tensor(cb[:, g, :], ps[:, 4 if g == 0 else 7, 0:SC], cst[:, C_CAUSAL:C_CAUSAL + SC],
                                    ALU.mult).then_inc(cb_ready, 1)
                for b in range(NB):
                    dve.wait_ge(xtok_ready, 2 * l + b + 1)
                    V.tensor_tensor(xdt[:, b, :].rearrange("p (h d) -> p h d", h=SH),
                                    ps[:, 5 + b, :].rearrange("p (h d) -> p h d", h=SH),
                                    bc(sm(5)[:, 8 * b:8 * b + 8].unsqueeze(2), [P, SH, HD]), ALU.mult)\
                        .then_inc(xdt_ready, 1)
                win_split(l, 5, (0,))
                dve.wait_ge(qk_ready, l + 1)
                for g in range(SG):
                    dve.wait_ge(csb_psum, 2 * l + g + 1)
                    for hh in range(4):
                        h = 4 * g + hh
                        src = ps[:, 4 + 2 * g + hh // 2, (hh % 2) * T:(hh % 2) * T + T]
                        V.tensor_scalar(scr[:, g, hh * SC:hh * SC + T], src, sm(7)[:, h:h + 1], 0.0,
                                        ALU.subtract, ALU.min)
                        ins = V.tensor_scalar(scr[:, g, hh * SC + T:hh * SC + SC], src[:, P:T],
                                              sm(7)[:, 8 + h:9 + h], 0.0, ALU.subtract, ALU.min)
                    ins.then_inc(seg_ready, 1)
                win_split(l, 5, (1,))
                for b in range(NB):
                    xh = xtok[:, b, :].rearrange("p (h d) -> p h d", h=SH)
                    ins = V.tensor_tensor(xh, xh, bc(heads8[:, l, 2, :].unsqueeze(2), [P, SH, HD]), ALU.mult)
                chain(ins)
                win_split(l, 6, (0,))
                dve.wait_ge(ret_psum, l + 1)
                V.tensor_tensor(scr[:, 2, :].rearrange("p (h n) -> p h n", h=RH), ps[:, 4:8, 0:SC],
                                cst[:, C_RET:C_RET + RH * SC].rearrange("p (h n) -> p h n", h=RH), ALU.mult)\
                    .then_inc(s_ret, 1)
                for g in range(SG):
                    dve.wait_ge(seg_exp, 2 * l + g + 1)
                    s4 = scr[:, g, :].rearrange("p (h n) -> p h n", h=4)
                    V.tensor_tensor(s4, s4, bc(cb[:, g, :].unsqueeze(1), [P, 4, SC]), ALU.mult).then_inc(s_ssd, 1)
                win_split(l, 6, (1,))
                z4 = ps[:, 4:8, 0:SC]
                xb4 = xbf.rearrange("p (h n) -> p h n", h=BH)
                sp4 = qkr[:].rearrange("p (h n) -> p h n", h=BH)
                strict = bc(cst[:, C_STRICT:C_STRICT + SC].unsqueeze(1), [P, BH, SC])
                dve.wait_ge(sb_ln, l + 1)
                chain(V.scalar_tensor_tensor(sp4, z4, 0.0, xb4, ALU.max, ALU.add))
                V.tensor_tensor(sp4, sp4, strict, ALU.mult).then_inc(sb_sp, 1)
                wout_split(l, 0)
                r8 = lambda a: a.rearrange("p (h d) -> p h d", h=8)
                ry = ps[:, 1, :]
                dve.wait_ge(ret_y, l + 1)
                chain(V.tensor_reduce(sm(8, 8), r8(ry), AX.X, ALU.add))
                chain(V.tensor_scalar(sm(8, 8), sm(8, 8), 1.0 / HD, None, ALU.mult))
                chain(V.tensor_tensor(r8(cvf[:, 0:512]), r8(ry), bc(sm(8, 8).unsqueeze(2), [P, 8, HD]), ALU.subtract))
                chain(V.tensor_tensor(cvf[:, 512:1024], cvf[:, 0:512], cvf[:, 0:512], ALU.mult))
                V.tensor_reduce(sm(9, 8), r8(cvf[:, 512:1024]), AX.X, ALU.add).then_inc(ret_var, 1)
                wout_split(l, 1)
                dve.wait_ge(ssd_y, l + 1)
                szf = sz[:].rearrange("p a b -> p (a b)")
                xf = xtok[:].rearrange("p a b -> p (a b)")
                chain(V.tensor_tensor(xf, banks(2, 4), xf, ALU.add))
                V.tensor_tensor(szf, szf, xf, ALU.mult).then_inc(gated, 1)
                dve.wait_ge(ret_std, l + 1)
                chain(V.reciprocal(sm(9, 8), sm(9, 8)))
                chain(V.tensor_tensor(r8(cvf[:, 0:512]), r8(cvf[:, 0:512]), bc(sm(9, 8).unsqueeze(2), [P, 8, HD]),
                                      ALU.mult))
                V.tensor_tensor(hm[:, :, 0:256], cvf[:, 0:512].rearrange("p (b n) -> p b n", b=NB), rg[:], ALU.mult)\
                    .then_inc(mix_ret, 1)
                dve.wait_ge(ssd_rms, l + 1)
                chain(V.reciprocal(sm(10, 4), sm(10, 4)))
                for b in range(NB):
                    ins = V.tensor_tensor(hm[:, b, 256:768].rearrange("p (g n) -> p g n", g=SG),
                                          sz[:, b, :].rearrange("p (g n) -> p g n", g=SG),
                                          bc(sm(10)[:, 2 * b:2 * b + 2].unsqueeze(2), [P, SG, 256]), ALU.mult)
                ins.then_inc(mix_ssd, 1)

                def mixT(q):
                    dve.wait_ge(mixT_hi, 4 * l + q + 1)
                    for k in (2 * q, 2 * q + 1):
                        dst = aT_lo[:, 2 * k:2 * k + 2, :].rearrange("p a b -> p (a b)")
                        hi = aT_hi[:, 2 * k:2 * k + 2, :].rearrange("p a b -> p (a b)").bitcast(F32)
                        src = ps[:, MIXT[q], (k % 2) * 256:(k % 2) * 256 + 256]
                        if k < 6:
                            ins = V.scalar_tensor_tensor(dst, src, prm[:, PRM_N + k:PRM_N + k + 1], hi,
                                                         ALU.mult, ALU.subtract)
                        else:
                            ins = V.tensor_tensor(dst, src, hi, ALU.subtract)
                    ins.then_inc(mixT_lo, 1)

                mixT(0)
                mixT(1)
                dve.wait_ge(sb_log, l + 1)
                V.tensor_scalar(xb4, z4, 0.0, None, ALU.min).then_inc(sb_min, 1)
                dve.wait_ge(sb_w, l + 1)
                V.tensor_tensor(xb4, xb4, strict, ALU.mult).then_inc(sb_wm, 1)
                wout_split(l, 2)
                mixT(2)
                wout_split(l, 3)
                mixT(3)
                wout_split(l, 4)

                def add_mixed(b, n):
                    xs = x[:, b, n * 512:(n + 1) * 512]
                    return V.tensor_tensor(xs, ps[:, 2 * b + n, :], xs, ALU.add)

                dve.wait_ge(split_used, MIX_BASE[l] + 17)
                add_mixed(0, 0)
                add_mixed(1, 0)
                wout_split(l, 5)
                dve.wait_ge(mix_block0, l + 1)
                add_mixed(0, 1).then_inc(x_mixed, 1)
                dve.wait_ge(split_used, MIX_BASE[l] + 18)
                add_mixed(1, 1).then_inc(x_mixed, 1)

            def route():
                lg, oh1, oh2, tmp, t2, gts = (sm3(i) for i in (11, 12, 13, 14, 15, 3))
                e8 = bc(cst[:, C_E8:C_E8 + E].unsqueeze(1), [P, NB, E])
                col = lambda i: bc(sm(i, 2).unsqueeze(2), [P, NB, E])
                dve.wait_ge(logits, 1)
                chain(V.tensor_copy(sm(11), ps[:, 4, 0:16]))
                chain(V.tensor_reduce(sm(8, 2), lg, AX.X, ALU.max))
                chain(V.tensor_tensor(tmp, lg, col(8), ALU.is_equal))
                chain(V.tensor_tensor(tmp, tmp, e8, ALU.mult))
                chain(V.tensor_reduce(sm(9, 2), tmp, AX.X, ALU.min))
                chain(V.tensor_tensor(oh1, e8, col(9), ALU.is_equal))
                chain(V.scalar_tensor_tensor(t2, oh1, -3e38, lg, ALU.mult, ALU.add))
                chain(V.tensor_reduce(sm(10, 2), t2, AX.X, ALU.max))
                V.tensor_tensor(sm(6, 2), sm(10, 2), sm(8, 2), ALU.subtract).then_inc(gate_diff, 1)
                chain(V.tensor_tensor(tmp, t2, col(10), ALU.is_equal))
                chain(V.tensor_tensor(tmp, tmp, e8, ALU.mult))
                chain(V.tensor_reduce(sm(9, 2), tmp, AX.X, ALU.min))
                chain(V.tensor_tensor(oh2, e8, col(9), ALU.is_equal))
                V.tensor_tensor(lg, oh1, oh2, ALU.add).then_inc(sel_ready, 1)
                dve.wait_ge(gate_exp, 1)
                chain(V.tensor_scalar(sm(7, 2), sm(6, 2), 1.0, None, ALU.add))
                chain(V.reciprocal(sm(7, 2), sm(7, 2)))
                chain(V.tensor_tensor(sm(6, 2), sm(6, 2), sm(7, 2), ALU.mult))
                chain(V.tensor_tensor(gts, oh1, col(7), ALU.mult))
                chain(V.tensor_tensor(tmp, oh2, col(6), ALU.mult))
                for half in range(2):
                    V.tensor_tensor(rank_gate[:, 1, :, 1 + E * half:1 + E * half + E], gts, tmp, ALU.add)
                dve.wait_ge(sel_ready, 1)
                dve.wait_ge(ranks, 1)
                chain(V.tensor_tensor(t2, ps[:, 5, 0:16].rearrange("p (b e) -> p b e", b=NB), lg, ALU.mult))
                for half in range(2):
                    V.tensor_scalar(rank_gate[:, 0, :, 1 + E * half:1 + E * half + E], t2, -1.0 - P * half, None, ALU.add)
                chain(V.tensor_reduce(sm(8, 1), ps[:, 5, 16:16 + E], AX.X, ALU.max))
                chain(V.tensor_scalar(sm(8, 1), sm(8, 1), float(P), float(E), ALU.is_gt, ALU.mult))
                V.tensor_scalar(n_items[:, 0:1], sm(8, 1), float(E), None, ALU.add)
                V.tensor_scalar(n_items[:, 1:2], sm(8, 1), float(E - 1), None, ALU.add).then_inc(routed, 1)
                dve.wait_ge(routed, 1)

            def select(i, dyn):
                n = i
                cols = rank_gate[:, :, :, bass.ds(i, 2)] if dyn else rank_gate[:, :, :, i:i + 2]
                V.tensor_copy(cur[:].rearrange("p a b i -> p (a b) i"), cols.rearrange("p a b i -> p (a b) i"))\
                    .then_inc(cur_ready, 1)
                dve.wait_ge(cur_ready, n + 1)
                for b in range(NB):
                    V.tensor_scalar(sel[:, b, :], iota, cur[:, 0, b, 1:2], None, ALU.is_equal)
                    ins = V.tensor_scalar(selg[:, b, :], iota, cur[:, 0, b, 0:1], cur[:, 1, b, 0:1],
                                          ALU.is_equal, ALU.mult)
                ins.then_inc(sel_built, 1)

            def gathered(i):
                n = i
                for q in range(2):
                    dve.wait_ge(gath_hi, n * 2 + q + 1)
                    lo_part(aT_lo[:, 4 * q:4 * q + 4, :], ps[:, 5 + q, :], aT_hi[:, 4 * q:4 * q + 4, :])\
                        .then_inc(gath_lo, 1)

            def add_y(i):
                n = i
                for b in range(NB):
                    dve.wait_ge(comb_psum, n * 2 + b + 1)
                    for h in range(2):
                        xs = x[:, b, h * 512:(h + 1) * 512]
                        ins = V.tensor_tensor(xs, ps[:, COMB[2 * b + h], :], xs, ALU.add)
                    ins.then_inc(x_added, 1)

            def item(i, more=True):
                it = i + 1
                g0 = i * ITEM_SUBS + MOE_BASE

                def lo(pos, c=None):
                    split(g0 + pos if c is None else g0 + pos + (c - 1) * 6, pos % 6)

                def evac_sT(c):
                    dve.wait_ge(sT_hi, it * FC + c + 1)
                    lo_part(aT_lo[:, 8:12, :], ps[:, 2, :], aT_hi[:, 8:12, :]).then_inc(sT_lo, 1)

                def gate_times_up(c, done):
                    dve.wait_ge(silu_done, it * FC + c + 1)
                    dve.wait_ge(split_used, done)
                    V.tensor_tensor(s_act, ps[:, 1, :], silu_g, ALU.mult).then_inc(s_ready, 1)

                lo(2)
                lo(3)
                lo(4)
                add_y(i)
                gate_times_up(0, g0 + 4)
                with dve.Fori(1, FC) as c:
                    lo(5, c)
                    lo(6, c)
                    lo(7, c)
                    evac_sT(c - 1)
                    lo(8, c)
                    lo(9, c)
                    lo(10, c)
                    gate_times_up(c, g0 + 2 + c * 6)
                dve.wait_ge(x_added, i * 2 + 2)
                select(i + 1, True)
                evac_sT(FC - 1)
                lo(6 * FC - 1)
                if more:
                    lo(6 * FC)
                gathered(i + 1)
                if more:
                    lo(6 * FC + 1)

            def moe(last):
                select(0, False)
                gathered(0)
                with dve.Fori(0, last) as i:
                    item(i)
                item(last, more=False)
                add_y(last + 1)
                dve.wait_ge(x_added, last * 2 + 4)

            def dense():
                def lo(pos, c=None):
                    split(DENSE_BASE + pos if c is None else DENSE_BASE + pos + (c - 1) * 6, pos % 6)

                def evac_sT(c):
                    dve.wait_ge(sT_hi, c + 1)
                    lo_part(s2T_lo[:], banks(2, 4), s2T_hi[:]).then_inc(sT_lo, 1)

                def gate_times_up(c, done):
                    dve.wait_ge(silu_done, c + 1)
                    dve.wait_ge(split_used, done)
                    V.tensor_tensor(s_act2, banks(2, 4), silu_g2, ALU.mult).then_inc(s_ready, 1)

                def add_dense(b):
                    xs = x[:, b, :]
                    V.tensor_tensor(xs, banks(4 + 2 * b, 6 + 2 * b), xs, ALU.add).then_inc(x_dense, 1)

                for q in range(4):
                    hT(1, 0, q)
                lo(2)
                lo(3)
                lo(4)
                gate_times_up(0, DENSE_BASE + 4)
                with dve.Fori(1, FC) as c:
                    lo(5, c)
                    evac_sT(c - 1)
                    lo(6, c)
                    lo(7, c)
                    lo(8, c)
                    lo(9, c)
                    gate_times_up(c, c * 6 + (DENSE_BASE + 2))
                    lo(10, c)
                evac_sT(FC - 1)
                lo(6 * FC - 1)
                lo(6 * FC)
                dve.wait_ge(dense_block0, 1)
                add_dense(0)
                dve.wait_ge(split_used, DENSE_BASE + ITEM_SUBS)
                add_dense(1)
                lo(6 * FC + 1)

            V.memset(rank_gate[:], -1.0)
            norm(0)
            mixer(0)
            norm(1)
            dense()
            norm(2)
            mixer(1)
            norm(3)
            route()
            last = dve.value_load(n_items[0:1, 1:2], min_val=E - 1, max_val=2 * E - 1)
            moe(last)
            norm(4)

        @block.tensor
        def _(pe):
            mm = nc.tensor.matmul

            def keep_warm(bank, n):
                for _ in range(n):
                    mm(ps[:, bank, :], zeros[:], zeros[:, 0:1].to_broadcast([P, 512]), start=True, stop=True,
                       skip_group_check=True)

            def passes(out, lhs_hi, lhs_lo, rhs_hi, rhs_lo, start, stop):
                mm(out, lhs_hi, rhs_hi, start=start, stop=False, skip_group_check=True)
                mm(out, lhs_hi, rhs_lo, start=False, stop=False, skip_group_check=True)
                return mm(out, lhs_lo, rhs_hi, start=False, stop=stop, skip_group_check=True)

            def win_chunk(l, ci, halves=(0, 1)):
                name, _, n = WIN[ci]
                par = 2 * (ci % 2)
                if ci >= 2:
                    pe.wait_ge(win_out, 7 * l + ci - 1)
                tiles = TILES_T.get(name, 0)
                for half in halves:
                    g = MIX_BASE[l] + 2 * ci + half
                    pe.wait_ge(lo_ready[g % 6], g // 6 + 1)
                    hi, lo = win_view(w_hi, g % SPL, n), win_view(w_lo, g % SPL, n)
                    first = half == 0
                    for m in range(tiles):
                        out = banks(par, par + 2)[:, m * T:(m + 1) * T]
                        for kk in range(4):
                            k = 4 * half + kk
                            cols = slice(m * P, (m + 1) * P)
                            ins = passes(out, hi[:, kk, cols], lo[:, kk, cols],
                                         aT_hi[:, 2 * k:2 * k + 2, :].rearrange("p a b -> p (a b)"),
                                         aT_lo[:, 2 * k:2 * k + 2, :].rearrange("p a b -> p (a b)"),
                                         start=first and kk == 0 and m % 2 == 0, stop=k == KD - 1)
                    c0 = tiles * P
                    if c0 < n:
                        for b in range(NB):
                            if tiles:
                                out = ps[:, par + 1, 8 * b:8 * b + n - c0]
                            elif n <= 256:
                                out = ps[:, par, b * n:(b + 1) * n]
                            else:
                                out = ps[:, par + b, 0:n]
                            for kk in range(4):
                                k = 4 * half + kk
                                ins = passes(out, aT_hi[:, 2 * k + b, :], aT_lo[:, 2 * k + b, :],
                                             hi[:, kk, c0:n], lo[:, kk, c0:n],
                                             start=first and kk == 0 and not ((tiles or n <= 256) and b), stop=k == KD - 1)
                    ins.then_inc(split_used, 1)

            def scores(dst, q, k):
                mm(dst[:, 0:T], k[:, 0:P], q, start=True, stop=True, skip_group_check=True)
                return mm(dst[:, T:SC], k[:, P:T], q[:, P:T], start=False, stop=True, skip_group_check=True)

            def weighted(dst, s, v, b):
                if b == 0:
                    return mm(dst, s[:, 0:P], v[:, 0], start=True, stop=True, skip_group_check=True)
                mm(dst, s[:, P:T], v[:, 0], start=True, stop=False, skip_group_check=True)
                return mm(dst, s[:, T:SC], v[:, 1], start=False, stop=True, skip_group_check=True)

            def transposed_norm(u, bank, quarter_done):
                for b in range(NB):
                    pe.wait_ge(h_ready, 2 * u + b + 1)
                    for q in range(4):
                        for k in (2 * q, 2 * q + 1):
                            j = 2 * (k % 2) + b
                            ins = nc.tensor.transpose(ps[:, bank + q, j * P:(j + 1) * P], hm[:, b, k * P:(k + 1) * P],
                                                      ident)
                        if b == NB - 1:
                            ins.then_inc(quarter_done, 1)

            def mixer(l):
                opts = dict(skip_group_check=True)
                transposed_norm(2 * l, 4, hT_psum)
                keep_warm(0, 5)
                pe.wait_ge(hT_lo, 8 * l + 2)
                win_chunk(l, 0, (0,))
                pe.wait_ge(hT_lo, 8 * l + 4)
                win_chunk(l, 0, (1,))
                pe.wait_ge(prm_in, 16 * 7 * LAYERS)
                nc.tensor.transpose(ps[:, 4, 0:PRM], prm_rows[:, l, :], cst[0:PRM, C_ID:C_ID + PRM]).then_inc(prm_psum, 1)
                win_chunk(l, 1)
                win_chunk(l, 2)
                pe.wait_ge(prm_ready, l + 1)
                pe.wait_ge(a_ready, l + 1)
                a3 = sm3(6)
                c4 = ps[:, 4, :]
                mm(c4[:, 0:8], m_le, a3[:, 0], start=True, stop=True, **opts)
                mm(c4[:, 8:16], ones, a3[:, 0], start=False, stop=False, **opts)
                mm(c4[:, 8:16], m_le, a3[:, 1], start=False, stop=True, **opts)
                cT = ps[0:SH, 4, P:P + T]
                mm(cT[:, 0:P], a3[:, 0], m_le, start=False, stop=True, **opts)
                mm(cT[:, P:T], a3[:, 0], ones, start=False, stop=False, **opts)
                mm(cT[:, P:T], a3[:, 1], m_le, start=False, stop=True, **opts).then_inc(cs_psum, 1)
                pe.wait_ge(win_out, 7 * l + 3)
                for m in range(4):
                    ins = mm(banks(5, 7)[:, m * T:(m + 1) * T], rot, scr[:, 2, m * T:(m + 1) * T],
                             start=True, stop=True, **opts)
                ins.then_inc(rot_psum, 1)
                win_chunk(l, 3)
                pe.wait_ge(conv_silu, l + 1)
                pe.wait_ge(cs_ready, l + 1)
                for g in range(SG):
                    s = slice(HD * g, HD * g + HD)
                    scores(ps[:, 4 if g == 0 else 7, :], cv[s, 5, :], cv[s, 4, :]).then_inc(cb_psum, 1)
                pe.wait_ge(qk_ready, l + 1)
                for b in range(NB):
                    for m in range(4):
                        ins = nc.tensor.transpose(ps[:, 5 + b, m * P:(m + 1) * P],
                                                  cv[:, m, b * P:(b + 1) * P], ident)
                    ins.then_inc(xT_psum, 1)
                win_chunk(l, 4, (0,))
                pe.wait_ge(cb_ready, 2 * (l + 1))
                pe.wait_ge(xdt_ready, 2 * (l + 1))
                for g in range(SG):
                    for hh in range(4):
                        h = 4 * g + hh
                        ins = mm(ps[:, 4 + 2 * g + hh // 2, (hh % 2) * T:(hh % 2) * T + T],
                                 cst[0:SH, C_ID + h:C_ID + h + 1].to_broadcast([SH, P]), csT,
                                 start=True, stop=True, **opts)
                    ins.then_inc(csb_psum, 1)
                win_chunk(l, 4, (1,))
                pe.wait_ge(seg_ready, 2 * (l + 1))
                for h in range(RH):
                    s = slice(HD * (h % 2), HD * (h % 2) + HD)
                    q, k = h // 2 * T, (2 + h // 2) * T
                    ins = scores(ps[:, 4 + h, :], qkr[s, q:q + T], qkr[s, k:k + T])
                ins.then_inc(ret_psum, 1)
                win_chunk(l, 5, (0,))
                pe.wait_ge(s_ret, l + 1)
                for h in range(BH):
                    s = slice(HD * (h % 2), HD * (h % 2) + HD)
                    ins = scores(ps[:, 4 + h, :], bqk[s, h // 2, :], bqk[s, 2 + h // 2, :])
                ins.then_inc(sb_z, 1)
                win_chunk(l, 5, (1,))
                win_chunk(l, 6, (0,))
                pe.wait_ge(rv_ready, l + 1)
                for h in range(RH):
                    for b in range(NB):
                        ins = weighted(ps[:, 1, b * 256 + h * HD:b * 256 + h * HD + HD],
                                       scr[:, 2, h * SC:(h + 1) * SC], rv[:, :, h * HD:(h + 1) * HD], b)
                ins.then_inc(ret_y, 1)
                pe.wait_ge(win_out, 7 * l + 6)
                for g in range(SG):
                    pe.wait_ge(s_ssd, 2 * l + g + 1)
                    for hh in range(4):
                        h = 4 * g + hh
                        for b in range(NB):
                            ins = weighted(ps[:, 2 + b, h * HD:(h + 1) * HD], scr[:, g, hh * SC:(hh + 1) * SC],
                                           xdt[:, :, h * HD:(h + 1) * HD], b)
                ins.then_inc(ssd_y, 1)
                win_chunk(l, 6, (1,))

                def log_weights(h):
                    z = ps[:, 4 + h, :]
                    sp0 = qkr[:, h * SC:h * SC + T]
                    sp1 = qkr[:, h * SC + T:(h + 1) * SC]
                    mm(z[:, 0:T], m_ge, sp0, start=False, stop=True, **opts)
                    mm(z[:, P:T], ones, sp1, start=False, stop=True, **opts)
                    return mm(z[:, T:SC], m_ge, sp1, start=False, stop=True, **opts)

                def mixT(q):
                    for j in range(4):
                        k, b = (4 * q + j) // 2, j % 2
                        ins = nc.tensor.transpose(ps[:, MIXT[q], j * P:(j + 1) * P], hm[:, b, k * P:(k + 1) * P], ident)
                    ins.then_inc(mixT_psum, 1)

                def w_out(half, n, blocks=(0, 1)):
                    g = MIX_BASE[l] + 14 + 2 * half + n
                    pe.wait_ge(lo_ready[g % 6], g // 6 + 1)
                    hi, lo = win_view(w_hi, g % SPL, 512), win_view(w_lo, g % SPL, 512)
                    for b in blocks:
                        for kk in range(4):
                            k = 4 * half + kk
                            ins = passes(ps[:, 2 * b + n, :], aT_hi[:, 2 * k + b, :], aT_lo[:, 2 * k + b, :],
                                         hi[:, kk, :], lo[:, kk, :], start=k == 0, stop=k == KD - 1)
                        if (half, n, b) == (1, 1, 0):
                            ins.then_inc(mix_block0, 1)
                    if blocks[-1] == NB - 1:
                        ins.then_inc(split_used, 1)

                pe.wait_ge(sb_sp, l + 1)
                for h in range(BH):
                    ins = log_weights(h)
                ins.then_inc(sb_log, 1)
                pe.wait_ge(mix_ret, l + 1)
                mixT(0)
                keep_warm(2, 5)
                pe.wait_ge(win_out, 7 * l + 7)
                pe.wait_ge(mix_ssd, l + 1)
                mixT(1)
                keep_warm(2, 9)
                pe.wait_ge(mixT_lo, 4 * l + 2)
                w_out(0, 0)
                pe.wait_ge(sb_wm, l + 1)
                for h in range(BH):
                    for b in range(NB):
                        ins = weighted(ps[:, 7, b * 256 + h * HD:b * 256 + h * HD + HD],
                                       xbf[:, h * SC:(h + 1) * SC], bv[:, :, h * HD:(h + 1) * HD], b)
                ins.then_inc(sb_y, 1)
                mixT(2)
                w_out(0, 1, (0,))
                pe.wait_ge(mix_sb, l + 1)
                mixT(3)
                w_out(0, 1, (1,))
                pe.wait_ge(mixT_lo, 4 * l + 4)
                w_out(1, 0)
                w_out(1, 1)
                keep_warm(6, 13)

            def item(i):
                it = i + 1
                g0 = i * ITEM_SUBS + MOE_BASE
                r0 = i * FC + MOE_BASE // 6

                def wait_sub(pos, c):
                    slot, r = at(pos)
                    pe.wait_ge(lo_ready[slot], r0 + (r + 1) if c is None else r0 + (r + 1) + (c - 1))
                    return slot % SPL

                def proj(bank, pos, c, half):
                    q = wait_sub(pos, c)
                    hi, lo = win_view(w_hi, q, 512), win_view(w_lo, q, 512)
                    for kk in range(4):
                        k = 4 * half + kk
                        ins = passes(ps[:, bank, :], aT_hi[:, k, :], aT_lo[:, k, :], hi[:, kk, :], lo[:, kk, :],
                                     start=k == 0, stop=k == KD - 1)
                    ins.then_inc(split_used, 1)

                def transpose_s(c):
                    pe.wait_ge(s_ready, it * FC + c + 1)
                    for j in range(4):
                        ins = nc.tensor.transpose(ps[:, 2, j * P:(j + 1) * P], s_act[:, j * P:(j + 1) * P], ident)
                    ins.then_inc(sT_psum, 1)

                def down(pos, c, cc):
                    pe.wait_ge(sT_lo, it * FC + cc + 1)
                    for half in range(2):
                        q = wait_sub(pos + half, c)
                        hi = w_hi[:, q, :].rearrange("p (k n) -> p k n", k=2)
                        lo = w_lo[:, q, :].rearrange("p (k n) -> p k n", k=2)
                        for kk in range(2):
                            j = 8 + 2 * half + kk
                            for n in range(2):
                                cols = slice(n * 512, (n + 1) * 512)
                                ins = passes(ps[:, 3 + n, :], aT_hi[:, j, :], aT_lo[:, j, :], hi[:, kk, cols],
                                             lo[:, kk, cols], start=False, stop=False)
                        ins.then_inc(split_used, 1)

                pe.wait_ge(gath_lo, i * 2 + 1)
                proj(0, 0, None, 0)
                pe.wait_ge(gath_lo, i * 2 + 2)
                proj(0, 1, None, 1)
                scatter(i)
                zero_y()
                proj(1, 2, None, 0)
                proj(1, 3, None, 1)
                with pe.Fori(1, FC) as c:
                    pe.wait_ge(silu_done, it * FC + c)
                    proj(0, 4, c, 0)
                    proj(0, 5, c, 1)
                    transpose_s(c - 1)
                    proj(1, 6, c, 0)
                    proj(1, 7, c, 1)
                    down(8, c, c - 1)
                transpose_s(FC - 1)
                gather(i + 1)
                down(6 * FC - 2, None, FC - 1)

            def gather(i):
                pe.wait_ge(sel_built, i + 1)
                for k in range(KD):
                    for b in range(NB):
                        ins = mm(ps[:, 5 + k // 4, (k % 4) * P:(k % 4 + 1) * P], hm[:, b, k * P:(k + 1) * P],
                                 sel[:, b, :], start=b == 0, stop=b == NB - 1, skip_group_check=True)
                    if k % 4 == 3:
                        ins.then_inc(gath_psum, 1)
                for b in range(NB):
                    ins = nc.tensor.transpose(ps[:, 7, b * P:(b + 1) * P], selg[:, b, :], ident)
                ins.then_inc(selgT_psum, 1)

            def scatter(i):
                n = i + 1
                pe.wait_ge(selgT_ready, n)
                pe.wait_ge(y_ready, n)
                for b in range(NB):
                    for h in range(2):
                        ins = mm(ps[:, COMB[2 * b + h], :], selgT[:, b, :], y_sb[:, h * 512:(h + 1) * 512],
                                 start=True, stop=True, skip_group_check=True)
                    ins.then_inc(comb_psum, 1)

            def zero(at_banks):
                for bank in at_banks:
                    ins = mm(ps[:, bank, :], zeros[0:1, 0:P], zeros[0:1, 0:1].to_broadcast([1, 512]), start=True,
                             stop=False, skip_group_check=True)
                return ins

            def zero_y():
                zero((3, 4)).then_inc(y_zero, 1)

            def moe(n):
                gather(0)
                zero_y()
                with pe.Fori(0, n) as i:
                    item(i)
                pe.wait_ge(gath_lo, n * 2 + 2)
                scatter(n)

            def dense():
                def wait_sub(pos, c):
                    slot, r = at(pos)
                    pe.wait_ge(lo_ready[slot], DENSE_BASE // 6 + r + 1 + (0 if c is None else c - 1))
                    return slot % SPL

                def proj(bank, pos, c, half):
                    q = wait_sub(pos, c)
                    hi, lo = win_view(w_hi, q, 512), win_view(w_lo, q, 512)
                    for b in range(NB):
                        for kk in range(4):
                            k = 4 * half + kk
                            ins = passes(ps[:, bank + b, :], aT_hi[:, 2 * k + b, :], aT_lo[:, 2 * k + b, :],
                                         hi[:, kk, :], lo[:, kk, :], start=k == 0, stop=k == KD - 1)
                    ins.then_inc(split_used, 1)

                def transpose_s(c):
                    pe.wait_ge(s_ready, c + 1)
                    for b in range(NB):
                        for j in range(4):
                            cols = slice(b * 512 + j * P, b * 512 + (j + 1) * P)
                            ins = nc.tensor.transpose(ps[:, 2 + b, j * P:(j + 1) * P], s_act2[:, cols], ident)
                    ins.then_inc(sT_psum, 1)

                def down(pos, c, half, last=False):
                    q = wait_sub(pos, c)
                    hi = w_hi[:, q, :].rearrange("p (k n) -> p k n", k=2)
                    lo = w_lo[:, q, :].rearrange("p (k n) -> p k n", k=2)
                    for b in range(NB):
                        for kk in range(2):
                            j = 4 * b + 2 * half + kk
                            for n in range(2):
                                cols = slice(n * 512, (n + 1) * 512)
                                ins = passes(ps[:, 4 + 2 * b + n, :], s2T_hi[:, j, :], s2T_lo[:, j, :],
                                             hi[:, kk, cols], lo[:, kk, cols], start=False, stop=False)
                        if last and b == 0:
                            ins.then_inc(dense_block0, 1)
                    ins.then_inc(split_used, 1)

                transposed_norm(1, 0, hT_psum)
                zero(range(4, 8))
                pe.wait_ge(hT_lo, 6)
                proj(0, 0, None, 0)
                pe.wait_ge(hT_lo, 8)
                proj(0, 1, None, 1)
                proj(2, 2, None, 0)
                proj(2, 3, None, 1)
                transpose_s(0)
                with pe.Fori(1, FC) as c:
                    pe.wait_ge(silu_done, c)
                    proj(0, 4, c, 0)
                    proj(0, 5, c, 1)
                    pe.wait_ge(sT_lo, c)
                    proj(2, 6, c, 0)
                    proj(2, 7, c, 1)
                    down(8, c, 0)
                    transpose_s(c)
                    down(9, c, 1)
                keep_warm(0, 11)
                pe.wait_ge(sT_lo, FC)
                down(6 * FC - 2, None, 0)
                down(6 * FC - 1, None, 1, last=True)
                keep_warm(2, 23)

            pe.wait_ge(zeros_set, 1)
            keep_warm(0, 20)
            pe.wait_ge(const_in, 16)
            mixer(0)
            dense()
            mixer(1)
            transposed_norm(3, 0, h2T_psum)
            keep_warm(6, 4)
            pe.wait_ge(h2T_ready, 4)
            pe.wait_ge(rw_in, 16)
            for b in range(NB):
                for k in range(KD):
                    ins = mm(ps[:, 4, b * E:(b + 1) * E], h2T[:, 2 * k + b, :], rw[:, k, :], start=k == 0,
                             stop=k == KD - 1, skip_group_check=True)
            ins.then_inc(logits, 1)
            keep_warm(6, 12)
            pe.wait_ge(sel_ready, 1)
            s3 = sm3(11)
            opts = dict(skip_group_check=True)
            mm(ps[:, 5, 0:8], m_le, s3[:, 0], start=True, stop=True, **opts)
            mm(ps[:, 5, 8:16], ones, s3[:, 0], start=False, stop=False, **opts)
            mm(ps[:, 5, 8:16], m_le, s3[:, 1], start=False, stop=True, **opts)
            mm(ps[:, 5, 16:24], ones, s3[:, 0], start=False, stop=False, **opts)
            mm(ps[:, 5, 16:24], ones, s3[:, 1], start=False, stop=True, **opts).then_inc(ranks, 1)
            keep_warm(0, 12)
            pe.wait_ge(routed, 1)
            n = pe.value_load(n_items[0:1, 0:1], min_val=E, max_val=2 * E)
            moe(n)


_INS = ['x', 'norm1_w', 'w_in', 'ret_norm_w', 'ssd_conv_w', 'ssd_conv_b', 'ssd_dt_bias', 'ssd_a_log', 'ssd_d',
        'ssd_norm_w', 'w_out', 'norm2_w', 'ffn_w_gate', 'ffn_w_up', 'ffn_w_down', 'moe_router', 'moe_w_gate',
        'moe_w_up', 'moe_w_down', 'final_norm_w']
_OUTS = [((1, T, D), 'float32')]


def kernel(**inputs):
    import concourse.bacc as _bacc
    from concourse.bass_utils import run_bass_kernel_spmd as _run

    nc = _bacc.Bacc("TRN2", target_bir_lowering=False, num_devices=1)
    arrays, args = {}, []
    for name in _INS:
        a = np.ascontiguousarray(inputs[name])
        arrays[f"in_{name}_dram"] = a
        args.append(nc.dram_tensor(f"in_{name}_dram", a.shape, mybir.dt.from_np(a.dtype), kind="ExternalInput").ap())
    c = tables()
    arrays["tables_dram"] = c
    args.append(nc.dram_tensor("tables_dram", c.shape, mybir.dt.from_np(c.dtype), kind="ExternalInput").ap())
    for i, (shape, dtype) in enumerate(_OUTS):
        dt = mybir.dt.from_np(np.dtype(dtype))
        args.append(nc.dram_tensor(f"out_{i}_dram", shape, dt, kind="ExternalOutput").ap())
    hybrid_kernel(nc, *args)
    r = _run(nc, [arrays], core_ids=[0])
    return r.results[0]["out_0_dram"]
```
